# Optimizing a Trainium2 kernel written in Bass

```python
import math
import jax, jax.numpy as jnp
from jax import lax
import numpy as np

D_MODEL = 1024
BATCH = 1
SEQ = 256
DEPTH = 2

GRID_W = 64
CTX_LEN = 256
HEAD_DIM = 64
ROPE_THETA = 10000.0
Q_BLOCK = 128
EPS = 1e-6

B_WIDTH = D_MODEL // 4
B_GROUPS = 4
B_GROUP_DIM = B_WIDTH // B_GROUPS
POOL_WINDOWS = (2, 4, 8, 16)
A_WIDTH = D_MODEL - B_WIDTH
A_Q_HEADS = A_WIDTH // HEAD_DIM
A_KV_HEADS = A_Q_HEADS // 3
A_GROUP = A_Q_HEADS // A_KV_HEADS
A_KV_WIDTH = A_KV_HEADS * HEAD_DIM
A_IN_WIDTH = A_WIDTH + 2 * A_KV_WIDTH + B_WIDTH
D_CH = D_MODEL // 4
C_QK_DIM = HEAD_DIM
C_V_DIM = 2 * HEAD_DIM
C_WIDTH = D_MODEL - D_CH
C_HEADS = C_WIDTH // C_V_DIM
CONV_WIDTH = 31
C_IN_WIDTH = 3 * C_WIDTH + 2 * D_CH
FFN_HIDDEN = -(-8 * D_MODEL // (3 * 256)) * 256
ALPHA = (2.0 * DEPTH) ** 0.25
BETA = (8.0 * DEPTH) ** -0.25

F32 = jnp.float32


def layer_norm(x, g, b):
    xf = x.astype(F32)
    mu = jnp.mean(xf, axis=-1, keepdims=True)
    var = jnp.mean(jnp.square(xf - mu), axis=-1, keepdims=True)
    return ((xf - mu) * lax.rsqrt(var + EPS) * g.astype(F32) + b.astype(F32)).astype(x.dtype)

def rms_norm(x, g):
    xf = x.astype(F32)
    return (xf * lax.rsqrt(jnp.mean(jnp.square(xf), axis=-1, keepdims=True) + EPS) * g.astype(F32)).astype(x.dtype)

def axial_rope_tables(n_tokens):
    rows = n_tokens // GRID_W
    row = jnp.repeat(jnp.arange(rows, dtype=F32), GRID_W)
    col = jnp.tile(jnp.arange(GRID_W, dtype=F32), rows)
    axis_dim = HEAD_DIM // 2
    freqs = ROPE_THETA ** (-jnp.arange(0, axis_dim, 2, dtype=F32) / axis_dim)
    ang = jnp.concatenate([row[:, None] * freqs, col[:, None] * freqs], axis=-1)
    return jnp.cos(ang), jnp.sin(ang)

def apply_axial_rope(x, cos, sin):
    q = HEAD_DIM // 4
    xf = x.astype(F32)

    def rot(xa, c, s):
        x1, x2 = xa[..., :q], xa[..., q:]
        return jnp.concatenate([x1 * c - x2 * s, x2 * c + x1 * s], axis=-1)

    out = jnp.concatenate([rot(xf[..., :2 * q], cos[:, :q], sin[:, :q]),
                           rot(xf[..., 2 * q:], cos[:, q:], sin[:, q:])], axis=-1)
    return out.astype(x.dtype)

def map_query_blocks(fn, q):
    t = q.shape[-2]
    nb = t // Q_BLOCK
    qb = jnp.moveaxis(q.reshape(q.shape[:-2] + (nb, Q_BLOCK, q.shape[-1])), -3, 0)
    out = jnp.moveaxis(lax.map(fn, qb), 0, -3)
    return out.reshape(out.shape[:-3] + (t, out.shape[-1]))

def gqa_attend(q, k, v):
    s = jnp.einsum('bkgqd,bksd->bkgqs', q, k, preferred_element_type=F32) * (HEAD_DIM ** -0.5)
    p = jax.nn.softmax(s, axis=-1)
    return jnp.einsum('bkgqs,bksd->bkgqd', p.astype(v.dtype), v)

def diff_attend(q, k, v, lam):
    s = jnp.einsum('bhiqd,bhisd->bhiqs', q, k, preferred_element_type=F32) * (C_QK_DIM ** -0.5)
    p = jax.nn.softmax(s, axis=-1)
    a = p[:, :, 0] - lam * p[:, :, 1]
    return jnp.einsum('bhqs,bhsd->bhqd', a.astype(v.dtype), v)

def centred_window_mean(x, w):
    t_len = x.shape[1]
    cs = jnp.pad(jnp.cumsum(x.astype(F32), axis=1), ((0, 0), (1, 0), (0, 0)))
    t = jnp.arange(t_len)
    lo = jnp.clip(t - w // 2, 0, t_len)
    hi = jnp.clip(t + (w - 1 - w // 2) + 1, 0, t_len)
    s = jnp.take(cs, hi, axis=1) - jnp.take(cs, lo, axis=1)
    return (s / (hi - lo).astype(F32)[None, :, None]).astype(x.dtype)

def pool_mixer(u, w_pool, pool_scale):
    bsz, n, _ = u.shape
    ug = u.reshape(bsz, n, B_GROUPS, B_GROUP_DIM)
    pooled = jnp.stack([centred_window_mean(ug[:, :, g], w) - ug[:, :, g]
                        for g, w in enumerate(POOL_WINDOWS)], axis=2)
    mixed = jnp.einsum('bngc,gcd->bngd', pooled, w_pool)
    return mixed.reshape(bsz, n, B_WIDTH) * pool_scale

def conformer_conv(u, conv_w, conv_b, ln_g, ln_b):
    a, g = jnp.split(u, 2, axis=-1)
    z = a * jax.nn.sigmoid(g)
    z = lax.conv_general_dilated(z, conv_w[:, None, :].astype(z.dtype), window_strides=(1,),
                                 padding=[(CONV_WIDTH // 2, CONV_WIDTH // 2)],
                                 dimension_numbers=('NWC', 'WIO', 'NWC'),
                                 feature_group_count=D_CH) + conv_b
    return jax.nn.silu(layer_norm(z, ln_g, ln_b))

def swiglu(h, w_in, w_out):
    a, g = jnp.split(h @ w_in, 2, axis=-1)
    return (jax.nn.silu(g) * a) @ w_out

def mixer_ab(h, hc, w_in, q_gain, k_gain, w_pool, pool_scale, w_out, cos, sin, with_ctx_out):
    bsz, n_lat, _ = h.shape
    n_ctx = hc.shape[1]
    n = n_ctx + n_lat
    p = jnp.concatenate([hc, h], axis=1) @ w_in
    q, k, v, u = jnp.split(p, [A_WIDTH, A_WIDTH + A_KV_WIDTH, A_WIDTH + 2 * A_KV_WIDTH], axis=-1)
    q = rms_norm(q.reshape(bsz, n, A_KV_HEADS, A_GROUP, HEAD_DIM), q_gain).transpose(0, 2, 3, 1, 4)
    k = rms_norm(k.reshape(bsz, n, A_KV_HEADS, HEAD_DIM), k_gain).transpose(0, 2, 1, 3)
    v = v.reshape(bsz, n, A_KV_HEADS, HEAD_DIM).transpose(0, 2, 1, 3)
    k_all = jnp.concatenate([k[..., :n_ctx, :], apply_axial_rope(k[..., n_ctx:, :], cos, sin)], axis=-2)
    q_lat = apply_axial_rope(q[..., n_ctx:, :], cos, sin)
    o_lat = map_query_blocks(lambda qb: gqa_attend(qb, k_all, v), q_lat)

    def finish(o, uu):
        o = o.transpose(0, 3, 1, 2, 4).reshape(o.shape[0], o.shape[3], A_WIDTH)
        return jnp.concatenate([o, pool_mixer(uu, w_pool, pool_scale)], axis=-1) @ w_out

    y = finish(o_lat, u[:, n_ctx:])
    yc = None
    if with_ctx_out:
        o_ctx = gqa_attend(q[..., :n_ctx, :], k[..., :n_ctx, :], v[:, :, :n_ctx])
        yc = finish(o_ctx, u[:, :n_ctx])
    return y, yc

def mixer_cd(h, hc, w_in, lq1, lk1, lq2, lk2, subln_gain, conv_w, conv_b, conv_ln_g, conv_ln_b,
             w_out, cos, sin, lam_init, with_ctx_out):
    bsz, n_lat, _ = h.shape
    n_ctx = hc.shape[1]
    n = n_ctx + n_lat
    p = jnp.concatenate([hc, h], axis=1) @ w_in
    q, k, v, u = jnp.split(p, [C_WIDTH, 2 * C_WIDTH, 3 * C_WIDTH], axis=-1)
    q = q.reshape(bsz, n, C_HEADS, 2, C_QK_DIM).transpose(0, 2, 3, 1, 4)
    k = k.reshape(bsz, n, C_HEADS, 2, C_QK_DIM).transpose(0, 2, 3, 1, 4)
    v = v.reshape(bsz, n, C_HEADS, C_V_DIM).transpose(0, 2, 1, 3)
    lam = (jnp.exp(jnp.sum(lq1.astype(F32) * lk1.astype(F32)))
           - jnp.exp(jnp.sum(lq2.astype(F32) * lk2.astype(F32))) + lam_init)
    k_all = jnp.concatenate([k[..., :n_ctx, :], apply_axial_rope(k[..., n_ctx:, :], cos, sin)], axis=-2)
    q_lat = apply_axial_rope(q[..., n_ctx:, :], cos, sin)
    o_lat = map_query_blocks(lambda qb: diff_attend(qb, k_all, v, lam), q_lat)

    def finish(o, uu):
        o = rms_norm(o, subln_gain) * (1.0 - lam_init)
        o = o.transpose(0, 2, 1, 3).reshape(o.shape[0], o.shape[2], C_WIDTH)
        conv = conformer_conv(uu, conv_w, conv_b, conv_ln_g, conv_ln_b)
        return jnp.concatenate([o, conv], axis=-1) @ w_out

    y = finish(o_lat, u[:, n_ctx:])
    yc = None
    if with_ctx_out:
        o_ctx = diff_attend(q[..., :n_ctx, :], k[..., :n_ctx, :], v[:, :, :n_ctx], lam)
        yc = finish(o_ctx, u[:, :n_ctx])
    return y, yc

def first_inputs(seed: int = 0) -> dict:
    key = jax.random.key(seed)
    ks = iter(jax.random.split(key, 32))
    n_even = (DEPTH + 1) // 2
    n_odd = DEPTH // 2

    def nrm(shape, scale):
        return jax.random.normal(next(ks), shape, F32) * scale

    def gain(shape):
        return 1.0 + nrm(shape, 0.05)

    return {
        'x': nrm((BATCH, SEQ, D_MODEL), 1.0),
        'c': nrm((BATCH, D_MODEL), 1.0),
        'ctx': nrm((BATCH, CTX_LEN, D_MODEL), 1.0),
        'c_ctx': nrm((D_MODEL,), 1.0),
        'ab_w_in': nrm((n_even, D_MODEL, A_IN_WIDTH), D_MODEL ** -0.5),
        'ab_q_gain': gain((n_even, HEAD_DIM)),
        'ab_k_gain': gain((n_even, HEAD_DIM)),
        'ab_w_pool': nrm((n_even, B_GROUPS, B_GROUP_DIM, B_GROUP_DIM), B_GROUP_DIM ** -0.5),
        'ab_pool_scale': gain((n_even, B_WIDTH)),
        'ab_w_out': nrm((n_even, D_MODEL, D_MODEL), BETA * D_MODEL ** -0.5),
        'cd_w_in': nrm((n_odd, D_MODEL, C_IN_WIDTH), D_MODEL ** -0.5),
        'cd_lambda_q1': nrm((n_odd, C_QK_DIM), 0.1),
        'cd_lambda_k1': nrm((n_odd, C_QK_DIM), 0.1),
        'cd_lambda_q2': nrm((n_odd, C_QK_DIM), 0.1),
        'cd_lambda_k2': nrm((n_odd, C_QK_DIM), 0.1),
        'cd_subln_gain': gain((n_odd, C_V_DIM)),
        'cd_conv_w': nrm((n_odd, CONV_WIDTH, D_CH), CONV_WIDTH ** -0.5),
        'cd_conv_b': nrm((n_odd, D_CH), 0.02),
        'cd_conv_ln_g': gain((n_odd, D_CH)),
        'cd_conv_ln_b': nrm((n_odd, D_CH), 0.02),
        'cd_w_out': nrm((n_odd, D_MODEL, D_MODEL), BETA * D_MODEL ** -0.5),
        'ada_w': nrm((DEPTH, D_MODEL, 6 * D_MODEL), 0.5 * D_MODEL ** -0.5),
        'ada_b': nrm((DEPTH, 6 * D_MODEL), 0.02),
        'ln1_g': gain((DEPTH, D_MODEL)),
        'ln1_b': nrm((DEPTH, D_MODEL), 0.02),
        'ln2_g': gain((DEPTH, D_MODEL)),
        'ln2_b': nrm((DEPTH, D_MODEL), 0.02),
        'ffn_w_in': nrm((DEPTH, D_MODEL, 2 * FFN_HIDDEN), D_MODEL ** -0.5),
        'ffn_w_out': nrm((DEPTH, FFN_HIDDEN, D_MODEL), BETA * FFN_HIDDEN ** -0.5),
    }

def first_block(x, c, ctx, c_ctx, ab_w_in, ab_q_gain, ab_k_gain, ab_w_pool, ab_pool_scale, ab_w_out,
              cd_w_in, cd_lambda_q1, cd_lambda_k1, cd_lambda_q2, cd_lambda_k2, cd_subln_gain,
              cd_conv_w, cd_conv_b, cd_conv_ln_g, cd_conv_ln_b, cd_w_out,
              ada_w, ada_b, ln1_g, ln1_b, ln2_g, ln2_b, ffn_w_in, ffn_w_out):
    cos, sin = axial_rope_tables(x.shape[1])
    xc = ctx
    for l in range(DEPTH):
        with_ctx_out = l < DEPTH - 1
        mod = (jax.nn.silu(c) @ ada_w[l] + ada_b[l])[:, None, :]
        mod_c = (jax.nn.silu(c_ctx) @ ada_w[l] + ada_b[l])[None, None, :]
        sh1, sc1, g1, sh2, sc2, g2 = jnp.split(mod, 6, axis=-1)
        csh1, csc1, cg1, csh2, csc2, cg2 = jnp.split(mod_c, 6, axis=-1)
        h = x * (1.0 + sc1) + sh1
        hc = xc * (1.0 + csc1) + csh1
        i = l // 2
        if l % 2 == 0:
            y, yc = mixer_ab(h, hc, ab_w_in[i], ab_q_gain[i], ab_k_gain[i], ab_w_pool[i], ab_pool_scale[i],
                             ab_w_out[i], cos, sin, with_ctx_out)
        else:
            lam_init = 0.8 - 0.6 * math.exp(-0.3 * l)
            y, yc = mixer_cd(h, hc, cd_w_in[i], cd_lambda_q1[i], cd_lambda_k1[i], cd_lambda_q2[i], cd_lambda_k2[i],
                             cd_subln_gain[i], cd_conv_w[i], cd_conv_b[i], cd_conv_ln_g[i], cd_conv_ln_b[i],
                             cd_w_out[i], cos, sin, lam_init, with_ctx_out)
        x = layer_norm(ALPHA * x + g1 * y, ln1_g[l], ln1_b[l])
        x = layer_norm(ALPHA * x + g2 * swiglu(x * (1.0 + sc2) + sh2, ffn_w_in[l], ffn_w_out[l]), ln2_g[l], ln2_b[l])
        if with_ctx_out:
            xc = layer_norm(ALPHA * xc + cg1 * yc, ln1_g[l], ln1_b[l])
            xc = layer_norm(ALPHA * xc + cg2 * swiglu(xc * (1.0 + csc2) + csh2, ffn_w_in[l], ffn_w_out[l]),
                            ln2_g[l], ln2_b[l])
    return x


N_MEM = 256
N_MIXERS = 2
D_MIX = D_MODEL
ML_HEADS = 4
ML_HEAD_DIM = 192
ML_WIDTH = ML_HEADS * ML_HEAD_DIM
ML_CHUNK = 64
RG_WIDTH = 768
RG_BLOCKS = 8
RG_BLOCK_DIM = RG_WIDTH // RG_BLOCKS
RG_CONV = 4
RG_C = 8.0
XA_HEADS = 4
XA_HEAD_DIM = 64
XA_WIDTH = XA_HEADS * XA_HEAD_DIM
PEER_HEADS = 8
PEER_KEYS = 128
PEER_EXPERTS = PEER_KEYS * PEER_KEYS
PEER_HALF = 128
PEER_QDIM = 2 * PEER_HALF
PEER_TOPK = 16
PEER_TOK_BLOCK = 128
DN_ALPHA = (2 * DEPTH) ** 0.25
DN_BETA = (8 * DEPTH) ** -0.25
LN_EPS = 1e-5
N_A = (DEPTH + 1) // 2
N_B = DEPTH // 2
ML_IN = 4 * ML_WIDTH + 2 * ML_HEADS + XA_WIDTH
RG_IN = 2 * RG_WIDTH + XA_WIDTH


def layer_norm_2(x, g, b):
    xf = x.astype(jnp.float32)
    mu = jnp.mean(xf, axis=-1, keepdims=True)
    var = jnp.mean(jnp.square(xf - mu), axis=-1, keepdims=True)
    y = (xf - mu) * lax.rsqrt(var + LN_EPS) * g.astype(jnp.float32) + b.astype(jnp.float32)
    return y.astype(x.dtype)

def cross_attention(xq, mem, w_kv):
    B, S, _ = xq.shape
    M = mem.shape[1]
    q = xq.reshape(B, S, XA_HEADS, XA_HEAD_DIM).astype(jnp.float32)
    kv = (mem @ w_kv).astype(jnp.float32)
    k = kv[..., :XA_WIDTH].reshape(B, M, XA_HEADS, XA_HEAD_DIM)
    v = kv[..., XA_WIDTH:].reshape(B, M, XA_HEADS, XA_HEAD_DIM)
    s = jnp.einsum('bshd,bmhd->bhsm', q, k) * (XA_HEAD_DIM ** -0.5)
    p = jax.nn.softmax(s, axis=-1)
    o = jnp.einsum('bhsm,bmhd->bshd', p, v)
    return o.reshape(B, S, XA_WIDTH).astype(xq.dtype)

def mlstm_mixer(zm, b_gates, norm_g):
    B, S, _ = zm.shape
    H, dh, L = ML_HEADS, ML_HEAD_DIM, ML_CHUNK
    nc = S // L
    W = ML_WIDTH
    q, k, v, o, g = jnp.split(zm, [W, 2 * W, 3 * W, 4 * W], axis=-1)
    g = g.astype(jnp.float32) + b_gates.astype(jnp.float32)
    ig = g[..., :H]
    lf = jax.nn.log_sigmoid(g[..., H:])

    def to_chunks(t):
        return t.astype(jnp.float32).reshape(B, nc, L, H, dh).transpose(1, 0, 3, 2, 4)

    def gate_chunks(t):
        return t.reshape(B, nc, L, H).transpose(1, 0, 3, 2)

    qc = to_chunks(q)
    kc = to_chunks(k) * (dh ** -0.5)
    vc = to_chunks(v)
    causal = jnp.tril(jnp.ones((L, L), dtype=bool))

    def step(carry, inp):
        C, n, m = carry
        qq, kk, vv, ii, ff = inp
        b = jnp.cumsum(ff, axis=-1)
        dmat = b[..., :, None] - b[..., None, :] + ii[..., None, :]
        dmat = jnp.where(causal, dmat, -jnp.inf)
        inter = b + m[..., None]
        mj = jnp.maximum(jnp.max(dmat, axis=-1), inter)
        w = jnp.exp(dmat - mj[..., None])
        s = jnp.einsum('bhld,bhsd->bhls', qq, kk) * w
        sc = jnp.exp(inter - mj)
        num = sc[..., None] * jnp.einsum('bhld,bhde->bhle', qq, C) + jnp.einsum('bhls,bhse->bhle', s, vv)
        den = sc * jnp.einsum('bhld,bhd->bhl', qq, n) + jnp.sum(s, axis=-1)
        h = num / jnp.maximum(jnp.abs(den), jnp.exp(-mj))[..., None]
        bl = b[..., -1]
        gl = bl[..., None] - b + ii
        m_new = jnp.maximum(bl + m, jnp.max(gl, axis=-1))
        wg = jnp.exp(gl - m_new[..., None])
        decay = jnp.exp(bl + m - m_new)
        C_new = decay[..., None, None] * C + jnp.einsum('bhl,bhld,bhle->bhde', wg, kk, vv)
        n_new = decay[..., None] * n + jnp.einsum('bhl,bhld->bhd', wg, kk)
        return (C_new, n_new, m_new), h

    init = (jnp.zeros((B, H, dh, dh), jnp.float32), jnp.zeros((B, H, dh), jnp.float32),
            jnp.zeros((B, H), jnp.float32))
    _, hc = lax.scan(step, init, (qc, kc, vc, gate_chunks(ig), gate_chunks(lf)))
    h = hc.transpose(1, 0, 3, 2, 4).reshape(B, S, H, dh)
    mu = jnp.mean(h, axis=-1, keepdims=True)
    var = jnp.mean(jnp.square(h - mu), axis=-1, keepdims=True)
    hn = (h - mu) * lax.rsqrt(var + LN_EPS) * norm_g.astype(jnp.float32).reshape(H, dh)
    y = hn.reshape(B, S, W) * jax.nn.sigmoid(o.astype(jnp.float32))
    return y.astype(zm.dtype)

def rglru_mixer(zr, conv_w, conv_b, w_a, b_a, w_x, b_x, lam):
    B, S, _ = zr.shape
    gate = zr[..., :RG_WIDTH]
    xr = zr[..., RG_WIDTH:]
    xr = lax.conv_general_dilated(xr, conv_w[:, None, :], window_strides=(1,),
                                  padding=[(RG_CONV - 1, 0)],
                                  dimension_numbers=('NWC', 'WIO', 'NWC'),
                                  feature_group_count=RG_WIDTH) + conv_b
    xb = xr.reshape(B, S, RG_BLOCKS, RG_BLOCK_DIM)
    r = jax.nn.sigmoid((jnp.einsum('bsgi,gij->bsgj', xb, w_a).reshape(B, S, RG_WIDTH) + b_a).astype(jnp.float32))
    i = jax.nn.sigmoid((jnp.einsum('bsgi,gij->bsgj', xb, w_x).reshape(B, S, RG_WIDTH) + b_x).astype(jnp.float32))
    log_a = -RG_C * r * jax.nn.softplus(-lam.astype(jnp.float32))
    a = jnp.exp(log_a)
    u = jnp.sqrt(-jnp.expm1(2.0 * log_a)) * (i * xr.astype(jnp.float32))

    def combine(e1, e2):
        a1, b1 = e1
        a2, b2 = e2
        return a1 * a2, a2 * b1 + b2

    _, h = lax.associative_scan(combine, (a, u), axis=1)
    y = h * jax.nn.gelu(gate.astype(jnp.float32), approximate=False)
    return y.astype(zr.dtype)

def peer_ffn(x, w_q, subkeys, u_tab, v_tab):
    B, S, D = x.shape
    n = PEER_TOK_BLOCK
    xt = x.reshape((B * S) // n, n, D)
    sk = subkeys.astype(jnp.float32)

    def block(xb):
        q = (xb @ w_q).reshape(n, PEER_HEADS, 2, PEER_HALF).astype(jnp.float32)
        s = jnp.einsum('nhpc,pkc->nhpk', q, sk)
        sv, si = lax.top_k(s, PEER_TOPK)
        cand = sv[:, :, 0, :, None] + sv[:, :, 1, None, :]
        cand_id = si[:, :, 0, :, None] * PEER_KEYS + si[:, :, 1, None, :]
        fv, fi = lax.top_k(cand.reshape(n, PEER_HEADS, PEER_TOPK * PEER_TOPK), PEER_TOPK)
        eid = jnp.take_along_axis(cand_id.reshape(n, PEER_HEADS, PEER_TOPK * PEER_TOPK), fi, axis=-1)
        gw = jax.nn.softmax(fv, axis=-1)
        u = u_tab[eid]
        act = jax.nn.gelu(jnp.einsum('nhkd,nd->nhk', u, xb).astype(jnp.float32), approximate=False)
        coef = (gw * act).astype(x.dtype)
        return jnp.einsum('nhk,nhkd->nd', coef, v_tab[eid])

    y = lax.map(block, xt)
    return y.reshape(B, S, D)

def second_inputs(seed: int = 0) -> dict:
    key = jax.random.key(seed)
    ks = jax.random.split(key, 24)
    D = D_MODEL
    nrm = jax.random.normal
    x = nrm(ks[0], (BATCH, SEQ, D), jnp.float32)
    mem = nrm(ks[1], (BATCH, N_MEM, D), jnp.float32)
    mlstm_w_in = nrm(ks[2], (N_A, D, ML_IN), jnp.float32) * D ** -0.5
    f_bias = jnp.linspace(3.0, 6.0, ML_HEADS, dtype=jnp.float32)
    mlstm_b_gates = jnp.concatenate([
        0.1 * nrm(ks[3], (N_A, ML_HEADS), jnp.float32),
        f_bias[None, :] + 0.1 * nrm(ks[4], (N_A, ML_HEADS), jnp.float32)], axis=-1)
    mlstm_norm_g = 1.0 + 0.02 * nrm(ks[5], (N_A, ML_WIDTH), jnp.float32)
    rglru_w_in = nrm(ks[6], (N_B, D, RG_IN), jnp.float32) * D ** -0.5
    rglru_conv_w = nrm(ks[7], (N_B, RG_CONV, RG_WIDTH), jnp.float32) * RG_CONV ** -0.5
    rglru_conv_b = 0.01 * nrm(ks[8], (N_B, RG_WIDTH), jnp.float32)
    rglru_w_a = nrm(ks[9], (N_B, RG_BLOCKS, RG_BLOCK_DIM, RG_BLOCK_DIM), jnp.float32) * RG_BLOCK_DIM ** -0.5
    rglru_b_a = 0.01 * nrm(ks[10], (N_B, RG_WIDTH), jnp.float32)
    rglru_w_x = nrm(ks[11], (N_B, RG_BLOCKS, RG_BLOCK_DIM, RG_BLOCK_DIM), jnp.float32) * RG_BLOCK_DIM ** -0.5
    rglru_b_x = 0.01 * nrm(ks[12], (N_B, RG_WIDTH), jnp.float32)
    a0 = jax.random.uniform(ks[13], (N_B, RG_WIDTH), jnp.float32, 0.9, 0.999)
    p = a0 ** (1.0 / RG_C)
    rglru_lam = jnp.log(p) - jnp.log1p(-p)
    xattn_w_kv = nrm(ks[14], (DEPTH, D, 2 * XA_WIDTH), jnp.float32) * D ** -0.5
    w_out = nrm(ks[15], (DEPTH, D_MIX, D), jnp.float32) * (D_MIX ** -0.5) * DN_BETA
    ln1_g = 1.0 + 0.02 * nrm(ks[16], (DEPTH, D), jnp.float32)
    ln1_b = 0.01 * nrm(ks[17], (DEPTH, D), jnp.float32)
    peer_w_q = nrm(ks[18], (DEPTH, D, PEER_HEADS * PEER_QDIM), jnp.float32) * D ** -0.5
    peer_subkeys = nrm(ks[19], (DEPTH, 2, PEER_KEYS, PEER_HALF), jnp.float32) * PEER_HALF ** -0.5
    peer_u = nrm(ks[20], (DEPTH, PEER_EXPERTS, D), jnp.float32) * D ** -0.5
    peer_v = nrm(ks[21], (DEPTH, PEER_EXPERTS, D), jnp.float32) * (D ** -0.5) * DN_BETA
    ln2_g = 1.0 + 0.02 * nrm(ks[22], (DEPTH, D), jnp.float32)
    ln2_b = 0.01 * nrm(ks[23], (DEPTH, D), jnp.float32)
    return {"x": x, "mem": mem,
            "mlstm_w_in": mlstm_w_in, "mlstm_b_gates": mlstm_b_gates, "mlstm_norm_g": mlstm_norm_g,
            "rglru_w_in": rglru_w_in, "rglru_conv_w": rglru_conv_w, "rglru_conv_b": rglru_conv_b,
            "rglru_w_a": rglru_w_a, "rglru_b_a": rglru_b_a, "rglru_w_x": rglru_w_x, "rglru_b_x": rglru_b_x,
            "rglru_lam": rglru_lam, "xattn_w_kv": xattn_w_kv, "w_out": w_out,
            "ln1_g": ln1_g, "ln1_b": ln1_b, "peer_w_q": peer_w_q, "peer_subkeys": peer_subkeys,
            "peer_u": peer_u, "peer_v": peer_v, "ln2_g": ln2_g, "ln2_b": ln2_b}

def second_block(x, mem, mlstm_w_in, mlstm_b_gates, mlstm_norm_g, rglru_w_in, rglru_conv_w, rglru_conv_b,
              rglru_w_a, rglru_b_a, rglru_w_x, rglru_b_x, rglru_lam, xattn_w_kv, w_out,
              ln1_g, ln1_b, peer_w_q, peer_subkeys, peer_u, peer_v, ln2_g, ln2_b):
    for i in range(DEPTH):
        j = i // N_MIXERS
        if i % N_MIXERS == 0:
            z = x @ mlstm_w_in[j]
            hm = mlstm_mixer(z[..., :ML_IN - XA_WIDTH], mlstm_b_gates[j], mlstm_norm_g[j])
            xq = z[..., ML_IN - XA_WIDTH:]
        else:
            z = x @ rglru_w_in[j]
            hm = rglru_mixer(z[..., :RG_IN - XA_WIDTH], rglru_conv_w[j], rglru_conv_b[j],
                             rglru_w_a[j], rglru_b_a[j], rglru_w_x[j], rglru_b_x[j], rglru_lam[j])
            xq = z[..., RG_IN - XA_WIDTH:]
        ha = cross_attention(xq, mem, xattn_w_kv[i])
        mix = jnp.concatenate([hm, ha], axis=-1) @ w_out[i]
        x = layer_norm_2(DN_ALPHA * x + mix, ln1_g[i], ln1_b[i])
        y = peer_ffn(x, peer_w_q[i], peer_subkeys[i], peer_u[i], peer_v[i])
        x = layer_norm_2(DN_ALPHA * x + y, ln2_g[i], ln2_b[i])
    return x


def setup_inputs(seed=0):
    out = dict(first_inputs(seed))
    for name, value in second_inputs(seed + 1).items():
        if name != "x":
            out[name + "_2"] = value
    return out


def reference(
    x, c, ctx, c_ctx, ab_w_in, ab_q_gain, ab_k_gain, ab_w_pool, ab_pool_scale, ab_w_out,
    cd_w_in, cd_lambda_q1, cd_lambda_k1, cd_lambda_q2, cd_lambda_k2, cd_subln_gain, cd_conv_w,
    cd_conv_b, cd_conv_ln_g, cd_conv_ln_b, cd_w_out, ada_w, ada_b, ln1_g, ln1_b, ln2_g, ln2_b,
    ffn_w_in, ffn_w_out, mem_2, mlstm_w_in_2, mlstm_b_gates_2, mlstm_norm_g_2, rglru_w_in_2,
    rglru_conv_w_2, rglru_conv_b_2, rglru_w_a_2, rglru_b_a_2, rglru_w_x_2, rglru_b_x_2,
    rglru_lam_2, xattn_w_kv_2, w_out_2, ln1_g_2, ln1_b_2, peer_w_q_2, peer_subkeys_2, peer_u_2,
    peer_v_2, ln2_g_2, ln2_b_2,
):
    x = first_block(
        x, c, ctx, c_ctx, ab_w_in, ab_q_gain, ab_k_gain, ab_w_pool, ab_pool_scale, ab_w_out,
        cd_w_in, cd_lambda_q1, cd_lambda_k1, cd_lambda_q2, cd_lambda_k2, cd_subln_gain,
        cd_conv_w, cd_conv_b, cd_conv_ln_g, cd_conv_ln_b, cd_w_out, ada_w, ada_b, ln1_g, ln1_b,
        ln2_g, ln2_b, ffn_w_in, ffn_w_out,
    )
    return second_block(
        x, mem_2, mlstm_w_in_2, mlstm_b_gates_2, mlstm_norm_g_2, rglru_w_in_2, rglru_conv_w_2,
        rglru_conv_b_2, rglru_w_a_2, rglru_b_a_2, rglru_w_x_2, rglru_b_x_2, rglru_lam_2,
        xattn_w_kv_2, w_out_2, ln1_g_2, ln1_b_2, peer_w_q_2, peer_subkeys_2, peer_u_2, peer_v_2,
        ln2_g_2, ln2_b_2,
    )


_drawn_inputs = setup_inputs


def setup_inputs(seed=0):
    import zlib

    import numpy as np

    out = dict(_drawn_inputs(seed))
    spreads = {}
    factors = {'ab_q_gain': 8.0,
     'ab_k_gain': 8.0,
     'ab_pool_scale': 8.0,
     'cd_lambda_q1': 4.581,
     'cd_lambda_k1': 8.0,
     'cd_lambda_q2': 8.0,
     'cd_lambda_k2': 8.0,
     'cd_subln_gain': 8.0,
     'cd_conv_b': 8.0,
     'cd_conv_ln_g': 8.0,
     'cd_conv_ln_b': 8.0,
     'ada_b': 4.349,
     'mlstm_norm_g_2': 8.0,
     'rglru_conv_b_2': 7.358,
     'rglru_b_a_2': 22.698,
     'rglru_b_x_2': 8.0,
     'ln1_b_2': 3.363,
     'peer_w_q_2': 7.512,
     'peer_subkeys_2': 7.503,
     'peer_u_2': 8.0,
     'peer_v_2': 7.542,
     'ln2_b_2': 3.558}
    for name, (base, spread) in spreads.items():
        noise = np.random.default_rng([zlib.crc32(name.encode()), seed]).standard_normal(out[name].shape)
        drawn = base * np.exp(spread * noise) if base else spread * noise
        out[name] = __import__('jax').numpy.asarray(drawn.astype(out[name].dtype))
    for name, factor in factors.items():
        out[name] = (out[name] * factor).astype(out[name].dtype)
    return out
```

```python
import math
from contextlib import ExitStack

import numpy as np

import concourse.bass as bass
from concourse import mybir

ALU = mybir.AluOpType
ACT = mybir.ActivationFunctionType
F32 = mybir.dt.float32
U32 = mybir.dt.uint32
AX_X = mybir.AxisListType.X

P = 128
D = 1024
T = 256
KD = D // P
DEPTH = 2
HD = 64
FFN = 2816
FH = FFN // P
ALPHA = (2.0 * DEPTH) ** 0.25
LAM_INIT = 0.8 - 0.6 * math.exp(-0.3)
EPS1 = 1e-6
EPS2 = 1e-5
WINDOWS = (2, 4, 8, 16)
CONV = 31
CPAD = CONV // 2
RG_CONV = 4
RB = 96
NRB = 8
RG_C = 8.0
MH = 4
MDH = 192
PH = 8
KEYS = 128
TOPK = 16
NEG = -3.0e38
ROOT_MIN = 2.0 ** -115
R = 6
CTX, LAT = 0, 1

Q_ORDER = [0, 3, 1, 4, 2, 5, 6, 9, 7, 10, 8, 11]


def const_layout():
    at, off = {}, 0
    for name, n in (("ident", P), ("mean_d", P), ("mean_64", P), ("mean_128", P), ("mean_192", P), ("mean_192_half", 2 * P), ("mean_256", P),
                    ("ones", P), ("rot", P), ("cos", T), ("sin", T), ("inv_count", 2 * T), ("iota", P),
                    ("head_rows", MH * P)):
        at[name] = (off, off + n)
        off += n
    return at, off


def param_layout():
    at, off = {}, 0
    names = [("ada_b0", 48), ("ada_b1", 48), ("q_gain", 1), ("k_gain", 1), ("pool_scale", 2), ("pool_w", 2 * P), ("subln", 1),
             ("conv_w", 2 * CONV), ("conv_b", 2), ("conv_g", 2), ("conv_bb", 2), ("lq1", HD), ("lk1", HD),
             ("lq2", HD), ("lk2", HD), ("mnorm", 6), ("i_bias", 1), ("f_bias", 1),
             ("rconv_w", NRB * RG_CONV), ("rconv_b", NRB), ("r_ba", NRB), ("r_bx", NRB), ("r_lam", NRB)]
    for n in range(4):
        names += [(f"ln{n}{k}", KD) for k in ("g1", "b1", "g2", "b2")]
    for name, n in names:
        at[name] = (off, off + n)
        off += n
    return at, off


def stage_list():
    s = [("lambda", "va")]
    for l in range(2):
        s += [(f"ada{l}", "pav" if l == 0 else "pv"), (f"modulate{l}", "v"), (f"project{l}", "pav")]
        s += [("heads_norm", "pav")] if l == 0 else []
        s += [(f"rope{l}", "pv"), (f"attend{l}", "pav")]
        s += [("pool", "pv")] if l == 0 else [("subln", "pav"), ("conv", "pav")]
        for n in ((CTX, LAT) if l == 0 else (LAT,)):
            s += [(f"out{l}{n}", "pv"), (f"norm1{l}{n}", "pav"), (f"shift{l}{n}", "v"), (f"hidden{l}{n}", "pav"),
                  (f"norm2{l}{n}", "pav")]
    for l in (2, 3):
        s += [(f"project{l}", "pav")]
        s += [("gates", "pav"), ("mlstm", "pavg"), ("mlstm_norm", "pav")] if l == 2 else [("rglru", "pav")]
        s += [(f"memory{l}", "pav"), (f"attend{l}", "pav"), (f"out{l}{LAT}", "pv"), (f"norm1{l}{LAT}", "pav"),
              (f"query{l}", "pav"), (f"choose{l}", "pav"), (f"spread{l}", "pav"), (f"hidden{l}{LAT}", "pav"),
              (f"norm2{l}{LAT}", "pav")]
    return s


STAGES = stage_list()


def stages_of(engine, before):
    n = 0
    for name, engines in STAGES:
        if name == before:
            return n
        n += engine in engines
    raise KeyError(before)


FEATURES, TOKENS = "features", "tokens"
PROJECT = {
    0: [(0, 8, 0, 2 * T, FEATURES, P), (8, 2, 0, 2 * T, TOKENS, P), (10, 2, 0, 2 * T, FEATURES, P)],
    1: [(0, 6, T, T, FEATURES, P), (6, 6, 0, 2 * T, FEATURES, P), (12, 6, 0, 2 * T, TOKENS, P),
        (18, 4, T, T, FEATURES, P)],
    2: [(0, 12, 0, T, FEATURES, P), (12, 6, 0, T, TOKENS, P), (18, 8, 0, T, FEATURES, P)],
    3: [(0, 16, 0, T, FEATURES, RB), (24, 2, 0, T, FEATURES, P)],
}
PROJECT_MEMORY = [(0, 2, 0, T, FEATURES, P), (2, 2, 0, T, TOKENS, P)]
PROJECT_QUERY = [(0, 16, 0, T, FEATURES, P)]
ROPE = {0: [(j, T) for j in range(8)], 1: [(j, 0) for j in range(6)] + [(j, T) for j in range(6, 12)]}

HIDDEN = {"ffn": (FH, 2), "peer": (KEYS, 1)}
WEIGHTS = [("ada0", "ada0", 48), ("project0", "ab_in", 12),
           ("out00", "ab_out", 8), ("hidden00", "ffn0", 0), ("out01", "ab_out", 8), ("hidden01", "ffn0", 0),
           ("ada1", "ada1", 48), ("project1", "cd_in", 22), ("out11", "cd_out", 8), ("hidden11", "ffn1", 0),
           ("project2", "ml_in", 26), ("memory2", "kv0", 4), ("out21", "ml_out", 8), ("query2", "pq0", 16),
           ("hidden21", "peer0", 0),
           ("project3", "rg_in_r", 16), ("project3", "rg_in_q", 2), ("memory3", "kv1", 4),
           ("out31", "rg_out_q", 2), ("out31", "rg_out_r", NRB), ("query3", "pq1", 16), ("hidden31", "peer1", 0)]


def blocks_of(tensor, n):
    if n:
        return n
    tiles, unit = HIDDEN[tensor[:-1]]
    return tiles * (unit + 1)


def first_block(stage):
    total = 0
    for name, tensor, n in WEIGHTS:
        if name == stage:
            return total
        total += blocks_of(tensor, n)
    raise KeyError(stage)


def blocks_in(stage):
    return sum(blocks_of(tensor, n) for name, tensor, n in WEIGHTS if name == stage)


def after_input(stage, t, unit):
    if isinstance(t, int) and t == 0:
        return first_block(stage) + unit
    return t * (unit + 1) + (first_block(stage) + unit - 1)


def after_output(stage, t, unit):
    return t * (unit + 1) + (first_block(stage) + 2 * unit + 1)


class Chain:

    def __init__(self, eng, sem):
        self.eng, self.sem, self.n = eng, sem, 0

    def __call__(self, ins):
        self.n += 1
        ins.then_inc(self.sem, 1)
        self.eng.wait_ge(self.sem, self.n)


class RingPlace:

    def __init__(self):
        self.at = 0

    def steps(self, eng, n, unit, step):
        per = R // math.gcd(R, unit)
        if per % 2:
            per *= 2
        if self.at == 0 and n > per:
            self.steps(eng, per, unit, step)
            self.steps(eng, n - per, unit, lambda i, par, b: step(i + per, par, b))
            return
        turns = n // per
        if turns < 2:
            turns = 0
        base = self.at

        def blocks(k, it):
            out = []
            for b in range(unit):
                s = base + k * unit + b
                out.append((s % R, s // R + it * (per * unit // R), s + it * (per * unit)))
            return out

        if turns:
            with eng.Fori(0, turns) as it:
                for k in range(per):
                    step(it * per + k, k % 2, blocks(k, it))
        for i in range(turns * per, n):
            step(i, i % 2, blocks(i, 0))
        self.at += n * unit


def program(nc, a, out):
    ctx = ExitStack()
    with ctx:
        def sb(name, shape, dt=F32):
            return ctx.enter_context(nc.sbuf_tensor(name, shape, dt))

        def sem(name):
            return ctx.enter_context(nc.semaphore(name))

        C_AT, C_N = const_layout()
        Q_AT, Q_N = param_layout()
        ring = sb("ring", [P, R, D])
        consts = sb("consts", [P, C_N])
        params = sb("params", [P, Q_N])
        x = sb("x", [P, 2, KD, T])
        res = sb("res", [P, KD, T])
        mod = sb("mod", [P, 2, 48, 2])
        cond = sb("cond", [P, 2, KD, 2])
        gate_w = sb("gate_w", [P, KD, 2 * MH])
        subk = sb("subk", [P, 2, KEYS])
        cols = sb("cols", [P, 128])
        neg_lam = sb("neg_lam", [P, 1])
        eps_col = sb("eps_col", [P, 2])
        arena = sb("arena", [P, T * KEYS])
        ps = ctx.enter_context(nc.psum_tensor("ps", [P, 8, 512], F32))
        wide = ps[:, 0:4, :].rearrange("p b (c n) -> p (b c) n", c=2)
        pair = ps[:, 4:6, :]
        single = ps[:, 6:8, :]

        def const(name, rows=P, lo_row=0):
            lo, hi = C_AT[name]
            return consts[lo_row:lo_row + rows, lo:hi]

        def param(name, i=0, rows=P, n=1):
            lo = Q_AT[name][0] + i
            return params[0:rows, lo:lo + n]

        def part(off, *dims):
            v = arena[:, off:off + int(np.prod(dims))]
            if len(dims) == 2:
                v = v.rearrange("p (a b) -> p a b", a=dims[0])
            elif len(dims) == 3:
                v = v.rearrange("p (a b c) -> p a b c", a=dims[0], b=dims[1])
            return v

        def over(v, n):
            return v.unsqueeze(1).to_broadcast([v.shape[0], n, v.shape[1]])

        PROJ = 4096
        hT = part(0, KD, 2 * T)
        proj = part(PROJ, 26, 512)
        mixed = part(17408, 10, 512)
        probs = part(22528, 2, 2, 512)
        probsT = part(24576, 2, 1024)
        diag = part(26624, 4, P)
        work = part(27136, 5632)
        h2 = part(0, KD, T)
        gate = part(2048, 2, T)
        hid = part(2560, 2, T)
        G = part(0, T, KEYS)
        chosen = res[:, 0:3, :]
        spare = x[:, CTX, :, :]
        hot_i = spare[:, 0:4, :].rearrange("p a (b c) -> p (a b) c", b=2)
        hot_j = spare[:, 4:8, :].rearrange("p a (b c) -> p (a b) c", b=2)
        gelu = spare[:, 0:2, :]
        coef = spare[:, 2:4, :]

        stage = {e: sem(f"{n}_stages") for e, n in (("p", "tensor"), ("a", "scalar"), ("v", "vector"), ("g", "gpsimd"))}
        loaded = sem("loaded")
        filled = [sem(f"slot{i}_filled") for i in range(R)]
        block_used = sem("block_used")
        mem_loaded, subk_loaded, rg_loaded = sem("mem_loaded"), sem("subkeys_loaded"), sem("rg_loaded")
        tile_out = [sem("even_tile_out"), sem("odd_tile_out")]
        chain_a, chain_v = sem("scalar_chain"), sem("vector_chain")
        silu_done, ada_done = sem("silu_done"), sem("ada_done")
        squared, mean_ready, normed, turned_pos, roped = (sem(n) for n in (
            "squared", "mean_ready", "normed", "partner_ready", "roped"))
        s_ready, m_ready, e_ready, d_ready, t_ready, pt_ready, o_ready, o_out = (sem(n) for n in (
            "scores_ready", "max_ready", "exp_ready", "diag_ready", "turned", "turned_out", "heads_ready", "heads_out"))
        ln_mean, ln_centred, ln_squared, ln_var = (sem(n) for n in ("ln_mean", "ln_centred", "ln_squared", "ln_var"))
        gate_ready, hid_ready = sem("gate_ready"), sem("hid_ready")
        lam_sum, lam_exp = sem("lam_sum"), sem("lam_exp")
        pool_in, pool_out = sem("pooled"), sem("pool_mixed")
        conv_v, conv_a, conv_p = sem("conv_v"), sem("conv_a"), sem("conv_p")
        gates_p, gates_a, gates_v = sem("gates_p"), sem("gates_a"), sem("gates_v")
        m_cast, m_weight, m_mask, m_score, m_st, m_sum, m_head = (sem(n) for n in (
            "m_broadcast", "m_weights", "m_masked", "m_scores", "m_weighted", "m_summed", "m_divided"))
        mn_v, mn_p, mn_a = sem("mnorm_v"), sem("mnorm_p"), sem("mnorm_a")
        rg_v, rg_a, rg_p = sem("rglru_v"), sem("rglru_a"), sem("rglru_p")
        k_score, k_shift, k_exp, k_pick, k_turn, k_keep = (sem(n) for n in (
            "keys_scored", "picks_shifted", "picks_exp", "picks_ready", "picks_turned", "picks_kept"))
        hot_ready = [sem("hot_ready0"), sem("hot_ready1")]
        g_ready = [sem("g_ready0"), sem("g_ready1")]
        g_kept = [sem("g_kept0"), sem("g_kept1")]
        rooted = sem("rooted")
        stored = sem("stored")

        def enter(eng, name):
            for e in "pavg":
                n = stages_of(e, name)
                if n:
                    eng.wait_ge(stage[e], n)

        def units_of(l):
            units = []
            if l == 0:
                for s in (CTX, LAT):
                    for n, head in enumerate(Q_ORDER):
                        j, half, kv = n // 2, n % 2, head // 3
                        assert half == kv % 2
                        rows = slice(half * HD, (half + 1) * HD)
                        units.append(dict(
                            nk=T if s == CTX else 2 * T, diff=False, rows=(half * HD, HD),
                            q=[proj[rows, j, s * T + r * P:s * T + (r + 1) * P] for r in range(2)],
                            k=[proj[rows, 6 + kv // 2, 0:T if s == CTX else 2 * T]] * 2,
                            v=lambda c, kv=kv: proj[:, 8 + kv // 2, c * P + (kv % 2) * HD:c * P + (kv % 2 + 1) * HD],
                            out=mixed[rows, j, s * T:(s + 1) * T]))
            elif l == 1:
                for h in range(6):
                    for t in range(2):
                        units.append(dict(
                            nk=2 * T, diff=True, rows=(0, P),
                            q=[proj[r * HD:(r + 1) * HD, h, t * P:(t + 1) * P] for r in range(2)],
                            k=[proj[r * HD:(r + 1) * HD, 6 + h, :] for r in range(2)],
                            v=lambda c, h=h: proj[:, 12 + h, c * P:(c + 1) * P],
                            out=mixed[:, h, t * P:(t + 1) * P]))
            else:
                for h in range(4):
                    j, half = h // 2, h % 2
                    rows = slice(half * HD, (half + 1) * HD)
                    units.append(dict(
                        nk=T, diff=False, rows=(half * HD, HD),
                        q=[proj[rows, 24 + j, r * P:(r + 1) * P] for r in range(2)],
                        k=[proj[rows, j, 0:T]] * 2,
                        v=lambda c, j=j, half=half: proj[:, 2 + j, c * P + half * HD:c * P + (half + 1) * HD],
                        out=mixed[rows, (6 if l == 2 else 8) + j, 0:T]))
            return units

        def scores_at(i, nk):
            return ps[:, 2 * (i % 2):2 * (i % 2) + 2, 0:nk]

        def m_tiles(h, first):
            half = slice((h % 2) * HD, (h % 2 + 1) * HD)
            return [(slice(0, P), first + h), (half, first + 4 + h // 2)]

        block = ctx.enter_context(nc.Block())

        @block.sync
        def _(sp):
            for dst, src in ((cond[:, 0, :, :], a["cond"]), (x[:, CTX, :, :], a["ctx"]), (x[:, LAT, :, :], a["x"]),
                             (params[:, :], a["params"]), (consts[:, :], a["consts"]), (gate_w[:, :, :], a["gate_w"])):
                sp.dma_start(dst, src).then_inc(loaded, 16)
            place = RingPlace()

            def fetch(t, i, blk):
                slot, _, seq = blk
                src = t[i, :, :] if isinstance(i, int) else t[bass.ds(i, 1), :, :].rearrange("o p n -> (o p) n")
                if not isinstance(seq, int) or seq >= R:
                    sp.wait_ge(block_used, seq - (R - 1))
                sp.dma_start(ring[0:t.shape[1], slot, 0:t.shape[2]], src).then_inc(filled[slot], 16)

            def stream(t, n):
                place.steps(sp, n, 1, lambda i, par, b: fetch(t, i, b[0]))

            def stream_hidden(w_in, w_out, n, unit):
                def one(i, par, b):
                    for j in range(unit):
                        fetch(w_in, (i + 1) * unit + j, b[j])
                    fetch(w_out, i, b[unit])
                place.steps(sp, unit, 1, lambda i, par, b: fetch(w_in, i, b[0]))
                place.steps(sp, n - 1, unit + 1, one)
                place.steps(sp, 1, 1, lambda i, par, b: fetch(w_out, n - 1, b[0]))

            for _, name, n in WEIGHTS:
                if n:
                    stream(a[name], n)
                elif name.startswith("ffn"):
                    stream_hidden(a[name + "_in"], a[name + "_out"], FH, 2)
                else:
                    stream_hidden(a[name + "_u"], a[name + "_v"], KEYS, 1)

        @block.gpsimd
        def _(pool):
            enter(pool, "mlstm")
            for h in range(MH):
                for c in range(2):
                    pool.wait_ge(m_weight, 3 * h + c + 1)
                    w = work[:, (2 * (h % 2) + c) * T:(2 * (h % 2) + c + 1) * T]
                    nc.gpsimd.affine_select(out=w, in_=w, compare_op=ALU.is_ge, fill=0.0, base=-P * c,
                                            pattern=[[1, T]], channel_multiplier=-1).then_inc(m_mask, 1)
            pool.drain().then_inc(stage["g"], 1)
            for l in (2, 3):
                if l == 3:
                    enter(pool, "project3")
                    pool.dma_start(work[0:RB, 2560:2560 + 2 * NRB * RB], a["rg_w"]).then_inc(rg_loaded, 16)
                enter(pool, f"memory{l}")
                pool.dma_start(hT[:, :, 0:T], a["mem"]).then_inc(mem_loaded, 16)
                pool.dma_start(subk[:, :, :], a[f"subk{l - 2}"]).then_inc(subk_loaded, 16)
            for e in "pav":
                pool.wait_ge(stage[e], stages_of(e, f"norm23{LAT}") + 1)
            pool.dma_start(out, x[:, LAT, :, :]).then_inc(stored, 16)
            pool.wait_ge(stored, 16)

        @block.tensor
        def _(pe):
            place = RingPlace()
            n_tiles, n_out = [0], [0, 0]
            n_unit, n_ln, n_hid, n_mean = [0], [0], [0], [0]
            mm = nc.tensor.matmul

            def leave():
                pe.drain().then_inc(stage["p"], 1)

            def wait_filled(blk):
                slot, turn, _ = blk
                pe.wait_ge(filled[slot], (turn + 1) * 16)

            def ada(l):
                enter(pe, f"ada{l}")
                pe.wait_ge(loaded, 16 * 6)
                pe.wait_ge(silu_done, 1)

                def one(m, par, b):
                    wait_filled(b[0])
                    dst = pair[:, 0, 2 * m:2 * m + 2] if isinstance(m, int) else pair[:, 0, bass.ds(m * 2, 2)]
                    for k in range(KD):
                        last = mm(dst, ring[:, b[0][0], k * P:(k + 1) * P], cond[:, 1, k, :],
                                  start=(k == 0), stop=(k == KD - 1))
                    last.then_inc(block_used, 1)
                place.steps(pe, 48, 1, one)
                pe.drain().then_inc(ada_done, 1)
                leave()

            def project(src, runs):
                for _, n, t0, nt, form, width in runs:
                    def one(m, par, b):
                        wait_filled(b[0])
                        if isinstance(m, int):
                            if n_out[par] + m // 2:
                                pe.wait_ge(tile_out[par], n_out[par] + m // 2)
                        else:
                            pe.wait_ge(tile_out[par], m // 2 + n_out[par])
                        w = ring[:, b[0][0], 0:KD * width].rearrange("p (k c) -> p k c", k=KD)
                        if form == FEATURES:
                            for k in range(KD):
                                last = mm(pair[0:width, par, 0:nt], w[:, k, :], src[:, k, t0:t0 + nt],
                                          start=(k == 0), stop=(k == KD - 1))
                        else:
                            for t in range(nt // P):
                                for k in range(KD):
                                    last = mm(pair[:, par, t * P:(t + 1) * P],
                                              src[:, k, t0 + t * P:t0 + (t + 1) * P], w[:, k, :],
                                              start=(k == 0), stop=(k == KD - 1))
                        last.then_inc(block_used, 1)

                    place.steps(pe, n, 1, one)
                    n_tiles[0] += n
                    n_out[0] += (n + 1) // 2
                    n_out[1] += n // 2
                leave()

            def means(name, ones, n, tiles):
                enter(pe, name)
                for i in range(tiles):
                    pe.wait_ge(squared, n_mean[0] + i + 1)
                    if n_mean[0] + i >= 2:
                        pe.wait_ge(normed, n_mean[0] + i - 1)
                    mm(pair[:, i % 2, 0:n], const(ones), work[:, (i % 2) * 512:(i % 2) * 512 + n],
                       start=True, stop=True).then_inc(mean_ready, 1)
                n_mean[0] += tiles
                leave()

            def rope(l):
                enter(pe, f"rope{l}")
                base = len(ROPE[0]) if l else 0
                for i, (j, lat) in enumerate(ROPE[l]):
                    if base + i >= 2:
                        pe.wait_ge(roped, base + i - 1)
                    mm(pair[:, i % 2, 0:T], const("rot"), proj[:, j, lat:lat + T],
                       start=True, stop=True).then_inc(turned_pos, 1)
                leave()

            def attend(l):
                units = units_of(l)
                enter(pe, f"attend{l}")
                base = n_unit[0]

                def scores(i):
                    u = units[i]
                    if base + i >= 2:
                        pe.wait_ge(e_ready, base + i - 1)
                    for r in range(2):
                        last = mm(scores_at(i, u["nk"])[:, r, :], u["q"][r], u["k"][r], start=True, stop=True)
                    last.then_inc(s_ready, 1)

                def turn(i):
                    u = units[i]
                    pe.wait_ge(d_ready, base + i + 1)
                    if base + i:
                        pe.wait_ge(pt_ready, base + i)
                    for c in range(u["nk"] // P):
                        for r in range(2):
                            e = probs[:, i % 2, r, c * P:(c + 1) * P]
                            dg = diag[:, 2 * (i % 2) + r, :]
                            if u["diff"]:
                                last = mm(pair[:, 0, c * P:(c + 1) * P], e, dg, start=(r == 0), stop=(r == 1))
                            else:
                                at = (c % 2) * T + r * P
                                last = mm(pair[:, c // 2, at:at + P], e, dg, start=True, stop=True)
                    last.then_inc(t_ready, 1)

                def heads(i):
                    u = units[i]
                    pe.wait_ge(pt_ready, base + i + 1)
                    if base + i >= 2:
                        pe.wait_ge(o_out, base + i - 1)
                    nq = P if u["diff"] else 2 * P
                    lo, m = u["rows"]
                    chunks = u["nk"] // P
                    for c in range(chunks):
                        last = mm(single[lo:lo + m, i % 2, 0:nq], u["v"](c), probsT[:, i % 2, c * nq:(c + 1) * nq],
                                  start=(c == 0), stop=(c == chunks - 1))
                    last.then_inc(o_ready, 1)

                n = len(units)
                scores(0)
                for i in range(n):
                    if i + 1 < n:
                        scores(i + 1)
                    if i:
                        heads(i - 1)
                    turn(i)
                heads(n - 1)
                n_unit[0] += n
                leave()

            def accumulate(rhs, blk, rows, first, final):
                for m in range(KD):
                    last = mm(wide[:, m, :], ring[0:rows, blk[0], m * P:(m + 1) * P], rhs,
                              start=(first and m % 2 == 0), stop=final, skip_group_check=True)
                return last

            def out_project(name, tiles):
                enter(pe, name)

                def one(i, par, b):
                    rhs, rows = tiles[i]
                    wait_filled(b[0])
                    last = accumulate(rhs, b[0], rows, i == 0, i == len(tiles) - 1)
                    last.then_inc(block_used, 1)
                for i in range(len(tiles)):
                    place.steps(pe, 1, 1, lambda _, par, b: one(i, par, b))
                leave()

            def norm(name):
                enter(pe, name)
                for k in range(KD):
                    last = mm(pair[:, 0, 0:T], const("mean_d"), res[:, k, :], start=(k == 0), stop=(k == KD - 1))
                last.then_inc(ln_mean, 1)
                pe.wait_ge(ln_squared, n_ln[0] + 1)
                for k in range(KD):
                    last = mm(pair[:, 1, 0:T], const("mean_d"), work[:, k * T:(k + 1) * T],
                              start=(k == 0), stop=(k == KD - 1))
                last.then_inc(ln_var, 1)
                n_ln[0] += 1
                leave()

            def hidden(name, n, unit, src, rhs):
                enter(pe, name)
                base = n_hid[0]

                def go_in(t, par, blks):
                    if not isinstance(t, int) or base + t >= 2:
                        pe.wait_ge(hid_ready, t + (base - 1))
                    for j in range(unit):
                        wait_filled(blks[j])
                        for k in range(KD):
                            last = mm(pair[:, par, j * T:(j + 1) * T], ring[:, blks[j][0], k * P:(k + 1) * P],
                                      src[:, k, :], start=(k == 0), stop=(k == KD - 1))
                        last.then_inc(block_used, 1)

                def go_out(t, par, blk, first=False, final=False):
                    pe.wait_ge(hid_ready, t + (base + 1))
                    wait_filled(blk)
                    accumulate(rhs[:, par, :], blk, P, first, final).then_inc(block_used, 1)

                def both(i, par, b, first=False):
                    go_in(i + 1, 1 - par, b)
                    go_out(i, par, b[unit], first)

                ins = []
                place.steps(pe, unit, 1, lambda i, par, b: ins.append(b[0]))
                go_in(0, 0, ins)
                place.steps(pe, 1, unit + 1, lambda i, par, b: both(0, 0, b, first=True))
                place.steps(pe, n - 2, unit + 1, lambda i, par, b: both(i + 1, 1 - par, b))
                place.steps(pe, 1, 1, lambda i, par, b: go_out(n - 1, (n - 1) % 2, b[0], final=True))
                n_hid[0] += n
                leave()

            def pool_mix():
                enter(pe, "pool")
                for s in range(2):
                    pe.wait_ge(pool_in, s + 1)
                    for n in range(2):
                        at = 2880 + (2 * s + n) * T
                        last = mm(ps[:, 4 + 2 * s + n, 0:T], param("pool_w", n * P, n=P), work[:, at:at + T],
                                  start=True, stop=True)
                    last.then_inc(pool_out, 1)
                leave()

            def conv_norm():
                enter(pe, "conv")
                for i, at in enumerate((0, 512)):
                    pe.wait_ge(conv_v if i == 0 else conv_a, 1 if i == 0 else 2)
                    for k in range(2):
                        last = mm(pair[:, i, 0:T], const("mean_256"), work[:, at + k * T:at + (k + 1) * T],
                                  start=(k == 0), stop=(k == 1))
                    last.then_inc(conv_p, 1)
                leave()

            def gates():
                enter(pe, "gates")
                for g in range(2):
                    for k in range(KD):
                        last = mm(pair[0:MH, g, 0:T], gate_w[:, k, g * MH:(g + 1) * MH], x[:, LAT, k, :],
                                  start=(k == 0), stop=(k == KD - 1))
                last.then_inc(gates_p, 1)
                pe.wait_ge(gates_v, 2)
                for c in range(2):
                    last = mm(single[:, 0, c * MH:(c + 1) * MH], work[0:MH, 2048 + c * P:2048 + (c + 1) * P],
                              const("ident", MH)[:, 0:MH], start=True, stop=True)
                last.then_inc(gates_p, 1)
                leave()

            def mlstm():
                enter(pe, "mlstm")

                def spread_rows(h):
                    if h >= 2:
                        pe.wait_ge(m_weight, 3 * (h - 1))
                    for i, at in enumerate((2304, 2560)):
                        last = mm(pair[:, h % 2, i * T:(i + 1) * T], const("head_rows", MH)[:, h * P:(h + 1) * P],
                                  work[0:MH, at:at + T], start=True, stop=True)
                    last.then_inc(m_cast, 1)

                def score(h):
                    if h >= 2:
                        pe.wait_ge(m_st, h - 1)
                    for c in range(2):
                        for i, ((rows, kt), (_, qt)) in enumerate(zip(m_tiles(h, 6), m_tiles(h, 0))):
                            last = mm(wide[:, 4 * (h % 2) + c, :], proj[rows, kt, c * P:(c + 1) * P],
                                      proj[rows, qt, 0:T], start=(i == 0), stop=(i == 1))
                    last.then_inc(m_score, 1)

                def sums(h):
                    pe.wait_ge(m_st, h + 1)
                    if h >= 2:
                        pe.wait_ge(m_head, h - 1)
                    (_, ta), (half, tb) = m_tiles(h, 12)
                    w = [work[:, (2 * (h % 2) + c) * T:(2 * (h % 2) + c + 1) * T] for c in range(2)]
                    for c in range(2):
                        mm(wide[:, 4 * (h % 2) + 2, :], proj[:, ta, c * P:(c + 1) * P], w[c],
                           start=(c == 0), stop=(c == 1))
                    for c in range(2):
                        mm(single[half, h % 2, 0:T], proj[:, tb, c * P + half.start:c * P + half.stop], w[c],
                           start=(c == 0), stop=(c == 1))
                    for c in range(2):
                        last = mm(wide[:, 4 * (h % 2) + 3, :], const("ones"), w[c], start=(c == 0), stop=(c == 1))
                    last.then_inc(m_sum, 1)

                for h in range(MH):
                    spread_rows(h)
                    score(h)
                    if h:
                        sums(h - 1)
                sums(MH - 1)
                leave()

            def mlstm_norm():
                enter(pe, "mlstm_norm")
                for v in range(2):
                    if v:
                        pe.wait_ge(mn_a, 1)
                    for h in range(MH):
                        for i, (_, t) in enumerate(m_tiles(h, 0)):
                            src = work[:, t * T:(t + 1) * T] if v else mixed[:, t, 0:T]
                            ones = const("mean_192_half")[:, (h % 2) * P:(h % 2 + 1) * P] if i else const("mean_192")
                            last = mm(wide[:, 4 * v + h, :], ones, src, start=(i == 0), stop=(i == 1))
                    last.then_inc(mn_p, 1)
                leave()

            def rglru():
                enter(pe, "rglru")
                pe.wait_ge(rg_loaded, 16)
                w = work[0:RB, 2560:2560 + 2 * NRB * RB].rearrange("p (g c) -> p g c", c=RB)
                pe.wait_ge(rg_v, 1)
                for g in range(2 * NRB):
                    dst = ps[0:RB, g // 2, (g % 2) * T:(g % 2 + 1) * T]
                    last = mm(dst, w[:, g, :], arena[0:RB, (g % NRB) * T:(g % NRB + 1) * T], start=True, stop=True)
                last.then_inc(rg_p, 1)
                leave()

            def choose(l):
                enter(pe, f"choose{l}")
                pe.wait_ge(subk_loaded, 16 * (l - 1))
                for t in range(2):
                    for n in range(2 * PH):
                        last = mm(ps[:, 4 * t + n // 4, (n % 4) * P:(n % 4 + 1) * P],
                                  proj[:, n, t * P:(t + 1) * P], subk[:, n % 2, :], start=True, stop=True)
                    last.then_inc(k_score, 1)
                for t in range(2):
                    pe.wait_ge(k_pick, 2 * (l - 2) + t + 1)
                    for i in range(3):
                        last = mm(ps[:, 4 * t, i * P:(i + 1) * P], part(22528 + i * P, P), const("ident"),
                                  start=True, stop=True)
                    last.then_inc(k_turn, 1)
                leave()

            def spread(l):
                enter(pe, f"spread{l}")
                base = (l - 2) * (T // 8)

                def one(it):
                    for half in range(2):
                        pe.wait_ge(hot_ready[half], it + (base + 1))
                        if not isinstance(it, int) or it + base:
                            pe.wait_ge(g_kept[half], it + base)
                        for u in range(4):
                            last = mm(ps[:, half, u * P:(u + 1) * P], hot_i[:, 4 * half + u, :],
                                      hot_j[:, 4 * half + u, :], start=True, stop=True)
                        last.then_inc(g_ready[half], 1)
                one(0)
                with pe.Fori(1, T // 8) as it:
                    one(it)
                leave()

            for l in range(2):
                ada(l)
                enter(pe, f"project{l}")
                project(hT, PROJECT[l])
                if l == 0:
                    means("heads_norm", "mean_64", 2 * T, 8)
                rope(l)
                attend(l)
                if l == 0:
                    pool_mix()
                else:
                    means("subln", "mean_128", T, 6)
                    conv_norm()
                for n in ((CTX, LAT) if l == 0 else (LAT,)):
                    lo = n * T if l == 0 else 0
                    out_project(f"out{l}{n}", [(mixed[:, k, lo:lo + T], P) for k in range(KD)])
                    norm(f"norm1{l}{n}")
                    hidden(f"hidden{l}{n}", FH, 2, h2, hid)
                    norm(f"norm2{l}{n}")
            for l in (2, 3):
                enter(pe, f"project{l}")
                project(x[:, LAT, :, :], PROJECT[l])
                if l == 2:
                    gates()
                    mlstm()
                    mlstm_norm()
                    tiles = [(mixed[:, k, 0:T], P) for k in range(KD)]
                else:
                    rglru()
                    tiles = [(mixed[:, k, 0:T], P) for k in (8, 9)] + [(mixed[0:RB, k, 0:T], RB) for k in range(NRB)]
                enter(pe, f"memory{l}")
                pe.wait_ge(mem_loaded, 16 * (l - 1))
                project(hT, PROJECT_MEMORY)
                attend(l)
                out_project(f"out{l}{LAT}", tiles)
                norm(f"norm1{l}{LAT}")
                enter(pe, f"query{l}")
                project(x[:, LAT, :, :], PROJECT_QUERY)
                choose(l)
                spread(l)
                hidden(f"hidden{l}{LAT}", KEYS, 1, x[:, LAT, :, :], coef)
                norm(f"norm2{l}{LAT}")

        def copy_tiles(eng, par, copy, name, runs):
            done = first_block(name)
            for first, n, _, nt, _, width in runs:
                mine = (n + 1 - par) // 2

                def one(i):
                    eng.wait_ge(block_used, 2 * i + (done + par + 1))
                    at = PROJ + (first + 2 * i + par) * 512
                    dst = arena[0:width, at:at + nt] if isinstance(i, int) else \
                        arena[0:width, bass.ds(i * 1024 + (PROJ + (first + par) * 512), nt)]
                    copy(dst, pair[0:width, par, 0:nt]).then_inc(tile_out[par], 1)
                if mine > 2:
                    with eng.Fori(0, mine) as it:
                        one(it)
                else:
                    for i in range(mine):
                        one(i)
                done += n

        def hidden_pairs(eng, n, step):
            for t in range(2):
                step(t, t)
            with eng.Fori(1, n // 2) as it:
                for par in range(2):
                    step(it * 2 + par, par)

        @block.scalar
        def _(act):
            chain = Chain(act, chain_a)
            n_unit, n_ln, n_hid, n_sq = [0], [0], [0], [0]
            f = nc.scalar.activation

            def leave():
                act.drain().then_inc(stage["a"], 1)

            def project(name, runs):
                enter(act, name)
                copy_tiles(act, 0, lambda o, i: f(o, i, ACT.Copy), name, runs)
                leave()

            def root(dst, src, eps):
                f(dst, src, ACT.Sqrt, bias=eps_col[0:dst.shape[0], eps:eps + 1]).then_inc(rooted, 1)

            def squares(name, tiles):
                enter(act, name)
                for i in range(len(tiles) + 1):
                    if i < len(tiles):
                        n = tiles[i].shape[1]
                        if i >= 2:
                            act.wait_ge(mean_ready, n_sq[0] + i - 1)
                        f(work[:, (i % 2) * 512:(i % 2) * 512 + n], tiles[i], ACT.Square).then_inc(squared, 1)
                    if i:
                        b = (i - 1) % 2
                        act.wait_ge(mean_ready, n_sq[0] + i)
                        if i >= 3:
                            act.wait_ge(normed, n_sq[0] + i - 2)
                        root(work[:, 1024 + b * 512:1024 + b * 512 + n], pair[:, b, 0:n], 0)
                n_sq[0] += len(tiles)
                leave()

            def attend(l):
                units = units_of(l)
                enter(act, f"attend{l}")
                base = n_unit[0]

                def exps(i):
                    act.wait_ge(m_ready, base + i + 1)
                    if base + i >= 2:
                        act.wait_ge(t_ready, base + i - 1)
                    b = 4 * (i % 2)
                    for r in range(2):
                        last = f(probs[:, i % 2, r, 0:units[i]["nk"]], scores_at(i, units[i]["nk"])[:, r, :], ACT.Exp,
                                 bias=cols[:, 8 + b + r:9 + b + r], scale=HD ** -0.5,
                                 accum_out=cols[:, 16 + b + r:17 + b + r])
                    last.then_inc(e_ready, 1)

                def heads(i):
                    u = units[i]
                    act.wait_ge(o_ready, base + i + 1)
                    lo, m = u["rows"]
                    f(u["out"], single[lo:lo + m, i % 2, 0:P if u["diff"] else 2 * P], ACT.Copy).then_inc(o_out, 1)

                n = len(units)
                exps(0)
                for i in range(n):
                    if i + 1 < n:
                        exps(i + 1)
                    if i:
                        heads(i - 1)
                heads(n - 1)
                n_unit[0] += n
                leave()

            def norm(name):
                enter(act, name)
                act.wait_ge(ln_centred, n_ln[0] + 1)
                f(work[:, 0:KD * T], res[:, :, :].rearrange("p k t -> p (k t)"), ACT.Square).then_inc(ln_squared, 1)
                n_ln[0] += 1
                act.wait_ge(ln_var, n_ln[0])
                root(work[:, 4096:4096 + T], pair[:, 1, 0:T], 0 if name[5] in "01" else 1)
                leave()

            def hidden(name, n, unit, func, at, dst):
                enter(act, name)
                base = n_hid[0]

                def one(t, par):
                    act.wait_ge(block_used, after_input(name, t, unit))
                    if not isinstance(t, int) or base + t >= 2:
                        act.wait_ge(hid_ready, t + (base - 1))
                    f(dst[:, par, :], pair[:, par, at:at + T], func).then_inc(gate_ready, 1)
                hidden_pairs(act, n, one)
                n_hid[0] += n
                leave()

            enter(act, "lambda")
            act.wait_ge(lam_sum, 1)
            f(cols[:, 34:36], cols[:, 32:34], ACT.Exp).then_inc(lam_exp, 1)
            leave()
            for l in range(2):
                if l == 0:
                    enter(act, "ada0")
                    act.wait_ge(loaded, 16 * 6)
                    f(cond[:, 1, :, :], cond[:, 0, :, :], ACT.Silu).then_inc(silu_done, 1)
                    leave()
                project(f"project{l}", PROJECT[l])
                if l == 0:
                    squares("heads_norm", [proj[:, j, :] for j in range(8)])
                attend(l)
                if l == 1:
                    squares("subln", [mixed[:, h, 0:T] for h in range(6)])
                    enter(act, "conv")
                    f(work[:, 2048:2560].rearrange("p (k t) -> p k t", k=2), proj[:, 20:22, 0:T],
                      ACT.Sigmoid).then_inc(conv_a, 1)
                    act.wait_ge(conv_v, 2)
                    f(work[:, 512:1024], work[:, 0:512], ACT.Square).then_inc(conv_a, 1)
                    act.wait_ge(conv_p, 2)
                    root(work[:, 1024:1024 + T], pair[:, 1, 0:T], 0)
                    for k in range(2):
                        act.wait_ge(conv_v, 3)
                        f(mixed[:, 6 + k, 0:T], work[:, k * T:(k + 1) * T], ACT.Silu,
                          bias=param("conv_bb", k), scale=param("conv_g", k)).then_inc(conv_a, 1)
                    leave()
                for n in ((CTX, LAT) if l == 0 else (LAT,)):
                    norm(f"norm1{l}{n}")
                    hidden(f"hidden{l}{n}", FH, 2, ACT.Silu, T, gate)
                    norm(f"norm2{l}{n}")
            for l in (2, 3):
                project(f"project{l}", PROJECT[l])
                if l == 2:
                    enter(act, "gates")
                    act.wait_ge(gates_v, 1)
                    f(work[0:MH, 768:1024], work[0:MH, 512:768], ACT.Exp, scale=-1.0).then_inc(gates_a, 1)
                    leave()
                    enter(act, "mlstm")
                    for h in range(MH):
                        act.wait_ge(m_cast, h + 1)
                        if h >= 2:
                            act.wait_ge(m_sum, h - 1)
                            act.wait_ge(m_head, h - 1)
                        for c in range(2):
                            at = (2 * (h % 2) + c) * T
                            f(work[:, at:at + T], pair[:, h % 2, 0:T], ACT.Exp, scale=-1.0,
                              bias=cols[:, c * MH + h:c * MH + h + 1]).then_inc(m_weight, 1)
                        f(work[:, 1024 + (h % 2) * T:1024 + (h % 2 + 1) * T], pair[:, h % 2, T:2 * T],
                          ACT.Exp).then_inc(m_weight, 1)
                    leave()
                    enter(act, "mlstm_norm")
                    act.wait_ge(mn_v, 1)
                    f(work[:, 0:6 * T].rearrange("p (k t) -> p k t", k=6), mixed[:, 0:6, 0:T],
                      ACT.Square).then_inc(mn_a, 1)
                    act.wait_ge(mn_p, 2)
                    root(work[:, 2048:2048 + MH * T].rearrange("p (h t) -> p h t", h=MH), wide[:, 4:8, :], 1)
                    f(proj[:, 18:24, 0:T], proj[:, 18:24, 0:T], ACT.Sigmoid).then_inc(mn_a, 1)
                    leave()
                else:
                    enter(act, "rglru")
                    rg = {"r": 2048, "i": 12288, "a": 14336, "t": 22528}
                    act.wait_ge(rg_v, 1)
                    f(cols[0:RB, 16:24], cols[0:RB, 8:16], ACT.Exp, scale=-1.0).then_inc(rg_a, 1)
                    act.wait_ge(rg_p, 1)
                    for g in range(NRB):
                        f(arena[0:RB, 2048 + g * T:2048 + (g + 1) * T], ps[0:RB, g // 2, (g % 2) * T:(g % 2 + 1) * T],
                          ACT.Sigmoid, bias=param("r_ba", g, RB))
                        last = f(arena[0:RB, 12288 + g * T:12288 + (g + 1) * T],
                                 ps[0:RB, 4 + g // 2, (g % 2) * T:(g % 2 + 1) * T],
                                 ACT.Sigmoid, bias=param("r_bx", g, RB))
                    last.then_inc(rg_a, 1)
                    act.wait_ge(rg_a, 2)
                    act.wait_ge(rg_v, 2)
                    for g in range(NRB):
                        r_g = arena[0:RB, 2048 + g * T:2048 + (g + 1) * T]
                        f(arena[0:RB, 14336 + g * T:14336 + (g + 1) * T], r_g, ACT.Exp,
                          scale=cols[0:RB, 24 + g:25 + g])
                        last = f(arena[0:RB, 22528 + g * T:22528 + (g + 1) * T], r_g, ACT.Tanh,
                                 scale=cols[0:RB, 32 + g:33 + g])
                    last.then_inc(rg_a, 1)
                    act.wait_ge(rg_v, 3)
                    i_ = arena[0:RB, 12288:12288 + NRB * T]
                    f(i_, i_, ACT.Sqrt).then_inc(rooted, 1)
                    f(proj[0:RB, 0:NRB, 0:T], proj[0:RB, 0:NRB, 0:T], ACT.Gelu).then_inc(rg_a, 1)
                    leave()
                project(f"memory{l}", PROJECT_MEMORY)
                attend(l)
                norm(f"norm1{l}{LAT}")
                project(f"query{l}", PROJECT_QUERY)
                enter(act, f"choose{l}")
                for t in range(2):
                    act.wait_ge(k_shift, 2 * (l - 2) + t + 1)
                    f(part(22016, P), part(22016, P), ACT.Exp).then_inc(k_exp, 1)
                for t in range(2):
                    act.wait_ge(k_turn, 2 * (l - 2) + t + 1)
                    f(chosen[:, :, t * P:(t + 1) * P], ps[:, 4 * t, 0:3 * P].rearrange("p (a b) -> p a b", a=3),
                      ACT.Copy).then_inc(k_keep, 1)
                leave()
                enter(act, f"spread{l}")
                base = (l - 2) * (T // 8)
                with act.Fori(0, T // 8) as it:
                    for half in range(2):
                        act.wait_ge(g_ready[half], it + (base + 1))
                        f(arena[:, bass.ds(it * (8 * KEYS) + half * 4 * KEYS, 4 * KEYS)], ps[:, half, :],
                          ACT.Copy).then_inc(g_kept[half], 1)
                leave()
                hidden(f"hidden{l}{LAT}", KEYS, 1, ACT.Gelu, 0, gelu)
                norm(f"norm2{l}{LAT}")

        @block.vector
        def _(dve):
            chain = Chain(dve, chain_v)
            n_unit, n_ln, n_hid, n_sq, n_root = [0], [0], [0], [0], [0]
            v = nc.vector

            def leave():
                dve.drain().then_inc(stage["v"], 1)

            def project(name, runs):
                enter(dve, name)
                copy_tiles(dve, 1, v.tensor_copy, name, runs)
                leave()

            def inverse_root(t):
                n_root[0] += 1
                dve.wait_ge(rooted, n_root[0])
                chain(v.reciprocal(t, t))

            def heads_norm(name, tiles, gain, factor):
                enter(dve, name)
                chain(v.tensor_scalar(cols[:, 40:41], gain, factor, None, ALU.mult))
                for i, t in enumerate(tiles):
                    n = t.shape[1]
                    r = work[:, 1024 + (i % 2) * 512:1024 + (i % 2) * 512 + n]
                    inverse_root(r)
                    g = gain if name != "heads_norm" else (param("q_gain") if i < 6 else param("k_gain"))
                    v.scalar_tensor_tensor(t, t, cols[:, 40:41] if name != "heads_norm" else g, r,
                                           ALU.mult, ALU.mult).then_inc(normed, 1)
                n_sq[0] += len(tiles)
                leave()

            def rope(l):
                enter(dve, f"rope{l}")
                base = len(ROPE[0]) if l else 0
                for i, (j, lat) in enumerate(ROPE[l]):
                    t = proj[:, j, lat:lat + T]
                    s = work[:, (i % 2) * T:(i % 2 + 1) * T]
                    dve.wait_ge(turned_pos, base + i + 1)
                    v.tensor_tensor(s, pair[:, i % 2, 0:T], const("sin"), ALU.mult)
                    chain(v.tensor_tensor(t, t, const("cos"), ALU.mult))
                    v.tensor_tensor(t, t, s, ALU.add).then_inc(roped, 1)
                leave()

            def attend(l):
                units = units_of(l)
                enter(dve, f"attend{l}")
                base = n_unit[0]

                def maxima(i):
                    b = 4 * (i % 2)
                    dve.wait_ge(s_ready, base + i + 1)
                    chain(v.tensor_reduce(cols[:, b:b + 2], scores_at(i, units[i]["nk"]), AX_X, ALU.max))
                    v.tensor_scalar(cols[:, 8 + b:10 + b], cols[:, b:b + 2], -HD ** -0.5, None,
                                    ALU.mult).then_inc(m_ready, 1)

                def diagonals(i):
                    b = 4 * (i % 2)
                    dve.wait_ge(e_ready, base + i + 1)
                    chain(v.reciprocal(cols[:, 24 + b:26 + b], cols[:, 16 + b:18 + b]))
                    for r in range(2):
                        second = neg_lam[:, 0:1] if units[i]["diff"] and r else None
                        op = (ALU.mult, ALU.mult) if second is not None else (ALU.mult,)
                        last = v.tensor_scalar(diag[:, 2 * (i % 2) + r, :], const("ident"),
                                               cols[:, 24 + b + r:25 + b + r], second, *op)
                    last.then_inc(d_ready, 1)

                def turned(i):
                    u = units[i]
                    dve.wait_ge(t_ready, base + i + 1)
                    if base + i >= 2:
                        dve.wait_ge(o_ready, base + i - 1)
                    n = u["nk"] * (1 if u["diff"] else 2)
                    v.tensor_copy(probsT[:, i % 2, 0:n], ps[:, 4:6, :].rearrange("p b n -> p (b n)")[:, 0:n])\
                        .then_inc(pt_ready, 1)

                n = len(units)
                maxima(0)
                for i in range(n):
                    diagonals(i)
                    if i + 1 < n:
                        maxima(i + 1)
                    turned(i)
                n_unit[0] += n
                leave()

            def gated_sum(name, s, l, part_):
                j = 1 if s == CTX else 0
                chain(v.tensor_scalar(res[:, :, :], x[:, s, :, :], ALPHA, None, ALU.mult))
                dve.wait_ge(block_used, first_block(name) + blocks_in(name))
                for k in range(KD):
                    m = part_ * KD + k
                    v.scalar_tensor_tensor(res[:, k, :], wide[:, k, :], mod[:, l, m, j:j + 1], res[:, k, :],
                                           ALU.mult, ALU.add)

            def plain_sum(name):
                dve.wait_ge(block_used, first_block(name) + blocks_in(name))
                v.scalar_tensor_tensor(res[:, :, :], x[:, LAT, :, :], ALPHA, wide, ALU.mult, ALU.add)

            def norm(name, s, ln, k12, eps):
                enter(dve, name)
                n_ln[0] += 1
                dve.wait_ge(ln_mean, n_ln[0])
                v.tensor_tensor(res[:, :, :], res[:, :, :], over(pair[:, 0, 0:T], KD), ALU.subtract)\
                    .then_inc(ln_centred, 1)
                inverse_root(work[:, 4096:4096 + T])
                chain(v.tensor_tensor(res[:, :, :], res[:, :, :], over(work[:, 4096:4096 + T], KD), ALU.mult))
                for k in range(KD):
                    v.tensor_scalar(x[:, s, k, :], res[:, k, :], param(f"ln{ln}g{k12}", k), param(f"ln{ln}b{k12}", k),
                                    ALU.mult, ALU.add)
                leave()

            def hidden(name, n, unit, step):
                base = n_hid[0]

                def one(t, par):
                    dve.wait_ge(gate_ready, t + (base + 1))
                    if not isinstance(t, int) or t >= 2:
                        dve.wait_ge(block_used, after_output(name, t - 2, unit))
                    step(t, par).then_inc(hid_ready, 1)
                hidden_pairs(dve, n, one)
                n_hid[0] += n

            def swiglu(t, par):
                return v.tensor_tensor(hid[:, par, :], pair[:, par, 0:T], gate[:, par, :], ALU.mult)

            def weigh(t, par):
                g = G[:, :, t] if isinstance(t, int) else G[:, :, bass.ds(t, 1)].rearrange("p n o -> p (n o)")
                return v.tensor_tensor(coef[:, par, :], gelu[:, par, :], g, ALU.mult)

            def pool_windows():
                enter(dve, "pool")
                W = T + 32
                U, S2, S4, S8, S16 = (work[:, i * 2 * W:(i + 1) * 2 * W].rearrange("p (n t) -> p n t", n=2)
                                      for i in range(5))
                chain(v.memset(work[:, 0:10 * W], 0.0))
                for s in range(2):
                    chain(v.tensor_copy(U[:, :, 16:16 + T], proj[:, 10:12, s * T:(s + 1) * T]))
                    chain(v.tensor_tensor(S2[:, :, 1:W], U[:, :, 0:W - 1], U[:, :, 1:W], ALU.add))
                    chain(v.tensor_tensor(S4[:, :, 2:W - 1], S2[:, :, 1:W - 2], S2[:, :, 3:W], ALU.add))
                    chain(v.tensor_tensor(S8[:, :, 4:W - 3], S4[:, :, 2:W - 5], S4[:, :, 6:W - 1], ALU.add))
                    chain(v.tensor_tensor(S16[:, :, 8:W - 7], S8[:, :, 4:W - 11], S8[:, :, 12:W - 3], ALU.add))
                    pooled = work[:, 10 * W + 2 * s * T:10 * W + 2 * (s + 1) * T].rearrange("p (n t) -> p n t", n=2)
                    inv = const("inv_count").rearrange("p (n t) -> p n t", n=2)
                    for g, S in enumerate((S2, S4, S8, S16)):
                        rows, n = slice((g % 2) * 64, (g % 2 + 1) * 64), g // 2
                        last = v.tensor_tensor(pooled[rows, n, :], S[rows, n, 16:16 + T], inv[rows, n, :], ALU.mult)
                    chain(last)
                    v.tensor_tensor(pooled, pooled, U[:, :, 16:16 + T], ALU.subtract).then_inc(pool_in, 1)
                    dve.wait_ge(pool_in, s + 1)
                for s in range(2):
                    dve.wait_ge(pool_out, s + 1)
                    for n in range(2):
                        v.tensor_scalar(mixed[:, 6 + n, s * T:(s + 1) * T], ps[:, 4 + 2 * s + n, 0:T],
                                        param("pool_scale", n), None, ALU.mult)
                leave()

            def conformer():
                enter(dve, "conv")
                Z = work[:, 2560:2560 + 2 * (T + 2 * CPAD)].rearrange("p (k t) -> p k t", k=2)
                acc = work[:, 0:512].rearrange("p (k t) -> p k t", k=2)
                chain(v.memset(Z, 0.0))
                dve.wait_ge(conv_a, 1)
                chain(v.tensor_tensor(Z[:, :, CPAD:CPAD + T], proj[:, 18:20, 0:T],
                                      work[:, 2048:2560].rearrange("p (k t) -> p k t", k=2), ALU.mult))
                for i in range(CONV):
                    for k in range(2):
                        w = param("conv_w", k * CONV + i)
                        if i == 0:
                            last = v.tensor_scalar(acc[:, k, :], Z[:, k, 0:T], w, param("conv_b", k), ALU.mult, ALU.add)
                        else:
                            last = v.scalar_tensor_tensor(acc[:, k, :], Z[:, k, i:i + T], w, acc[:, k, :],
                                                          ALU.mult, ALU.add)
                    if i < CONV - 1:
                        chain(last)
                last.then_inc(conv_v, 1)
                dve.wait_ge(conv_p, 1)
                v.tensor_tensor(acc, acc, over(pair[:, 0, 0:T], 2), ALU.subtract).then_inc(conv_v, 1)
                inverse_root(work[:, 1024:1024 + T])
                v.tensor_tensor(acc, acc, over(work[:, 1024:1024 + T], 2), ALU.mult).then_inc(conv_v, 1)
                leave()

            def log1p(dst, e, s, s2):
                chain(v.tensor_scalar(s, e, 2.0, None, ALU.add))
                chain(v.reciprocal(s, s))
                chain(v.tensor_tensor(s, s, e, ALU.mult))
                chain(v.tensor_tensor(s2, s, s, ALU.mult))
                chain(v.tensor_scalar(dst, s2, 1.0 / 17, None, ALU.mult))
                for n in range(15, 2, -2):
                    chain(v.scalar_tensor_tensor(dst, dst, 1.0 / n, s2, ALU.add, ALU.mult))
                chain(v.scalar_tensor_tensor(dst, dst, 1.0, s, ALU.add, ALU.mult))
                chain(v.tensor_scalar(dst, dst, 2.0, None, ALU.mult))

            def gates():
                enter(dve, "gates")

                def row(i):
                    return work[0:MH, i * T:(i + 1) * T]
                ig, fg, nf, e, F, t1, t2, lf, g, mx, fl, one = (row(i) for i in range(12))
                dve.wait_ge(gates_p, 1)
                v.tensor_scalar(ig, pair[0:MH, 0, 0:T], param("i_bias", 0, MH), None, ALU.add)
                v.memset(one, 1.0)
                chain(v.tensor_scalar(fg, pair[0:MH, 1, 0:T], param("f_bias", 0, MH), None, ALU.add))
                chain(v.tensor_scalar(nf, fg, -1.0, None, ALU.mult))
                v.tensor_tensor(nf, nf, fg, ALU.max).then_inc(gates_v, 1)
                dve.wait_ge(gates_a, 1)
                log1p(lf, e, t1, t2)
                chain(v.tensor_scalar(fg, fg, 0.0, None, ALU.min))
                chain(v.tensor_tensor(lf, fg, lf, ALU.subtract))
                chain(v.tensor_tensor_scan(F, one, lf, 0.0, ALU.mult, ALU.add))
                v.tensor_tensor(g, ig, F, ALU.subtract).then_inc(gates_v, 1)
                dve.wait_ge(gates_v, 2)
                chain(v.tensor_tensor_scan(mx, one, g, 0.0, ALU.mult, ALU.max))
                chain(v.tensor_tensor(fl, F, mx, ALU.add))
                chain(v.tensor_scalar(fl, fl, -1.0, None, ALU.mult))
                dve.wait_ge(gates_p, 2)
                v.tensor_copy(cols[:, 0:2 * MH], single[:, 0, 0:2 * MH])
                leave()

            def mlstm():
                enter(dve, "mlstm")

                def weighted(h):
                    dve.wait_ge(m_score, h + 1)
                    dve.wait_ge(m_mask, 2 * h + 2)
                    for c in range(2):
                        w = work[:, (2 * (h % 2) + c) * T:(2 * (h % 2) + c + 1) * T]
                        last = v.scalar_tensor_tensor(w, wide[:, 4 * (h % 2) + c, :], MDH ** -0.5, w,
                                                      ALU.mult, ALU.mult)
                    last.then_inc(m_st, 1)

                def divided(h):
                    dve.wait_ge(m_sum, h + 1)
                    dve.wait_ge(m_weight, 3 * h + 3)
                    floor = work[:, 1024 + (h % 2) * T:1024 + (h % 2 + 1) * T]
                    den = wide[:, 4 * (h % 2) + 3, :]
                    chain(v.tensor_tensor(floor, den, floor, ALU.max))
                    chain(v.scalar_tensor_tensor(floor, den, -1.0, floor, ALU.mult, ALU.max))
                    chain(v.reciprocal(floor, floor))
                    (_, ta), (half, tb) = m_tiles(h, 0)
                    v.tensor_tensor(mixed[:, ta, 0:T], wide[:, 4 * (h % 2) + 2, :], floor, ALU.mult)
                    v.tensor_tensor(mixed[half, tb, 0:T], single[half, h % 2, 0:T], floor[half, :], ALU.mult)\
                        .then_inc(m_head, 1)

                for h in range(MH):
                    weighted(h)
                    if h:
                        divided(h - 1)
                divided(MH - 1)
                leave()

            def mlstm_norm():
                enter(dve, "mlstm_norm")
                for i in range(2):
                    dve.wait_ge(mn_p, i + 1)
                    if i:
                        rstd = work[:, 2048:2048 + MH * T].rearrange("p (h t) -> p h t", h=MH)
                        inverse_root(work[:, 2048:2048 + MH * T])
                    for h in range(MH):
                        for rows, t in m_tiles(h, 0):
                            src = rstd[rows, h, :] if i else wide[rows, h, :]
                            last = v.tensor_tensor(mixed[rows, t, 0:T], mixed[rows, t, 0:T], src,
                                                   ALU.mult if i else ALU.subtract)
                    last.then_inc(mn_v, 1)
                    dve.wait_ge(mn_v, i + 1)
                dve.wait_ge(mn_a, 2)
                for t in range(6):
                    v.scalar_tensor_tensor(mixed[:, t, 0:T], mixed[:, t, 0:T], param("mnorm", t),
                                           proj[:, 18 + t, 0:T], ALU.mult, ALU.mult)
                leave()

            def rglru():
                enter(dve, "rglru")
                W = T + RG_CONV - 1
                xp = work[0:RB, 0:NRB * W].rearrange("p (g t) -> p g t", g=NRB)
                xc, r, i_, a_, th, u = (arena[0:RB, at:at + NRB * T].rearrange("p (g t) -> p g t", g=NRB)
                                        for at in (0, 2048, 12288, 14336, 22528, 24576))
                chain(v.tensor_scalar(cols[0:RB, 8:16], param("r_lam", 0, RB, NRB), -1.0, None, ALU.mult))
                chain(v.tensor_tensor(cols[0:RB, 8:16], cols[0:RB, 8:16], param("r_lam", 0, RB, NRB), ALU.max))
                v.memset(xp[:, :, 0:RG_CONV - 1], 0.0)
                chain(v.tensor_copy(xp[:, :, RG_CONV - 1:W], proj[0:RB, 8:16, 0:T]))
                for j in range(RG_CONV):
                    for g in range(NRB):
                        w = param("rconv_w", g * RG_CONV + j, RB)
                        if j == 0:
                            last = v.tensor_scalar(xc[:, g, :], xp[:, g, 0:T], w, param("rconv_b", g, RB),
                                                   ALU.mult, ALU.add)
                        else:
                            last = v.scalar_tensor_tensor(xc[:, g, :], xp[:, g, j:j + T], w, xc[:, g, :],
                                                          ALU.mult, ALU.add)
                    if j < RG_CONV - 1:
                        chain(last)
                last.then_inc(rg_v, 1)
                dve.wait_ge(rg_v, 1)
                dve.wait_ge(rg_a, 1)
                log1p(cols[0:RB, 48:56], cols[0:RB, 16:24], cols[0:RB, 56:64], cols[0:RB, 64:72])
                chain(v.tensor_scalar(cols[0:RB, 72:80], param("r_lam", 0, RB, NRB), -1.0, 0.0, ALU.mult, ALU.max))
                chain(v.tensor_tensor(cols[0:RB, 48:56], cols[0:RB, 48:56], cols[0:RB, 72:80], ALU.add))
                v.tensor_scalar(cols[0:RB, 24:32], cols[0:RB, 48:56], -RG_C, None, ALU.mult)
                v.tensor_scalar(cols[0:RB, 32:40], cols[0:RB, 48:56], RG_C, None, ALU.mult).then_inc(rg_v, 1)
                dve.wait_ge(rg_a, 2)
                chain(v.tensor_tensor(u, i_, xc, ALU.mult))
                dve.wait_ge(rg_a, 3)
                chain(v.tensor_scalar(i_, th, 1.0, None, ALU.add))
                chain(v.reciprocal(i_, i_))
                chain(v.scalar_tensor_tensor(i_, th, 2.0, i_, ALU.mult, ALU.mult))
                v.tensor_scalar(i_, i_, ROOT_MIN, None, ALU.max).then_inc(rg_v, 1)
                n_root[0] += 1
                dve.wait_ge(rooted, n_root[0])
                chain(v.tensor_tensor(u, u, i_, ALU.mult))
                for g in range(NRB):
                    last = v.tensor_tensor_scan(xc[:, g, :], a_[:, g, :], u[:, g, :], 0.0, ALU.mult, ALU.add)
                chain(last)
                dve.wait_ge(rg_a, 4)
                v.tensor_tensor(mixed[0:RB, 0:NRB, 0:T], xc, proj[0:RB, 0:NRB, 0:T], ALU.mult)
                leave()

            def choose(l):
                enter(dve, f"choose{l}")
                tmp = part(12288, 2 * PH, KEYS)
                sv = part(14336, 2 * PH, TOPK)
                si = part(14592, 2 * PH, TOPK).bitcast(U32)
                sif = part(14848, 2 * PH, TOPK)
                cand = part(15104, PH, TOPK * TOPK)
                tmp2 = part(17152, PH, TOPK * TOPK)
                fv = part(19200, PH, TOPK)
                fi = part(19328, PH, TOPK).bitcast(U32)
                sel = [part(19456, PH, TOPK).bitcast(U32), part(19584, PH, TOPK).bitcast(U32)]
                self_ = [part(19712, PH, TOPK), part(19840, PH, TOPK)]
                eq = part(19968, P, TOPK)
                w = part(22016, PH, TOPK)
                wsum = part(22144, PH)
                picks = part(22528, 3, P)

                def top16(values, indices, at, spare_, n):
                    for i in range(n):
                        last = v.max(values[:, i, 0:8], at(i))
                    chain(last)
                    for i in range(n):
                        v.max_index(indices[:, i, 0:8], values[:, i, 0:8], at(i))
                        last = v.match_replace(spare_[:, i, :], values[:, i, 0:8], at(i), NEG)
                    chain(last)
                    for i in range(n):
                        last = v.max(values[:, i, 8:16], spare_[:, i, :])
                    chain(last)
                    for i in range(n):
                        last = v.max_index(indices[:, i, 8:16], values[:, i, 8:16], spare_[:, i, :])
                    chain(last)

                for t in range(2):
                    dve.wait_ge(k_score, 2 * (l - 2) + t + 1)
                    top16(sv, si, lambda i: ps[:, 4 * t + i // 4, (i % 4) * P:(i % 4 + 1) * P], tmp, 2 * PH)
                    chain(v.tensor_copy(sif, si))
                    for h in range(PH):
                        last = v.tensor_tensor(
                            cand[:, h, :].rearrange("p (a b) -> p a b", a=TOPK),
                            sv[:, 2 * h, :].unsqueeze(2).to_broadcast([P, TOPK, TOPK]),
                            sv[:, 2 * h + 1, :].unsqueeze(1).to_broadcast([P, TOPK, TOPK]), ALU.add)
                    chain(last)
                    top16(fv, fi, lambda h: cand[:, h, :], tmp2, PH)
                    if t:
                        dve.wait_ge(k_turn, 2 * (l - 2) + 1)
                    v.tensor_tensor(w, fv, fv[:, :, 0:1].to_broadcast([P, PH, TOPK]), ALU.subtract)\
                        .then_inc(k_shift, 1)
                    v.tensor_scalar(sel[0], fi, 4, None, ALU.logical_shift_right)
                    chain(v.tensor_scalar(sel[1], fi, TOPK - 1, None, ALU.bitwise_and))
                    for i in range(2):
                        last = v.tensor_copy(self_[i], sel[i])
                    chain(last)
                    iota = const("iota")[:, 0:TOPK].unsqueeze(1).to_broadcast([P, P, TOPK])
                    for i in range(2):
                        place = self_[i].rearrange("p h k -> p (h k)").unsqueeze(2).to_broadcast([P, P, TOPK])
                        chain(v.tensor_tensor(eq, place, iota, ALU.is_equal))
                        for h in range(PH):
                            rows = eq[:, h * TOPK:(h + 1) * TOPK, :]
                            last = v.tensor_tensor(rows, rows, over(sif[:, 2 * h + i, :], TOPK), ALU.mult)
                        chain(last)
                        chain(v.tensor_reduce(picks[:, i, :], eq, AX_X, ALU.add))
                    dve.wait_ge(k_exp, 2 * (l - 2) + t + 1)
                    chain(v.tensor_reduce(wsum, w, AX_X, ALU.add))
                    chain(v.reciprocal(wsum, wsum))
                    v.tensor_tensor(picks[:, 2, :].rearrange("p (h k) -> p h k", h=PH), w,
                                    wsum.unsqueeze(2).to_broadcast([P, PH, TOPK]), ALU.mult).then_inc(k_pick, 1)
                    dve.wait_ge(k_pick, 2 * (l - 2) + t + 1)
                leave()

            def spread(l):
                enter(dve, f"spread{l}")
                base = (l - 2) * (T // 8)

                def one(it):
                    for half in range(2):
                        if not isinstance(it, int) or it + base:
                            dve.wait_ge(g_ready[half], it + base)
                        for u in range(4):
                            n = it * 8 + (half * 4 + u)
                            v.tensor_scalar(hot_i[:, half * 4 + u, :], const("iota"), res[:, 0, bass.ds(n, 1)],
                                            res[:, 2, bass.ds(n, 1)], ALU.is_equal, ALU.mult)
                            last = v.tensor_scalar(hot_j[:, half * 4 + u, :], const("iota"),
                                                   res[:, 1, bass.ds(n, 1)], None, ALU.is_equal)
                        last.then_inc(hot_ready[half], 1)
                one(0)
                with dve.Fori(1, T // 8) as it:
                    one(it)
                leave()

            enter(dve, "lambda")
            v.memset(eps_col[:, 0:1], EPS1)
            v.memset(eps_col[:, 1:2], EPS2)
            dve.wait_ge(loaded, 16 * 6)
            for i in range(2):
                v.tensor_tensor(work[:, i * HD:(i + 1) * HD], param(f"lq{i + 1}", n=HD), param(f"lk{i + 1}", n=HD),
                                ALU.mult).then_inc(chain_v, 1)
            chain.n += 2
            dve.wait_ge(chain_v, chain.n)
            v.tensor_reduce(cols[:, 32:34], work[:, 0:2 * HD].rearrange("p (a b) -> p a b", a=2), AX_X, ALU.add)\
                .then_inc(lam_sum, 1)
            dve.wait_ge(lam_exp, 1)
            chain(v.tensor_tensor(neg_lam[:, :], cols[:, 35:36], cols[:, 34:35], ALU.subtract))
            v.tensor_scalar(neg_lam[:, :], neg_lam[:, :], -LAM_INIT, None, ALU.add)
            leave()

            for l in range(2):
                enter(dve, f"ada{l}")
                dve.wait_ge(ada_done, l + 1)
                chain(v.tensor_tensor(mod[:, l, :, :], pair[:, 0, 0:96].rearrange("p (m j) -> p m j", j=2),
                                      param(f"ada_b{l}", n=48).unsqueeze(2).to_broadcast([P, 48, 2]), ALU.add))
                for q in (1, 4):
                    v.tensor_scalar(mod[:, l, q * KD:(q + 1) * KD, :], mod[:, l, q * KD:(q + 1) * KD, :], 1.0, None,
                                    ALU.add)
                leave()
                enter(dve, f"modulate{l}")
                for s in (CTX, LAT):
                    j = 1 if s == CTX else 0
                    for k in range(KD):
                        v.tensor_scalar(hT[:, k, s * T:(s + 1) * T], x[:, s, k, :], mod[:, l, KD + k, j:j + 1],
                                        mod[:, l, k, j:j + 1], ALU.mult, ALU.add)
                leave()
                project(f"project{l}", PROJECT[l])
                if l == 0:
                    heads_norm("heads_norm", [proj[:, j, :] for j in range(8)], param("q_gain"), 1.0)
                rope(l)
                attend(l)
                if l == 0:
                    pool_windows()
                else:
                    heads_norm("subln", [mixed[:, h, 0:T] for h in range(6)], param("subln"), 1.0 - LAM_INIT)
                    conformer()
                for s in ((CTX, LAT) if l == 0 else (LAT,)):
                    j = 1 if s == CTX else 0
                    enter(dve, f"out{l}{s}")
                    gated_sum(f"out{l}{s}", s, l, 2)
                    leave()
                    norm(f"norm1{l}{s}", s, l, 1, EPS1)
                    enter(dve, f"shift{l}{s}")
                    for k in range(KD):
                        v.tensor_scalar(h2[:, k, :], x[:, s, k, :], mod[:, l, 4 * KD + k, j:j + 1],
                                        mod[:, l, 3 * KD + k, j:j + 1], ALU.mult, ALU.add)
                    leave()
                    enter(dve, f"hidden{l}{s}")
                    hidden(f"hidden{l}{s}", FH, 2, swiglu)
                    gated_sum(f"hidden{l}{s}", s, l, 5)
                    leave()
                    norm(f"norm2{l}{s}", s, l, 2, EPS1)
            for l in (2, 3):
                project(f"project{l}", PROJECT[l])
                if l == 2:
                    gates()
                    mlstm()
                    mlstm_norm()
                else:
                    rglru()
                project(f"memory{l}", PROJECT_MEMORY)
                attend(l)
                enter(dve, f"out{l}{LAT}")
                plain_sum(f"out{l}{LAT}")
                leave()
                norm(f"norm1{l}{LAT}", LAT, l, 1, EPS2)
                project(f"query{l}", PROJECT_QUERY)
                choose(l)
                spread(l)
                enter(dve, f"hidden{l}{LAT}")
                hidden(f"hidden{l}{LAT}", KEYS, 1, weigh)
                plain_sum(f"hidden{l}{LAT}")
                leave()
                norm(f"norm2{l}{LAT}", LAT, l, 2, EPS2)


def constants():
    at, n = const_layout()
    c = np.zeros((P, n), np.float32)

    def put(name, value):
        lo, hi = at[name]
        c[:value.shape[0], lo:hi] = value.reshape(value.shape[0], -1)

    put("ident", np.eye(P))
    put("mean_d", np.full((P, P), 1.0 / D))
    put("mean_64", np.kron(np.eye(2), np.full((HD, HD), 1.0 / HD)))
    put("mean_128", np.full((P, P), 1.0 / P))
    put("mean_192", np.full((P, P), 1.0 / MDH))
    put("mean_192_half", np.kron(np.eye(2), np.ones((HD, 1)))[:, :, None] * np.full(P, 1.0 / MDH))
    put("mean_256", np.full((P, P), 1.0 / 256))
    put("ones", np.ones((P, P)))
    rot = np.zeros((P, P))
    angle_of = np.zeros(P, int)
    for f in range(P):
        axis, half, i = (f % HD) // 32, (f % 32) // 16, f % 16
        rot[f + 16 if half == 0 else f - 16, f] = -1.0 if half == 0 else 1.0
        angle_of[f] = axis * 16 + i
    put("rot", rot)
    pos = np.arange(T)
    freqs = np.float32(10000.0) ** (-np.arange(0, 32, 2, dtype=np.float32) / np.float32(32))
    ang = np.concatenate([(pos // 64).astype(np.float32)[:, None] * freqs,
                          (pos % 64).astype(np.float32)[:, None] * freqs], axis=1)
    put("cos", np.cos(ang)[:, angle_of].T)
    put("sin", np.sin(ang)[:, angle_of].T)
    inv = np.zeros((P, 2, T))
    for g, w in enumerate(WINDOWS):
        lo, hi = np.clip(pos - w // 2, 0, T), np.clip(pos + (w - 1 - w // 2) + 1, 0, T)
        inv[(g % 2) * 64:(g % 2 + 1) * 64, g // 2] = 1.0 / (hi - lo)
    put("inv_count", inv)
    put("iota", np.tile(np.arange(P), (P, 1)))
    rows = np.zeros((MH, MH, P))
    for h in range(MH):
        rows[h, h] = 1.0
    put("head_rows", rows)
    return c


def columns(v, width=P):
    v = v.reshape(-1, width).T
    return np.concatenate([v, np.zeros((P - width, v.shape[1]), v.dtype)]) if width < P else v


def by_column(w, width=P):
    k, f = w.shape
    return w.reshape(k // P, P, f // width, width).transpose(2, 1, 0, 3).reshape(f // width, P, -1)


def by_row(w, rows=P):
    return w.reshape(-1, rows, w.shape[1])


def turned(x):
    return x.T.reshape(-1, P, x.shape[0]).transpose(1, 0, 2)


def mlstm_order():
    a_ = [np.arange(h * MDH, h * MDH + P) for h in range(MH)]
    return np.concatenate(a_ + [np.arange(h * MDH + P, (h + 1) * MDH) for h in range(MH)])


def lay_out(i):
    a = {}
    a["consts"] = constants()
    at, n = param_layout()
    prm = np.zeros((P, n), np.float32)

    def put(name, value):
        lo, hi = at[name]
        prm[:value.shape[0], lo:hi] = value

    for l in range(2):
        put(f"ada_b{l}", columns(i["ada_b"][l]))
        for k in "12":
            put(f"ln{l}g{k}", columns(i[f"ln{k}_g"][l]))
            put(f"ln{l}b{k}", columns(i[f"ln{k}_b"][l]))
            put(f"ln{l + 2}g{k}", columns(i[f"ln{k}_g_2"][l]))
            put(f"ln{l + 2}b{k}", columns(i[f"ln{k}_b_2"][l]))
    put("q_gain", np.tile(i["ab_q_gain"][0], 2)[:, None])
    put("k_gain", np.tile(i["ab_k_gain"][0], 2)[:, None])
    put("pool_scale", columns(i["ab_pool_scale"][0]))
    pool_w = np.zeros((P, 2, P), np.float32)
    for g in range(4):
        lo = (g % 2) * 64
        pool_w[lo:lo + 64, g // 2, lo:lo + 64] = i["ab_w_pool"][0, g]
    put("pool_w", pool_w.reshape(P, -1))
    put("subln", columns(i["cd_subln_gain"][0]))
    put("conv_w", i["cd_conv_w"][0].reshape(CONV, 2, P).transpose(2, 1, 0).reshape(P, -1))
    put("conv_b", columns(i["cd_conv_b"][0]))
    put("conv_g", columns(i["cd_conv_ln_g"][0]))
    put("conv_bb", columns(i["cd_conv_ln_b"][0]))
    for name, src in (("lq1", "cd_lambda_q1"), ("lk1", "cd_lambda_k1"), ("lq2", "cd_lambda_q2"), ("lk2", "cd_lambda_k2")):
        put(name, np.broadcast_to(i[src][0], (P, HD)))
    order = mlstm_order()
    put("mnorm", columns(i["mlstm_norm_g_2"][0][order]))
    bg = i["mlstm_b_gates_2"][0]
    put("i_bias", bg[:MH, None])
    put("f_bias", bg[MH:, None])
    put("rconv_w", columns(i["rglru_conv_w_2"][0].reshape(-1), RB).reshape(P, RG_CONV, NRB).transpose(0, 2, 1).reshape(P, -1))
    for name, src in (("rconv_b", "rglru_conv_b_2"), ("r_ba", "rglru_b_a_2"), ("r_bx", "rglru_b_x_2"), ("r_lam", "rglru_lam_2")):
        put(name, columns(i[src][0], RB))
    a["params"] = prm
    a["x"] = turned(i["x"][0])
    a["ctx"] = turned(i["ctx"][0])
    a["mem"] = turned(i["mem_2"][0])
    a["cond"] = turned(np.stack([i["c"][0], i["c_ctx"]]))

    for l in range(2):
        a[f"ada{l}"] = by_column(i["ada_w"][l])
        w = i["ffn_w_in"][l]
        a[f"ffn{l}_in"] = w.reshape(KD, P, 2, FH, P).transpose(3, 2, 1, 0, 4).reshape(2 * FH, P, D)
        a[f"ffn{l}_out"] = by_row(i["ffn_w_out"][l])
        a[f"kv{l}"] = by_column(i["xattn_w_kv_2"][l])
        a[f"pq{l}"] = by_column(i["peer_w_q_2"][l])
        a[f"subk{l}"] = i["peer_subkeys_2"][l].transpose(2, 0, 1)
        u = i["peer_u_2"][l].reshape(KEYS, KEYS, KD, P)
        a[f"peer{l}_u"] = u.transpose(1, 3, 2, 0).reshape(KEYS, P, D)
        a[f"peer{l}_v"] = i["peer_v_2"][l].reshape(KEYS, KEYS, D).transpose(1, 0, 2)
    heads = np.concatenate([np.arange(h * HD, (h + 1) * HD) for h in Q_ORDER])
    w = i["ab_w_in"][0]
    a["ab_in"] = by_column(np.concatenate([w[:, heads], w[:, 768:]], axis=1))
    w = i["ab_w_out"][0]
    a["ab_out"] = by_row(np.concatenate([w[heads], w[768:]]))
    a["cd_in"] = by_column(i["cd_w_in"][0])
    a["cd_out"] = by_row(i["cd_w_out"][0])
    w = i["mlstm_w_in_2"][0]
    W = MH * MDH
    a["ml_in"] = by_column(np.concatenate([w[:, s * W + order] for s in range(4)] + [w[:, 4 * W + 2 * MH:]], axis=1))
    a["gate_w"] = w[:, 4 * W:4 * W + 2 * MH].reshape(KD, P, 2 * MH).transpose(1, 0, 2)
    w = i["w_out_2"][0]
    a["ml_out"] = by_row(np.concatenate([w[order], w[W:]]))
    w = i["rglru_w_in_2"][0]
    a["rg_in_r"] = by_column(w[:, :2 * NRB * RB], RB)
    a["rg_in_q"] = by_column(w[:, 2 * NRB * RB:])
    a["rg_w"] = np.concatenate([i["rglru_w_a_2"][0], i["rglru_w_x_2"][0]]).transpose(1, 0, 2).reshape(RB, -1)
    w = i["w_out_2"][1]
    a["rg_out_q"] = by_row(w[NRB * RB:])
    a["rg_out_r"] = by_row(w[:NRB * RB], RB)
    return {k: np.ascontiguousarray(v) for k, v in a.items()}


def kernel(**inputs):
    import concourse.bacc as bacc
    from concourse.bass_utils import run_bass_kernel_spmd

    nc = bacc.Bacc("TRN2", target_bir_lowering=False, num_devices=1)
    arrays = {f"in_{k}": v for k, v in lay_out({k: np.asarray(v) for k, v in inputs.items()}).items()}
    aps = {k[3:]: nc.dram_tensor(k, v.shape, F32, kind="ExternalInput").ap() for k, v in arrays.items()}
    out = nc.dram_tensor("out", (P, KD, T), F32, kind="ExternalOutput").ap()
    program(nc, aps, out)
    got = run_bass_kernel_spmd(nc, [arrays], core_ids=[0]).results[0]["out"]
    return np.ascontiguousarray(got.transpose(1, 0, 2).reshape(D, T).T)[None]
```

```python
import math
from contextlib import ExitStack

import numpy as np

import concourse.bass as bass
from concourse import mybir

ALU = mybir.AluOpType
ACT = mybir.ActivationFunctionType
F32 = mybir.dt.float32
F32R = mybir.dt.float32r
BF16 = mybir.dt.bfloat16
U32 = mybir.dt.uint32
AX_X = mybir.AxisListType.X

P = 128
D = 1024
T = 256
KD = D // P
DEPTH = 2
HD = 64
FFN = 2816
FH = FFN // P
ALPHA = (2.0 * DEPTH) ** 0.25
LAM_INIT = 0.8 - 0.6 * math.exp(-0.3)
EPS1 = 1e-6
EPS2 = 1e-5
WINDOWS = (2, 4, 8, 16)
CONV = 31
CPAD = CONV // 2
RG_CONV = 4
RB = 96
NRB = 8
RG_C = 8.0
MH = 4
MDH = 192
PH = 8
KEYS = 128
TOPK = 16
NEG = -3.0e38
ROOT_MIN = 2.0 ** -115
R = 6
SPLIT = 3
PHASES = 3
CTX, LAT = 0, 1

Q_ORDER = [0, 3, 1, 4, 2, 5, 6, 9, 7, 10, 8, 11]


def const_layout():
    at, off = {}, 0
    for name, n in (("ident", P), ("mean_d", P), ("mean_64", P), ("mean_128", P), ("mean_192", P), ("mean_192_half", 2 * P), ("mean_256", P),
                    ("ones", P), ("rot", P), ("cos", T), ("sin", T), ("inv_count", 2 * T), ("iota", P),
                    ("head_rows", MH * P)):
        at[name] = (off, off + n)
        off += n
    return at, off


def param_layout():
    at, off = {}, 0
    names = [("ada_b0", 48), ("ada_b1", 48), ("q_gain", 1), ("k_gain", 1), ("pool_scale", 2), ("pool_w", 2 * P), ("subln", 1),
             ("conv_w", 2 * CONV), ("conv_b", 2), ("conv_g", 2), ("conv_bb", 2), ("lq1", HD), ("lk1", HD),
             ("lq2", HD), ("lk2", HD), ("mnorm", 6), ("i_bias", 1), ("f_bias", 1),
             ("rconv_w", NRB * RG_CONV), ("rconv_b", NRB), ("r_ba", NRB), ("r_bx", NRB), ("r_lam", NRB)]
    for n in range(4):
        names += [(f"ln{n}{k}", KD) for k in ("g1", "b1", "g2", "b2")]
    for name, n in names:
        at[name] = (off, off + n)
        off += n
    return at, off


def stage_list():
    s = [("lambda", "va")]
    for l in range(2):
        s += [(f"ada{l}", "pav" if l == 0 else "pv"), (f"modulate{l}", "v"), (f"project{l}", "pav")]
        s += [("heads_norm", "pav")] if l == 0 else []
        s += [(f"rope{l}", "pv"), (f"attend{l}", "pav")]
        s += [("pool", "pv")] if l == 0 else [("subln", "pav"), ("conv", "pav")]
        for n in ((CTX, LAT) if l == 0 else (LAT,)):
            s += [(f"out{l}{n}", "pv"), (f"norm1{l}{n}", "pav"), (f"shift{l}{n}", "v"), (f"hidden{l}{n}", "pav"),
                  (f"norm2{l}{n}", "pav")]
    for l in (2, 3):
        s += [(f"project{l}", "pav")]
        s += [("gates", "pav"), ("mlstm", "pavg"), ("mlstm_norm", "pav")] if l == 2 else [("rglru", "pav")]
        s += [(f"memory{l}", "pav"), (f"attend{l}", "pav"), (f"out{l}{LAT}", "pv"), (f"norm1{l}{LAT}", "pav"),
              (f"query{l}", "pav"), (f"choose{l}", "pav"), (f"split{l}", "v"), (f"spread{l}a", "pav"),
              (f"hidden{l}a", "pav"), (f"spread{l}b", "pav"), (f"hidden{l}b", "pav"), (f"norm2{l}{LAT}", "pav")]
    return s


STAGES = stage_list()


def stages_of(engine, before):
    n = 0
    for name, engines in STAGES:
        if name == before:
            return n
        n += engine in engines
    raise KeyError(before)


FEATURES, TOKENS = "features", "tokens"
PROJECT = {
    0: [(0, 8, 0, 2 * T, FEATURES, P), (8, 2, 0, 2 * T, TOKENS, P), (10, 2, 0, 2 * T, FEATURES, P)],
    1: [(0, 6, T, T, FEATURES, P), (6, 6, 0, 2 * T, FEATURES, P), (12, 6, 0, 2 * T, TOKENS, P),
        (18, 4, T, T, FEATURES, P)],
    2: [(0, 12, 0, T, FEATURES, P), (12, 6, 0, T, TOKENS, P), (18, 8, 0, T, FEATURES, P)],
    3: [(0, 16, 0, T, FEATURES, RB), (24, 2, 0, T, FEATURES, P)],
}
PROJECT_MEMORY = [(0, 2, 0, T, FEATURES, P), (2, 2, 0, T, TOKENS, P)]
PROJECT_QUERY = [(0, 16, 0, T, FEATURES, P)]
ROPE = {0: [(j, T) for j in range(8)], 1: [(j, 0) for j in range(6)] + [(j, T) for j in range(6, 12)]}

HIDDEN = {"ffn": (FH, 2), "peer": (KEYS // 2, 1)}
WEIGHTS = [("ada0", "ada0", 48), ("project0", "ab_in", 12),
           ("out00", "ab_out", 8), ("hidden00", "ffn0", 0), ("out01", "ab_out", 8), ("hidden01", "ffn0", 0),
           ("ada1", "ada1", 48), ("project1", "cd_in", 22), ("out11", "cd_out", 8), ("hidden11", "ffn1", 0),
           ("project2", "ml_in", 26), ("memory2", "kv0", 4), ("out21", "ml_out", 8), ("query2", "pq0", 16),
           ("hidden2a", "peer0a", 0), ("hidden2b", "peer0b", 0),
           ("project3", "rg_in_r", 16), ("project3", "rg_in_q", 2), ("memory3", "kv1", 4),
           ("out31", "rg_out_q", 2), ("out31", "rg_out_r", NRB), ("query3", "pq1", 16),
           ("hidden3a", "peer1a", 0), ("hidden3b", "peer1b", 0)]


def blocks_of(tensor, n):
    if n:
        return n
    tiles, unit = HIDDEN[tensor.rstrip("01ab")]
    return tiles * (unit + 1)


def first_block(stage):
    total = 0
    for name, tensor, n in WEIGHTS:
        if name == stage:
            return total
        total += blocks_of(tensor, n)
    raise KeyError(stage)


def blocks_in(stage):
    return sum(blocks_of(tensor, n) for name, tensor, n in WEIGHTS if name == stage)


def after_input(stage, t, unit):
    if isinstance(t, int) and t < 2:
        return first_block(stage) + (t + 1) * unit
    return t * (unit + 1) + (first_block(stage) + unit - 2)


def after_output(stage, t, unit):
    return t * (unit + 1) + (first_block(stage) + 3 * unit + 1)


def split_before(stage):
    total = 0
    for name, tensor, n in WEIGHTS:
        if name == stage:
            return total
        total += 0 if n else blocks_of(tensor, n)
    raise KeyError(stage)


class Chain:

    def __init__(self, eng, sem):
        self.eng, self.sem, self.n = eng, sem, 0

    def __call__(self, ins):
        self.n += 1
        ins.then_inc(self.sem, 1)
        self.eng.wait_ge(self.sem, self.n)


class RingPlace:

    def __init__(self):
        self.at = 0

    def steps(self, eng, n, unit, step, phases=2):
        per = math.lcm(R // math.gcd(R, unit), phases)
        if self.at == 0 and n > per:
            self.steps(eng, per, unit, step, phases)
            self.steps(eng, n - per, unit, lambda i, par, b: step(i + per, par, b), phases)
            return
        turns = n // per
        if turns < 2:
            turns = 0
        base = self.at

        def blocks(k, it):
            out = []
            for b in range(unit):
                s = base + k * unit + b
                out.append((s % R, s // R + it * (per * unit // R), s + it * (per * unit), s % SPLIT))
            return out

        if turns:
            with eng.Fori(0, turns) as it:
                for k in range(per):
                    step(it * per + k, k % phases, blocks(k, it))
        for i in range(turns * per, n):
            step(i, i % phases, blocks(i, 0))
        self.at += n * unit


def program(nc, a, out):
    ctx = ExitStack()
    with ctx:
        def sb(name, shape, dt=F32):
            return ctx.enter_context(nc.sbuf_tensor(name, shape, dt))

        def sem(name):
            return ctx.enter_context(nc.semaphore(name))

        C_AT, C_N = const_layout()
        Q_AT, Q_N = param_layout()
        ring = sb("ring", [P, R, D])
        consts = sb("consts", [P, C_N])
        params = sb("params", [P, Q_N])
        x = sb("x", [P, 2, KD, T])
        res = sb("res", [P, KD, T])
        mod = sb("mod", [P, 2, 48, 2])
        cond = sb("cond", [P, 2, KD, 2])
        gate_w = sb("gate_w", [P, KD, 2 * MH])
        subk = sb("subk", [P, 2, KEYS])
        cols = sb("cols", [P, 128])
        neg_lam = sb("neg_lam", [P, 1])
        eps_col = sb("eps_col", [P, 2])
        arena = sb("arena", [P, 24064])
        w_split = sb("w_split", [P, SPLIT, 2, D], F32R)
        x_split = sb("x_split", [P, 2, KD, T], F32R)
        h_split = sb("h_split", [P, PHASES, 2, T], F32R)
        ps = ctx.enter_context(nc.psum_tensor("ps", [P, 8, 512], F32))
        wide = ps[:, 0:4, :].rearrange("p b (c n) -> p (b c) n", c=2)
        pair = ps[:, 4:6, :]
        single = ps[:, 6:8, :]

        def const(name, rows=P, lo_row=0):
            lo, hi = C_AT[name]
            return consts[lo_row:lo_row + rows, lo:hi]

        def param(name, i=0, rows=P, n=1):
            lo = Q_AT[name][0] + i
            return params[0:rows, lo:lo + n]

        def part(off, *dims):
            v = arena[:, off:off + int(np.prod(dims))]
            if len(dims) == 2:
                v = v.rearrange("p (a b) -> p a b", a=dims[0])
            elif len(dims) == 3:
                v = v.rearrange("p (a b c) -> p a b c", a=dims[0], b=dims[1])
            return v

        def over(v, n):
            return v.unsqueeze(1).to_broadcast([v.shape[0], n, v.shape[1]])

        PROJ, MIXED, WORK = 0, 13312, 18432
        proj = part(PROJ, 26, 512)
        mixed = part(MIXED, 10, 512)
        hT = part(MIXED, KD, 2 * T)
        work = part(WORK, 5632)
        probs = part(WORK, 2, 2, 512)
        probsT = part(WORK + 2048, 2, 1024)
        diag = part(WORK + 4096, 4, P)
        h2 = part(0, KD, T)
        gate = part(2048, PHASES, T)
        hid = part(2048 + PHASES * T, PHASES, T)
        HALF = KEYS // 2
        G = part(0, T, HALF)
        chosen = res[:, 0:3, :]
        spare = x[:, CTX, :, :]
        small = part(WORK, 5632).bitcast(BF16)
        GROUP = 512 // HALF
        hot_i = small[:, 0:2 * GROUP * KEYS].rearrange("p (b n t) -> p b n t", b=2, t=GROUP)
        at = 2 * GROUP * KEYS
        hot_j = small[:, at:at + 2 * GROUP * HALF].rearrange("p (b n t) -> p b n t", b=2, t=GROUP)
        at += 2 * GROUP * HALF
        hot_w = small[:, at:at + 6 * GROUP * HALF].rearrange("p (b c n t) -> p b c n t", b=2, t=GROUP, c=3)
        at += 6 * GROUP * HALF
        keys = small[:, at:at + 2 * T].rearrange("p (i t) -> p i t", i=2)
        at += 2 * T
        weight3 = small[:, at:at + 3 * T].rearrange("p (c t) -> p c t", c=3)
        at += 3 * T
        places = small[:, at:at + GROUP * KEYS].rearrange("p (n t) -> p n t", t=GROUP)
        gelu = spare[:, 0:PHASES, :]
        coef = spare[:, PHASES:2 * PHASES, :]

        stage = {e: sem(f"{n}_stages") for e, n in (("p", "tensor"), ("a", "scalar"), ("v", "vector"), ("g", "gpsimd"))}
        loaded = sem("loaded")
        filled = [sem(f"slot{i}_filled") for i in range(R)]
        block_used = sem("block_used")
        mem_loaded, subk_loaded, rg_loaded = sem("mem_loaded"), sem("subkeys_loaded"), sem("rg_loaded")
        tile_out = [sem("even_tile_out"), sem("odd_tile_out")]
        chain_a, chain_v = sem("scalar_chain"), sem("vector_chain")
        silu_done, ada_out = sem("silu_done"), sem("ada_out")
        squared, mean_ready, normed, turned_pos, roped = (sem(n) for n in (
            "squared", "mean_ready", "normed", "partner_ready", "roped"))
        s_ready, m_ready, e_ready, d_ready, t_ready, pt_ready, o_ready, o_out = (sem(n) for n in (
            "scores_ready", "max_ready", "exp_ready", "diag_ready", "turned", "turned_out", "heads_ready", "heads_out"))
        ln_mean, ln_centred, ln_squared, ln_var = (sem(n) for n in ("ln_mean", "ln_centred", "ln_squared", "ln_var"))
        w_high, w_low = sem("weights_high"), sem("weights_low")
        gate_ready, hid_made, hid_high, hid_ready = (sem(n) for n in ("gate_ready", "hid_made", "hid_high", "hid_ready"))
        lam_sum, lam_exp = sem("lam_sum"), sem("lam_exp")
        pool_in, pool_out = sem("pooled"), sem("pool_mixed")
        conv_v, conv_a, conv_p = sem("conv_v"), sem("conv_a"), sem("conv_p")
        gates_p, gates_a, gates_v = sem("gates_p"), sem("gates_a"), sem("gates_v")
        m_cast, m_weight, m_mask, m_score, m_st, m_sum, m_head = (sem(n) for n in (
            "m_broadcast", "m_weights", "m_masked", "m_scores", "m_weighted", "m_summed", "m_divided"))
        mn_v, mn_p, mn_a = sem("mnorm_v"), sem("mnorm_p"), sem("mnorm_a")
        rg_v, rg_a, rg_p = sem("rglru_v"), sem("rglru_a"), sem("rglru_p")
        k_score, k_shift, k_exp, k_pick, k_turn, k_keep = (sem(n) for n in (
            "keys_scored", "picks_shifted", "picks_exp", "picks_ready", "picks_turned", "picks_kept"))
        hot_ready = [sem("hot_ready0"), sem("hot_ready1")]
        hot_j_made = sem("hot_j_made")
        ada_rows, ada_turned = sem("ada_rows"), sem("ada_turned")
        g_ready = [sem("g_ready0"), sem("g_ready1")]
        g_kept = [sem("g_kept0"), sem("g_kept1")]
        rooted = sem("rooted")
        stored = sem("stored")

        def enter(eng, name):
            for e in "pavg":
                n = stages_of(e, name)
                if n:
                    eng.wait_ge(stage[e], n)

        def units_of(l):
            units = []
            if l == 0:
                for s in (CTX, LAT):
                    for n, head in enumerate(Q_ORDER):
                        j, half, kv = n // 2, n % 2, head // 3
                        assert half == kv % 2
                        rows = slice(half * HD, (half + 1) * HD)
                        units.append(dict(
                            nk=T if s == CTX else 2 * T, diff=False, rows=(half * HD, HD),
                            q=[proj[rows, j, s * T + r * P:s * T + (r + 1) * P] for r in range(2)],
                            k=[proj[rows, 6 + kv // 2, 0:T if s == CTX else 2 * T]] * 2,
                            v=lambda c, kv=kv: proj[:, 8 + kv // 2, c * P + (kv % 2) * HD:c * P + (kv % 2 + 1) * HD],
                            out=mixed[rows, j, s * T:(s + 1) * T]))
            elif l == 1:
                for h in range(6):
                    for t in range(2):
                        units.append(dict(
                            nk=2 * T, diff=True, rows=(0, P),
                            q=[proj[r * HD:(r + 1) * HD, h, t * P:(t + 1) * P] for r in range(2)],
                            k=[proj[r * HD:(r + 1) * HD, 6 + h, :] for r in range(2)],
                            v=lambda c, h=h: proj[:, 12 + h, c * P:(c + 1) * P],
                            out=mixed[:, h, t * P:(t + 1) * P]))
            else:
                for h in range(4):
                    j, half = h // 2, h % 2
                    rows = slice(half * HD, (half + 1) * HD)
                    units.append(dict(
                        nk=T, diff=False, rows=(half * HD, HD),
                        q=[proj[rows, 24 + j, r * P:(r + 1) * P] for r in range(2)],
                        k=[proj[rows, j, 0:T]] * 2,
                        v=lambda c, j=j, half=half: proj[:, 2 + j, c * P + half * HD:c * P + (half + 1) * HD],
                        out=mixed[rows, (6 if l == 2 else 8) + j, 0:T]))
            return units

        def scores_at(i, nk):
            return ps[:, 2 * (i % 2):2 * (i % 2) + 2, 0:nk]

        def m_tiles(h, first):
            half = slice((h % 2) * HD, (h % 2 + 1) * HD)
            return [(slice(0, P), first + h), (half, first + 4 + h // 2)]

        def rg_tiles():
            return [proj[0:RB, 0:8, T:2 * T], proj[0:RB, 8:16, T:2 * T], proj[0:RB, 16:24, 0:T],
                    proj[0:RB, 16:24, T:2 * T], mixed[0:RB, 0:8, T:2 * T]]

        block = ctx.enter_context(nc.Block())

        @block.sync
        def _(sp):
            for dst, src in ((cond[:, 0, :, :], a["cond"]), (x[:, CTX, :, :], a["ctx"]), (x[:, LAT, :, :], a["x"]),
                             (params[:, :], a["params"]), (consts[:, :], a["consts"]), (gate_w[:, :, :], a["gate_w"])):
                sp.dma_start(dst, src).then_inc(loaded, 16)
            place = RingPlace()

            def fetch(t, i, blk):
                slot, _, seq, _ = blk
                src = t[i, :, :] if isinstance(i, int) else t[bass.ds(i, 1), :, :].rearrange("o p n -> (o p) n")
                if not isinstance(seq, int) or seq >= R:
                    sp.wait_ge(block_used, seq - (R - 1))
                sp.dma_start(ring[0:t.shape[1], slot, 0:t.shape[2]], src).then_inc(filled[slot], 16)

            def stream(t, n):
                place.steps(sp, n, 1, lambda i, par, b: fetch(t, i, b[0]))

            def stream_hidden(w_in, w_out, t0, n, unit):
                def one(i, par, b):
                    for j in range(unit):
                        fetch(w_in, (i + (2 + t0)) * unit + j, b[j])
                    fetch(w_out, i + t0, b[unit])
                place.steps(sp, 2 * unit, 1, lambda i, par, b: fetch(w_in, i + t0 * unit, b[0]))
                place.steps(sp, n - 2, unit + 1, one)
                place.steps(sp, 2, 1, lambda i, par, b: fetch(w_out, i + (t0 + n - 2), b[0]))

            for _, name, n in WEIGHTS:
                if n:
                    stream(a[name], n)
                elif name.startswith("ffn"):
                    stream_hidden(a[name + "_in"], a[name + "_out"], 0, FH, 2)
                else:
                    stream_hidden(a[name[:-1] + "_u"], a[name[:-1] + "_v"], HALF * (name[-1] == "b"), HALF, 1)

        @block.gpsimd
        def _(pool):
            enter(pool, "mlstm")
            for h in range(MH):
                for c in range(2):
                    pool.wait_ge(m_weight, 3 * h + c + 1)
                    w = work[:, (2 * (h % 2) + c) * T:(2 * (h % 2) + c + 1) * T]
                    nc.gpsimd.affine_select(out=w, in_=w, compare_op=ALU.is_ge, fill=0.0, base=-P * c,
                                            pattern=[[1, T]], channel_multiplier=-1).then_inc(m_mask, 1)
            pool.drain().then_inc(stage["g"], 1)
            for l in (2, 3):
                if l == 3:
                    enter(pool, "project3")
                    pool.dma_start(work[0:RB, 2560:2560 + 2 * NRB * RB], a["rg_w"]).then_inc(rg_loaded, 16)
                enter(pool, f"memory{l}")
                pool.dma_start(res[:, :, :], a["mem"]).then_inc(mem_loaded, 16)
                pool.dma_start(subk[:, :, :], a[f"subk{l - 2}"]).then_inc(subk_loaded, 16)
            for e in "pav":
                pool.wait_ge(stage[e], stages_of(e, f"norm23{LAT}") + 1)
            pool.dma_start(out, x[:, LAT, :, :]).then_inc(stored, 16)
            pool.wait_ge(stored, 16)

        @block.tensor
        def _(pe):
            place = RingPlace()
            n_tiles, n_out = [0], [0, 0]
            n_unit, n_ln, n_hid, n_mean = [0], [0], [0], [0]
            mm = nc.tensor.matmul

            def leave():
                pe.drain().then_inc(stage["p"], 1)

            def wait_filled(blk):
                slot, turn, _, _ = blk
                pe.wait_ge(filled[slot], (turn + 1) * 16)

            def ada(l):
                enter(pe, f"ada{l}")
                pe.wait_ge(loaded, 16 * 6)
                pe.wait_ge(silu_done, 1)

                def turn(n):
                    pe.wait_ge(ada_rows, 6 * l + n + 1)
                    if n >= 2:
                        pe.wait_ge(ada_out, 6 * l + n - 1)
                    for m in range(KD):
                        last = mm(pair[:, n % 2, 2 * m:2 * m + 2],
                                  work[0:2, (n % 2) * D + m * P:(n % 2) * D + (m + 1) * P], const("ident", 2)[:, 0:2],
                                  start=True, stop=True)
                    last.then_inc(ada_turned, 1)

                def one(n, par, b):
                    for k in range(KD):
                        wait_filled(b[k])
                        for c in range(2):
                            last = mm(ps[0:2, 2 * par + c, :], cond[:, 1, k, :],
                                      ring[:, b[k][0], c * 512:(c + 1) * 512], start=(k == 0), stop=(k == KD - 1))
                        last.then_inc(block_used, 1)
                    if n:
                        turn(n - 1)
                place.steps(pe, 6, KD, one)
                turn(5)
                leave()

            def project(src, runs):
                for _, n, t0, nt, form, width in runs:
                    def one(m, par, b):
                        wait_filled(b[0])
                        if isinstance(m, int):
                            if n_out[par] + m // 2:
                                pe.wait_ge(tile_out[par], n_out[par] + m // 2)
                        else:
                            pe.wait_ge(tile_out[par], m // 2 + n_out[par])
                        w = ring[:, b[0][0], 0:KD * width].rearrange("p (k c) -> p k c", k=KD)
                        if form == FEATURES:
                            for k in range(KD):
                                last = mm(pair[0:width, par, 0:nt], w[:, k, :], src[:, k, t0:t0 + nt],
                                          start=(k == 0), stop=(k == KD - 1))
                        else:
                            for t in range(nt // P):
                                for k in range(KD):
                                    last = mm(pair[:, par, t * P:(t + 1) * P],
                                              src[:, k, t0 + t * P:t0 + (t + 1) * P], w[:, k, :],
                                              start=(k == 0), stop=(k == KD - 1))
                        last.then_inc(block_used, 1)

                    place.steps(pe, n, 1, one)
                    n_tiles[0] += n
                    n_out[0] += (n + 1) // 2
                    n_out[1] += n // 2
                leave()

            def means(name, ones, n, tiles):
                enter(pe, name)
                for i in range(tiles):
                    pe.wait_ge(squared, n_mean[0] + i + 1)
                    if n_mean[0] + i >= 2:
                        pe.wait_ge(normed, n_mean[0] + i - 1)
                    mm(pair[:, i % 2, 0:n], const(ones), work[:, (i % 2) * 512:(i % 2) * 512 + n],
                       start=True, stop=True).then_inc(mean_ready, 1)
                n_mean[0] += tiles
                leave()

            def rope(l):
                enter(pe, f"rope{l}")
                base = len(ROPE[0]) if l else 0
                for i, (j, lat) in enumerate(ROPE[l]):
                    if base + i >= 2:
                        pe.wait_ge(roped, base + i - 1)
                    mm(pair[:, i % 2, 0:T], const("rot"), proj[:, j, lat:lat + T],
                       start=True, stop=True).then_inc(turned_pos, 1)
                leave()

            def attend(l):
                units = units_of(l)
                enter(pe, f"attend{l}")
                base = n_unit[0]

                def scores(i):
                    u = units[i]
                    if base + i >= 2:
                        pe.wait_ge(e_ready, base + i - 1)
                    for r in range(2):
                        last = mm(scores_at(i, u["nk"])[:, r, :], u["q"][r], u["k"][r], start=True, stop=True)
                    last.then_inc(s_ready, 1)

                def turn(i):
                    u = units[i]
                    pe.wait_ge(d_ready, base + i + 1)
                    if base + i:
                        pe.wait_ge(pt_ready, base + i)
                    for c in range(u["nk"] // P):
                        for r in range(2):
                            e = probs[:, i % 2, r, c * P:(c + 1) * P]
                            dg = diag[:, 2 * (i % 2) + r, :]
                            if u["diff"]:
                                last = mm(pair[:, 0, c * P:(c + 1) * P], e, dg, start=(r == 0), stop=(r == 1))
                            else:
                                at = (c % 2) * T + r * P
                                last = mm(pair[:, c // 2, at:at + P], e, dg, start=True, stop=True)
                    last.then_inc(t_ready, 1)

                def heads(i):
                    u = units[i]
                    pe.wait_ge(pt_ready, base + i + 1)
                    if base + i >= 2:
                        pe.wait_ge(o_out, base + i - 1)
                    nq = P if u["diff"] else 2 * P
                    lo, m = u["rows"]
                    chunks = u["nk"] // P
                    for c in range(chunks):
                        last = mm(single[lo:lo + m, i % 2, 0:nq], u["v"](c), probsT[:, i % 2, c * nq:(c + 1) * nq],
                                  start=(c == 0), stop=(c == chunks - 1))
                    last.then_inc(o_ready, 1)

                n = len(units)
                scores(0)
                for i in range(n):
                    if i + 1 < n:
                        scores(i + 1)
                    if i:
                        heads(i - 1)
                    turn(i)
                heads(n - 1)
                n_unit[0] += n
                leave()

            def accumulate(rhs, blk, rows, first, final):
                for m in range(KD):
                    last = mm(wide[:, m, :], ring[0:rows, blk[0], m * P:(m + 1) * P], rhs,
                              start=(first and m % 2 == 0), stop=final, skip_group_check=True)
                return last

            def passes(dst, w, at, rhs, first, final, shared=False):
                for i, (wp, rp) in enumerate(((0, 0), (0, 1), (1, 0))):
                    last = mm(dst, w_split[:, w, wp, at:at + P], rhs[rp], start=(first and i == 0),
                              stop=(final and i == 2), skip_group_check=shared)
                return last

            def out_project(name, tiles):
                enter(pe, name)

                def one(i, par, b):
                    rhs, rows = tiles[i]
                    wait_filled(b[0])
                    last = accumulate(rhs, b[0], rows, i == 0, i == len(tiles) - 1)
                    last.then_inc(block_used, 1)
                for i in range(len(tiles)):
                    place.steps(pe, 1, 1, lambda _, par, b: one(i, par, b))
                leave()

            def norm(name):
                enter(pe, name)
                for k in range(KD):
                    last = mm(pair[:, 0, 0:T], const("mean_d"), res[:, k, :], start=(k == 0), stop=(k == KD - 1))
                last.then_inc(ln_mean, 1)
                pe.wait_ge(ln_squared, n_ln[0] + 1)
                for k in range(KD):
                    last = mm(pair[:, 1, 0:T], const("mean_d"), work[:, k * T:(k + 1) * T],
                              start=(k == 0), stop=(k == KD - 1))
                last.then_inc(ln_var, 1)
                n_ln[0] += 1
                leave()

            def hidden(name, n, unit, opens=True):
                enter(pe, name)
                base, w_base = n_hid[0], split_before(name) - first_block(name)

                def go_in(t, ph, blks):
                    if not isinstance(t, int) or t >= PHASES:
                        pe.wait_ge(hid_ready, t + (base - 2))
                    for j, b in enumerate(blks):
                        pe.wait_ge(w_low, b[2] + (w_base + 1))
                        for k in range(KD):
                            last = passes(ps[:, 4 + ph, j * T:(j + 1) * T], b[3], k * P,
                                          [x_split[:, i, k, :] for i in range(2)], k == 0, k == KD - 1)
                        last.then_inc(block_used, 1)

                def go_out(t, ph, b, first=False, final=False):
                    pe.wait_ge(hid_ready, t + (base + 1))
                    pe.wait_ge(w_low, b[2] + (w_base + 1))
                    for m in range(KD):
                        last = passes(wide[:, m, :], b[3], m * P, [h_split[:, ph, i, :] for i in range(2)],
                                      first and m % 2 == 0, final, shared=True)
                    last.then_inc(block_used, 1)

                def both(i, ph, b, first=False):
                    go_in(i + 2, (ph + 2) % PHASES, b[0:unit])
                    go_out(i, ph, b[unit], first)

                for t in range(2):
                    place.steps(pe, 1, unit, lambda _, ph, b, t=t: go_in(t, t, b))
                place.steps(pe, 1, unit + 1, lambda i, ph, b: both(0, 0, b, first=opens))
                place.steps(pe, n - 3, unit + 1, lambda i, ph, b: both(i + 1, (ph + 1) % PHASES, b), PHASES)
                for t in (n - 2, n - 1):
                    place.steps(pe, 1, 1, lambda _, ph, b, t=t: go_out(t, t % PHASES, b[0], final=(t == n - 1)))
                n_hid[0] += n
                leave()

            def pool_mix():
                enter(pe, "pool")
                for s in range(2):
                    pe.wait_ge(pool_in, s + 1)
                    for n in range(2):
                        at = 2880 + (2 * s + n) * T
                        last = mm(ps[:, 4 + 2 * s + n, 0:T], param("pool_w", n * P, n=P), work[:, at:at + T],
                                  start=True, stop=True)
                    last.then_inc(pool_out, 1)
                leave()

            def conv_norm():
                enter(pe, "conv")
                for i, at in enumerate((0, 512)):
                    pe.wait_ge(conv_v if i == 0 else conv_a, 1 if i == 0 else 2)
                    for k in range(2):
                        last = mm(pair[:, i, 0:T], const("mean_256"), work[:, at + k * T:at + (k + 1) * T],
                                  start=(k == 0), stop=(k == 1))
                    last.then_inc(conv_p, 1)
                leave()

            def gates():
                enter(pe, "gates")
                for g in range(2):
                    for k in range(KD):
                        last = mm(pair[0:MH, g, 0:T], gate_w[:, k, g * MH:(g + 1) * MH], x[:, LAT, k, :],
                                  start=(k == 0), stop=(k == KD - 1))
                last.then_inc(gates_p, 1)
                pe.wait_ge(gates_v, 2)
                for c in range(2):
                    last = mm(single[:, 0, c * MH:(c + 1) * MH], work[0:MH, 2048 + c * P:2048 + (c + 1) * P],
                              const("ident", MH)[:, 0:MH], start=True, stop=True)
                last.then_inc(gates_p, 1)
                leave()

            def mlstm():
                enter(pe, "mlstm")

                def spread_rows(h):
                    if h >= 2:
                        pe.wait_ge(m_weight, 3 * (h - 1))
                    for i, at in enumerate((2304, 2560)):
                        last = mm(pair[:, h % 2, i * T:(i + 1) * T], const("head_rows", MH)[:, h * P:(h + 1) * P],
                                  work[0:MH, at:at + T], start=True, stop=True)
                    last.then_inc(m_cast, 1)

                def score(h):
                    if h >= 2:
                        pe.wait_ge(m_st, h - 1)
                    for c in range(2):
                        for i, ((rows, kt), (_, qt)) in enumerate(zip(m_tiles(h, 6), m_tiles(h, 0))):
                            last = mm(wide[:, 4 * (h % 2) + c, :], proj[rows, kt, c * P:(c + 1) * P],
                                      proj[rows, qt, 0:T], start=(i == 0), stop=(i == 1))
                    last.then_inc(m_score, 1)

                def sums(h):
                    pe.wait_ge(m_st, h + 1)
                    if h >= 2:
                        pe.wait_ge(m_head, h - 1)
                    (_, ta), (half, tb) = m_tiles(h, 12)
                    w = [work[:, (2 * (h % 2) + c) * T:(2 * (h % 2) + c + 1) * T] for c in range(2)]
                    for c in range(2):
                        mm(wide[:, 4 * (h % 2) + 2, :], proj[:, ta, c * P:(c + 1) * P], w[c],
                           start=(c == 0), stop=(c == 1))
                    for c in range(2):
                        mm(single[half, h % 2, 0:T], proj[:, tb, c * P + half.start:c * P + half.stop], w[c],
                           start=(c == 0), stop=(c == 1))
                    for c in range(2):
                        last = mm(wide[:, 4 * (h % 2) + 3, :], const("ones"), w[c], start=(c == 0), stop=(c == 1))
                    last.then_inc(m_sum, 1)

                for h in range(MH):
                    spread_rows(h)
                    score(h)
                    if h:
                        sums(h - 1)
                sums(MH - 1)
                leave()

            def mlstm_norm():
                enter(pe, "mlstm_norm")
                for v in range(2):
                    if v:
                        pe.wait_ge(mn_a, 1)
                    for h in range(MH):
                        for i, (_, t) in enumerate(m_tiles(h, 0)):
                            src = work[:, t * T:(t + 1) * T] if v else mixed[:, t, 0:T]
                            ones = const("mean_192_half")[:, (h % 2) * P:(h % 2 + 1) * P] if i else const("mean_192")
                            last = mm(wide[:, 4 * v + h, :], ones, src, start=(i == 0), stop=(i == 1))
                    last.then_inc(mn_p, 1)
                leave()

            def rglru():
                enter(pe, "rglru")
                pe.wait_ge(rg_loaded, 16)
                w = work[0:RB, 2560:2560 + 2 * NRB * RB].rearrange("p (g c) -> p g c", c=RB)
                pe.wait_ge(rg_v, 1)
                for g in range(2 * NRB):
                    dst = ps[0:RB, g // 2, (g % 2) * T:(g % 2 + 1) * T]
                    last = mm(dst, w[:, g, :], proj[0:RB, g % NRB, T:2 * T], start=True, stop=True)
                last.then_inc(rg_p, 1)
                leave()

            def choose(l):
                enter(pe, f"choose{l}")
                pe.wait_ge(subk_loaded, 16 * (l - 1))
                for t in range(2):
                    for n in range(2 * PH):
                        last = mm(ps[:, 4 * t + n // 4, (n % 4) * P:(n % 4 + 1) * P],
                                  proj[:, n, t * P:(t + 1) * P], subk[:, n % 2, :], start=True, stop=True)
                    last.then_inc(k_score, 1)
                for t in range(2):
                    pe.wait_ge(k_pick, 2 * (l - 2) + t + 1)
                    for i in range(3):
                        last = mm(ps[:, 4 * t, i * P:(i + 1) * P], part(WORK + i * P, P), const("ident"),
                                  start=True, stop=True)
                    last.then_inc(k_turn, 1)
                leave()

            def spread(l, h):
                enter(pe, f"spread{l}{h}")
                base = (2 * (l - 2) + (h == "b")) * (T // (2 * GROUP))

                def one(it):
                    for b in range(2):
                        pe.wait_ge(hot_ready[b], it + (base + 1))
                        if not isinstance(it, int) or it + base:
                            pe.wait_ge(g_kept[b], it + base)
                        for u in range(GROUP):
                            for c in range(3):
                                last = mm(single[:, b, u * HALF:(u + 1) * HALF], hot_i[:, b, :, u],
                                          hot_w[:, b, c, :, u], start=(c == 0), stop=(c == 2))
                        last.then_inc(g_ready[b], 1)
                one(0)
                with pe.Fori(1, T // (2 * GROUP)) as it:
                    one(it)
                leave()

            for l in range(2):
                ada(l)
                enter(pe, f"project{l}")
                project(hT, PROJECT[l])
                if l == 0:
                    means("heads_norm", "mean_64", 2 * T, 8)
                rope(l)
                attend(l)
                if l == 0:
                    pool_mix()
                else:
                    means("subln", "mean_128", T, 6)
                    conv_norm()
                for n in ((CTX, LAT) if l == 0 else (LAT,)):
                    lo = n * T if l == 0 else 0
                    out_project(f"out{l}{n}", [(mixed[:, k, lo:lo + T], P) for k in range(KD)])
                    norm(f"norm1{l}{n}")
                    hidden(f"hidden{l}{n}", FH, 2)
                    norm(f"norm2{l}{n}")
            for l in (2, 3):
                enter(pe, f"project{l}")
                project(x[:, LAT, :, :], PROJECT[l])
                if l == 2:
                    gates()
                    mlstm()
                    mlstm_norm()
                    tiles = [(mixed[:, k, 0:T], P) for k in range(KD)]
                else:
                    rglru()
                    tiles = [(mixed[:, k, 0:T], P) for k in (8, 9)] + [(mixed[0:RB, k, 0:T], RB) for k in range(NRB)]
                enter(pe, f"memory{l}")
                pe.wait_ge(mem_loaded, 16 * (l - 1))
                project(res, PROJECT_MEMORY)
                attend(l)
                out_project(f"out{l}{LAT}", tiles)
                norm(f"norm1{l}{LAT}")
                enter(pe, f"query{l}")
                project(x[:, LAT, :, :], PROJECT_QUERY)
                choose(l)
                for h in "ab":
                    spread(l, h)
                    hidden(f"hidden{l}{h}", HALF, 1, opens=(h == "a"))
                norm(f"norm2{l}{LAT}")

        def copy_tiles(eng, par, copy, name, runs):
            done = first_block(name)
            for first, n, _, nt, _, width in runs:
                mine = (n + 1 - par) // 2

                def one(i):
                    eng.wait_ge(block_used, 2 * i + (done + par + 1))
                    at = PROJ + (first + 2 * i + par) * 512
                    dst = arena[0:width, at:at + nt] if isinstance(i, int) else \
                        arena[0:width, bass.ds(i * 1024 + (PROJ + (first + par) * 512), nt)]
                    copy(dst, pair[0:width, par, 0:nt]).then_inc(tile_out[par], 1)
                if mine > 2:
                    with eng.Fori(0, mine) as it:
                        one(it)
                else:
                    for i in range(mine):
                        one(i)
                done += n

        def hidden_steps(eng, place, name, n, unit, part_of, make):
            place.at = first_block(name)

            def parts(b):
                for blk in b:
                    part_of(blk)
            place.steps(eng, 2, unit, lambda i, ph, b: parts(b))
            make(0, 0)
            place.steps(eng, 1, unit + 1, lambda i, ph, b: (parts(b), make(1, 1)))
            place.steps(eng, 1, unit + 1, lambda i, ph, b: (parts(b), make(2, 2)))

            def one(i, ph, b):
                parts(b)
                make(i + 3, ph)
            place.steps(eng, n - 4, unit + 1, one, PHASES)
            place.steps(eng, 2, 1, lambda i, ph, b: parts(b))
            make(n - 1, (n - 1) % PHASES)

        @block.scalar
        def _(act):
            place = RingPlace()
            n_unit, n_ln, n_hid, n_sq = [0], [0], [0], [0]
            f = nc.scalar.activation

            def leave():
                act.drain().then_inc(stage["a"], 1)

            def project(name, runs):
                enter(act, name)
                copy_tiles(act, 0, lambda o, i: f(o, i, ACT.Copy), name, runs)
                leave()

            def root(dst, src, eps):
                f(dst, src, ACT.Sqrt, bias=eps_col[0:dst.shape[0], eps:eps + 1]).then_inc(rooted, 1)

            def squares(name, tiles):
                enter(act, name)
                for i in range(len(tiles) + 1):
                    if i < len(tiles):
                        n = tiles[i].shape[1]
                        if i >= 2:
                            act.wait_ge(mean_ready, n_sq[0] + i - 1)
                        f(work[:, (i % 2) * 512:(i % 2) * 512 + n], tiles[i], ACT.Square).then_inc(squared, 1)
                    if i:
                        b = (i - 1) % 2
                        act.wait_ge(mean_ready, n_sq[0] + i)
                        if i >= 3:
                            act.wait_ge(normed, n_sq[0] + i - 2)
                        root(work[:, 1024 + b * 512:1024 + b * 512 + n], pair[:, b, 0:n], 0)
                n_sq[0] += len(tiles)
                leave()

            def attend(l):
                units = units_of(l)
                enter(act, f"attend{l}")
                base = n_unit[0]

                def exps(i):
                    act.wait_ge(m_ready, base + i + 1)
                    if base + i >= 2:
                        act.wait_ge(t_ready, base + i - 1)
                    b = 4 * (i % 2)
                    for r in range(2):
                        last = f(probs[:, i % 2, r, 0:units[i]["nk"]], scores_at(i, units[i]["nk"])[:, r, :], ACT.Exp,
                                 bias=cols[:, 8 + b + r:9 + b + r], scale=HD ** -0.5,
                                 accum_out=cols[:, 16 + b + r:17 + b + r])
                    last.then_inc(e_ready, 1)

                def heads(i):
                    u = units[i]
                    act.wait_ge(o_ready, base + i + 1)
                    lo, m = u["rows"]
                    f(u["out"], single[lo:lo + m, i % 2, 0:P if u["diff"] else 2 * P], ACT.Copy).then_inc(o_out, 1)

                n = len(units)
                exps(0)
                for i in range(n):
                    if i + 1 < n:
                        exps(i + 1)
                    if i:
                        heads(i - 1)
                heads(n - 1)
                n_unit[0] += n
                leave()

            def norm(name):
                enter(act, name)
                act.wait_ge(ln_centred, n_ln[0] + 1)
                f(work[:, 0:KD * T], res[:, :, :].rearrange("p k t -> p (k t)"), ACT.Square).then_inc(ln_squared, 1)
                n_ln[0] += 1
                act.wait_ge(ln_var, n_ln[0])
                root(work[:, 4096:4096 + T], pair[:, 1, 0:T], 0 if name[5] in "01" else 1)
                leave()

            def hidden(name, n, unit, func, at, dst):
                enter(act, name)
                base = n_hid[0]

                def high(b):
                    slot, turn, seq, w = b
                    act.wait_ge(filled[slot], (turn + 1) * 16)
                    act.wait_ge(block_used, seq - (SPLIT - 1))
                    f(w_split[:, w, 0, :], ring[:, slot, :], ACT.Copy).then_inc(w_high, 1)

                def one(t, ph):
                    act.wait_ge(block_used, after_input(name, t, unit))
                    if not isinstance(t, int) or t >= PHASES:
                        act.wait_ge(hid_ready, t + (base - 2))
                    f(dst[:, ph, :], ps[:, 4 + ph, at:at + T], func).then_inc(gate_ready, 1)
                hidden_steps(act, place, name, n, unit, high, one)
                n_hid[0] += n
                leave()

            def spread(l, h):
                enter(act, f"spread{l}{h}")
                base = (2 * (l - 2) + (h == "b")) * (T // (2 * GROUP))
                with act.Fori(0, T // (2 * GROUP)) as it:
                    for b in range(2):
                        act.wait_ge(g_ready[b], it + (base + 1))
                        f(arena[:, bass.ds(it * 1024 + b * 512, 512)], single[:, b, :], ACT.Copy).then_inc(g_kept[b], 1)
                leave()

            enter(act, "lambda")
            act.wait_ge(lam_sum, 1)
            f(cols[:, 34:36], cols[:, 32:34], ACT.Exp).then_inc(lam_exp, 1)
            leave()
            for l in range(2):
                if l == 0:
                    enter(act, "ada0")
                    act.wait_ge(loaded, 16 * 6)
                    f(cond[:, 1, :, :], cond[:, 0, :, :], ACT.Silu).then_inc(silu_done, 1)
                    leave()
                project(f"project{l}", PROJECT[l])
                if l == 0:
                    squares("heads_norm", [proj[:, j, :] for j in range(8)])
                attend(l)
                if l == 1:
                    squares("subln", [mixed[:, h, 0:T] for h in range(6)])
                    enter(act, "conv")
                    f(work[:, 2048:2560].rearrange("p (k t) -> p k t", k=2), proj[:, 20:22, 0:T],
                      ACT.Sigmoid).then_inc(conv_a, 1)
                    act.wait_ge(conv_v, 2)
                    f(work[:, 512:1024], work[:, 0:512], ACT.Square).then_inc(conv_a, 1)
                    act.wait_ge(conv_p, 2)
                    root(work[:, 1024:1024 + T], pair[:, 1, 0:T], 0)
                    for k in range(2):
                        act.wait_ge(conv_v, 3)
                        f(mixed[:, 6 + k, 0:T], work[:, k * T:(k + 1) * T], ACT.Silu,
                          bias=param("conv_bb", k), scale=param("conv_g", k)).then_inc(conv_a, 1)
                    leave()
                for n in ((CTX, LAT) if l == 0 else (LAT,)):
                    norm(f"norm1{l}{n}")
                    hidden(f"hidden{l}{n}", FH, 2, ACT.Silu, T, gate)
                    norm(f"norm2{l}{n}")
            for l in (2, 3):
                project(f"project{l}", PROJECT[l])
                if l == 2:
                    enter(act, "gates")
                    act.wait_ge(gates_v, 1)
                    f(work[0:MH, 768:1024], work[0:MH, 512:768], ACT.Exp, scale=-1.0).then_inc(gates_a, 1)
                    leave()
                    enter(act, "mlstm")
                    for h in range(MH):
                        act.wait_ge(m_cast, h + 1)
                        if h >= 2:
                            act.wait_ge(m_sum, h - 1)
                            act.wait_ge(m_head, h - 1)
                        for c in range(2):
                            at = (2 * (h % 2) + c) * T
                            f(work[:, at:at + T], pair[:, h % 2, 0:T], ACT.Exp, scale=-1.0,
                              bias=cols[:, c * MH + h:c * MH + h + 1]).then_inc(m_weight, 1)
                        f(work[:, 1024 + (h % 2) * T:1024 + (h % 2 + 1) * T], pair[:, h % 2, T:2 * T],
                          ACT.Exp).then_inc(m_weight, 1)
                    leave()
                    enter(act, "mlstm_norm")
                    act.wait_ge(mn_v, 1)
                    f(work[:, 0:6 * T].rearrange("p (k t) -> p k t", k=6), mixed[:, 0:6, 0:T],
                      ACT.Square).then_inc(mn_a, 1)
                    act.wait_ge(mn_p, 2)
                    root(work[:, 2048:2048 + MH * T].rearrange("p (h t) -> p h t", h=MH), wide[:, 4:8, :], 1)
                    f(proj[:, 18:24, 0:T], proj[:, 18:24, 0:T], ACT.Sigmoid).then_inc(mn_a, 1)
                    leave()
                else:
                    enter(act, "rglru")
                    r, i_, a_, th = rg_tiles()[1:5]
                    act.wait_ge(rg_v, 1)
                    f(cols[0:RB, 16:24], cols[0:RB, 8:16], ACT.Exp, scale=-1.0).then_inc(rg_a, 1)
                    act.wait_ge(rg_p, 1)
                    for g in range(NRB):
                        f(r[:, g, :], ps[0:RB, g // 2, (g % 2) * T:(g % 2 + 1) * T],
                          ACT.Sigmoid, bias=param("r_ba", g, RB))
                        last = f(i_[:, g, :],
                                 ps[0:RB, 4 + g // 2, (g % 2) * T:(g % 2 + 1) * T],
                                 ACT.Sigmoid, bias=param("r_bx", g, RB))
                    last.then_inc(rg_a, 1)
                    act.wait_ge(rg_a, 2)
                    act.wait_ge(rg_v, 2)
                    for g in range(NRB):
                        f(a_[:, g, :], r[:, g, :], ACT.Exp,
                          scale=cols[0:RB, 24 + g:25 + g])
                        last = f(th[:, g, :], r[:, g, :], ACT.Tanh,
                                 scale=cols[0:RB, 32 + g:33 + g])
                    last.then_inc(rg_a, 1)
                    act.wait_ge(rg_v, 3)
                    f(r, r, ACT.Sqrt).then_inc(rooted, 1)
                    f(proj[0:RB, 0:NRB, 0:T], proj[0:RB, 0:NRB, 0:T], ACT.Gelu).then_inc(rg_a, 1)
                    leave()
                project(f"memory{l}", PROJECT_MEMORY)
                attend(l)
                norm(f"norm1{l}{LAT}")
                project(f"query{l}", PROJECT_QUERY)
                enter(act, f"choose{l}")
                for t in range(2):
                    act.wait_ge(k_shift, 2 * (l - 2) + t + 1)
                    f(part(17920, P), part(17920, P), ACT.Exp).then_inc(k_exp, 1)
                for t in range(2):
                    act.wait_ge(k_turn, 2 * (l - 2) + t + 1)
                    f(chosen[:, :, t * P:(t + 1) * P], ps[:, 4 * t, 0:3 * P].rearrange("p (a b) -> p a b", a=3),
                      ACT.Copy).then_inc(k_keep, 1)
                leave()
                for h in "ab":
                    spread(l, h)
                    hidden(f"hidden{l}{h}", HALF, 1, ACT.Gelu, 0, gelu)
                norm(f"norm2{l}{LAT}")

        @block.vector
        def _(dve):
            chain = Chain(dve, chain_v)
            place = RingPlace()
            n_unit, n_ln, n_hid, n_sq, n_root = [0], [0], [0], [0], [0]
            v = nc.vector

            def leave():
                dve.drain().then_inc(stage["v"], 1)

            def project(name, runs):
                enter(dve, name)
                copy_tiles(dve, 1, v.tensor_copy, name, runs)
                leave()

            def inverse_root(t):
                n_root[0] += 1
                dve.wait_ge(rooted, n_root[0])
                chain(v.reciprocal(t, t))

            def heads_norm(name, tiles, gain, factor):
                enter(dve, name)
                chain(v.tensor_scalar(cols[:, 40:41], gain, factor, None, ALU.mult))
                for i, t in enumerate(tiles):
                    n = t.shape[1]
                    r = work[:, 1024 + (i % 2) * 512:1024 + (i % 2) * 512 + n]
                    inverse_root(r)
                    g = gain if name != "heads_norm" else (param("q_gain") if i < 6 else param("k_gain"))
                    v.scalar_tensor_tensor(t, t, cols[:, 40:41] if name != "heads_norm" else g, r,
                                           ALU.mult, ALU.mult).then_inc(normed, 1)
                n_sq[0] += len(tiles)
                leave()

            def rope(l):
                enter(dve, f"rope{l}")
                base = len(ROPE[0]) if l else 0
                for i, (j, lat) in enumerate(ROPE[l]):
                    t = proj[:, j, lat:lat + T]
                    s = work[:, (i % 2) * T:(i % 2 + 1) * T]
                    dve.wait_ge(turned_pos, base + i + 1)
                    v.tensor_tensor(s, pair[:, i % 2, 0:T], const("sin"), ALU.mult)
                    chain(v.tensor_tensor(t, t, const("cos"), ALU.mult))
                    v.tensor_tensor(t, t, s, ALU.add).then_inc(roped, 1)
                leave()

            def attend(l):
                units = units_of(l)
                enter(dve, f"attend{l}")
                base = n_unit[0]

                def maxima(i):
                    b = 4 * (i % 2)
                    dve.wait_ge(s_ready, base + i + 1)
                    chain(v.tensor_reduce(cols[:, b:b + 2], scores_at(i, units[i]["nk"]), AX_X, ALU.max))
                    v.tensor_scalar(cols[:, 8 + b:10 + b], cols[:, b:b + 2], -HD ** -0.5, None,
                                    ALU.mult).then_inc(m_ready, 1)

                def diagonals(i):
                    b = 4 * (i % 2)
                    dve.wait_ge(e_ready, base + i + 1)
                    chain(v.reciprocal(cols[:, 24 + b:26 + b], cols[:, 16 + b:18 + b]))
                    for r in range(2):
                        second = neg_lam[:, 0:1] if units[i]["diff"] and r else None
                        op = (ALU.mult, ALU.mult) if second is not None else (ALU.mult,)
                        last = v.tensor_scalar(diag[:, 2 * (i % 2) + r, :], const("ident"),
                                               cols[:, 24 + b + r:25 + b + r], second, *op)
                    last.then_inc(d_ready, 1)

                def turned(i):
                    u = units[i]
                    dve.wait_ge(t_ready, base + i + 1)
                    if base + i >= 2:
                        dve.wait_ge(o_ready, base + i - 1)
                    n = u["nk"] * (1 if u["diff"] else 2)
                    v.tensor_copy(probsT[:, i % 2, 0:n], ps[:, 4:6, :].rearrange("p b n -> p (b n)")[:, 0:n])\
                        .then_inc(pt_ready, 1)

                n = len(units)
                maxima(0)
                for i in range(n):
                    diagonals(i)
                    if i + 1 < n:
                        maxima(i + 1)
                    turned(i)
                n_unit[0] += n
                leave()

            def gated_sum(name, s, l, part_):
                j = 1 if s == CTX else 0
                chain(v.tensor_scalar(res[:, :, :], x[:, s, :, :], ALPHA, None, ALU.mult))
                dve.wait_ge(block_used, first_block(name) + blocks_in(name))
                for k in range(KD):
                    m = part_ * KD + k
                    v.scalar_tensor_tensor(res[:, k, :], wide[:, k, :], mod[:, l, m, j:j + 1], res[:, k, :],
                                           ALU.mult, ALU.add)

            def plain_sum(name):
                dve.wait_ge(block_used, first_block(name) + blocks_in(name))
                v.scalar_tensor_tensor(res[:, :, :], x[:, LAT, :, :], ALPHA, wide, ALU.mult, ALU.add)

            def norm(name, s, ln, k12, eps):
                enter(dve, name)
                n_ln[0] += 1
                dve.wait_ge(ln_mean, n_ln[0])
                v.tensor_tensor(res[:, :, :], res[:, :, :], over(pair[:, 0, 0:T], KD), ALU.subtract)\
                    .then_inc(ln_centred, 1)
                inverse_root(work[:, 4096:4096 + T])
                chain(v.tensor_tensor(res[:, :, :], res[:, :, :], over(work[:, 4096:4096 + T], KD), ALU.mult))
                for k in range(KD):
                    v.tensor_scalar(x[:, s, k, :], res[:, k, :], param(f"ln{ln}g{k12}", k), param(f"ln{ln}b{k12}", k),
                                    ALU.mult, ALU.add)
                leave()

            def split(dst, src):
                chain(v.tensor_copy(dst[:, 0], src))
                chain(v.tensor_tensor(dst[:, 1], src, dst[:, 0].bitcast(F32), ALU.subtract))

            def hidden(name, n, unit, make, raw):
                base, w_base = n_hid[0], split_before(name) - first_block(name)

                def low(b):
                    slot, _, seq, w = b
                    dve.wait_ge(w_high, seq + (w_base + 1))
                    v.tensor_tensor(w_split[:, w, 1, :], ring[:, slot, :], w_split[:, w, 0, :].bitcast(F32),
                                    ALU.subtract).then_inc(w_low, 1)

                def one(t, ph):
                    dve.wait_ge(gate_ready, t + (base + 1))
                    make(t, ph).then_inc(hid_made, 1)
                    dve.wait_ge(hid_made, t + (base + 1))
                    if not isinstance(t, int) or t >= PHASES:
                        dve.wait_ge(block_used, after_output(name, t - PHASES, unit))
                    v.tensor_copy(h_split[:, ph, 0, :], raw[:, ph, :]).then_inc(hid_high, 1)
                    dve.wait_ge(hid_high, t + (base + 1))
                    v.tensor_tensor(h_split[:, ph, 1, :], raw[:, ph, :], h_split[:, ph, 0, :].bitcast(F32),
                                    ALU.subtract).then_inc(hid_ready, 1)
                hidden_steps(dve, place, name, n, unit, low, one)
                n_hid[0] += n

            def swiglu(t, ph):
                return v.tensor_tensor(hid[:, ph, :], ps[:, 4 + ph, 0:T], gate[:, ph, :], ALU.mult)

            def weigh(t, ph):
                g = G[:, :, t] if isinstance(t, int) else G[:, :, bass.ds(t, 1)].rearrange("p n o -> p (n o)")
                return v.tensor_tensor(coef[:, ph, :], gelu[:, ph, :], g, ALU.mult)

            def pool_windows():
                enter(dve, "pool")
                W = T + 32
                U, S2, S4, S8, S16 = (work[:, i * 2 * W:(i + 1) * 2 * W].rearrange("p (n t) -> p n t", n=2)
                                      for i in range(5))
                chain(v.memset(work[:, 0:10 * W], 0.0))
                for s in range(2):
                    chain(v.tensor_copy(U[:, :, 16:16 + T], proj[:, 10:12, s * T:(s + 1) * T]))
                    chain(v.tensor_tensor(S2[:, :, 1:W], U[:, :, 0:W - 1], U[:, :, 1:W], ALU.add))
                    chain(v.tensor_tensor(S4[:, :, 2:W - 1], S2[:, :, 1:W - 2], S2[:, :, 3:W], ALU.add))
                    chain(v.tensor_tensor(S8[:, :, 4:W - 3], S4[:, :, 2:W - 5], S4[:, :, 6:W - 1], ALU.add))
                    chain(v.tensor_tensor(S16[:, :, 8:W - 7], S8[:, :, 4:W - 11], S8[:, :, 12:W - 3], ALU.add))
                    pooled = work[:, 10 * W + 2 * s * T:10 * W + 2 * (s + 1) * T].rearrange("p (n t) -> p n t", n=2)
                    inv = const("inv_count").rearrange("p (n t) -> p n t", n=2)
                    for g, S in enumerate((S2, S4, S8, S16)):
                        rows, n = slice((g % 2) * 64, (g % 2 + 1) * 64), g // 2
                        last = v.tensor_tensor(pooled[rows, n, :], S[rows, n, 16:16 + T], inv[rows, n, :], ALU.mult)
                    chain(last)
                    v.tensor_tensor(pooled, pooled, U[:, :, 16:16 + T], ALU.subtract).then_inc(pool_in, 1)
                    dve.wait_ge(pool_in, s + 1)
                for s in range(2):
                    dve.wait_ge(pool_out, s + 1)
                    for n in range(2):
                        v.tensor_scalar(mixed[:, 6 + n, s * T:(s + 1) * T], ps[:, 4 + 2 * s + n, 0:T],
                                        param("pool_scale", n), None, ALU.mult)
                leave()

            def conformer():
                enter(dve, "conv")
                Z = work[:, 2560:2560 + 2 * (T + 2 * CPAD)].rearrange("p (k t) -> p k t", k=2)
                acc = work[:, 0:512].rearrange("p (k t) -> p k t", k=2)
                chain(v.memset(Z, 0.0))
                dve.wait_ge(conv_a, 1)
                chain(v.tensor_tensor(Z[:, :, CPAD:CPAD + T], proj[:, 18:20, 0:T],
                                      work[:, 2048:2560].rearrange("p (k t) -> p k t", k=2), ALU.mult))
                for i in range(CONV):
                    for k in range(2):
                        w = param("conv_w", k * CONV + i)
                        if i == 0:
                            last = v.tensor_scalar(acc[:, k, :], Z[:, k, 0:T], w, param("conv_b", k), ALU.mult, ALU.add)
                        else:
                            last = v.scalar_tensor_tensor(acc[:, k, :], Z[:, k, i:i + T], w, acc[:, k, :],
                                                          ALU.mult, ALU.add)
                    if i < CONV - 1:
                        chain(last)
                last.then_inc(conv_v, 1)
                dve.wait_ge(conv_p, 1)
                v.tensor_tensor(acc, acc, over(pair[:, 0, 0:T], 2), ALU.subtract).then_inc(conv_v, 1)
                inverse_root(work[:, 1024:1024 + T])
                v.tensor_tensor(acc, acc, over(work[:, 1024:1024 + T], 2), ALU.mult).then_inc(conv_v, 1)
                leave()

            def log1p(dst, e, s, s2):
                chain(v.tensor_scalar(s, e, 2.0, None, ALU.add))
                chain(v.reciprocal(s, s))
                chain(v.tensor_tensor(s, s, e, ALU.mult))
                chain(v.tensor_tensor(s2, s, s, ALU.mult))
                chain(v.tensor_scalar(dst, s2, 1.0 / 17, None, ALU.mult))
                for n in range(15, 2, -2):
                    chain(v.scalar_tensor_tensor(dst, dst, 1.0 / n, s2, ALU.add, ALU.mult))
                chain(v.scalar_tensor_tensor(dst, dst, 1.0, s, ALU.add, ALU.mult))
                chain(v.tensor_scalar(dst, dst, 2.0, None, ALU.mult))

            def gates():
                enter(dve, "gates")

                def row(i):
                    return work[0:MH, i * T:(i + 1) * T]
                ig, fg, nf, e, F, t1, t2, lf, g, mx, fl, one = (row(i) for i in range(12))
                dve.wait_ge(gates_p, 1)
                v.tensor_scalar(ig, pair[0:MH, 0, 0:T], param("i_bias", 0, MH), None, ALU.add)
                v.memset(one, 1.0)
                chain(v.tensor_scalar(fg, pair[0:MH, 1, 0:T], param("f_bias", 0, MH), None, ALU.add))
                chain(v.tensor_scalar(nf, fg, -1.0, None, ALU.mult))
                v.tensor_tensor(nf, nf, fg, ALU.max).then_inc(gates_v, 1)
                dve.wait_ge(gates_a, 1)
                log1p(lf, e, t1, t2)
                chain(v.tensor_scalar(fg, fg, 0.0, None, ALU.min))
                chain(v.tensor_tensor(lf, fg, lf, ALU.subtract))
                chain(v.tensor_tensor_scan(F, one, lf, 0.0, ALU.mult, ALU.add))
                v.tensor_tensor(g, ig, F, ALU.subtract).then_inc(gates_v, 1)
                dve.wait_ge(gates_v, 2)
                chain(v.tensor_tensor_scan(mx, one, g, 0.0, ALU.mult, ALU.max))
                chain(v.tensor_tensor(fl, F, mx, ALU.add))
                chain(v.tensor_scalar(fl, fl, -1.0, None, ALU.mult))
                dve.wait_ge(gates_p, 2)
                v.tensor_copy(cols[:, 0:2 * MH], single[:, 0, 0:2 * MH])
                leave()

            def mlstm():
                enter(dve, "mlstm")

                def weighted(h):
                    dve.wait_ge(m_score, h + 1)
                    dve.wait_ge(m_mask, 2 * h + 2)
                    for c in range(2):
                        w = work[:, (2 * (h % 2) + c) * T:(2 * (h % 2) + c + 1) * T]
                        last = v.scalar_tensor_tensor(w, wide[:, 4 * (h % 2) + c, :], MDH ** -0.5, w,
                                                      ALU.mult, ALU.mult)
                    last.then_inc(m_st, 1)

                def divided(h):
                    dve.wait_ge(m_sum, h + 1)
                    dve.wait_ge(m_weight, 3 * h + 3)
                    floor = work[:, 1024 + (h % 2) * T:1024 + (h % 2 + 1) * T]
                    den = wide[:, 4 * (h % 2) + 3, :]
                    chain(v.tensor_tensor(floor, den, floor, ALU.max))
                    chain(v.scalar_tensor_tensor(floor, den, -1.0, floor, ALU.mult, ALU.max))
                    chain(v.reciprocal(floor, floor))
                    (_, ta), (half, tb) = m_tiles(h, 0)
                    v.tensor_tensor(mixed[:, ta, 0:T], wide[:, 4 * (h % 2) + 2, :], floor, ALU.mult)
                    v.tensor_tensor(mixed[half, tb, 0:T], single[half, h % 2, 0:T], floor[half, :], ALU.mult)\
                        .then_inc(m_head, 1)

                for h in range(MH):
                    weighted(h)
                    if h:
                        divided(h - 1)
                divided(MH - 1)
                leave()

            def mlstm_norm():
                enter(dve, "mlstm_norm")
                for i in range(2):
                    dve.wait_ge(mn_p, i + 1)
                    if i:
                        rstd = work[:, 2048:2048 + MH * T].rearrange("p (h t) -> p h t", h=MH)
                        inverse_root(work[:, 2048:2048 + MH * T])
                    for h in range(MH):
                        for rows, t in m_tiles(h, 0):
                            src = rstd[rows, h, :] if i else wide[rows, h, :]
                            last = v.tensor_tensor(mixed[rows, t, 0:T], mixed[rows, t, 0:T], src,
                                                   ALU.mult if i else ALU.subtract)
                    last.then_inc(mn_v, 1)
                    dve.wait_ge(mn_v, i + 1)
                dve.wait_ge(mn_a, 2)
                for t in range(6):
                    v.scalar_tensor_tensor(mixed[:, t, 0:T], mixed[:, t, 0:T], param("mnorm", t),
                                           proj[:, 18 + t, 0:T], ALU.mult, ALU.mult)
                leave()

            def rglru():
                enter(dve, "rglru")
                W = T + RG_CONV - 1
                xp = work[0:RB, 0:NRB * W].rearrange("p (g t) -> p g t", g=NRB)
                xc, r, i_, a_, th = rg_tiles()
                chain(v.tensor_scalar(cols[0:RB, 8:16], param("r_lam", 0, RB, NRB), -1.0, None, ALU.mult))
                chain(v.tensor_tensor(cols[0:RB, 8:16], cols[0:RB, 8:16], param("r_lam", 0, RB, NRB), ALU.max))
                v.memset(xp[:, :, 0:RG_CONV - 1], 0.0)
                chain(v.tensor_copy(xp[:, :, RG_CONV - 1:W], proj[0:RB, 8:16, 0:T]))
                for j in range(RG_CONV):
                    for g in range(NRB):
                        w = param("rconv_w", g * RG_CONV + j, RB)
                        if j == 0:
                            last = v.tensor_scalar(xc[:, g, :], xp[:, g, 0:T], w, param("rconv_b", g, RB),
                                                   ALU.mult, ALU.add)
                        else:
                            last = v.scalar_tensor_tensor(xc[:, g, :], xp[:, g, j:j + T], w, xc[:, g, :],
                                                          ALU.mult, ALU.add)
                    if j < RG_CONV - 1:
                        chain(last)
                last.then_inc(rg_v, 1)
                dve.wait_ge(rg_v, 1)
                dve.wait_ge(rg_a, 1)
                log1p(cols[0:RB, 48:56], cols[0:RB, 16:24], cols[0:RB, 56:64], cols[0:RB, 64:72])
                chain(v.tensor_scalar(cols[0:RB, 72:80], param("r_lam", 0, RB, NRB), -1.0, 0.0, ALU.mult, ALU.max))
                chain(v.tensor_tensor(cols[0:RB, 48:56], cols[0:RB, 48:56], cols[0:RB, 72:80], ALU.add))
                v.tensor_scalar(cols[0:RB, 24:32], cols[0:RB, 48:56], -RG_C, None, ALU.mult)
                v.tensor_scalar(cols[0:RB, 32:40], cols[0:RB, 48:56], RG_C, None, ALU.mult).then_inc(rg_v, 1)
                dve.wait_ge(rg_a, 2)
                chain(v.tensor_tensor(i_, i_, xc, ALU.mult))
                dve.wait_ge(rg_a, 3)
                chain(v.tensor_scalar(r, th, 1.0, None, ALU.add))
                chain(v.reciprocal(r, r))
                chain(v.scalar_tensor_tensor(r, th, 2.0, r, ALU.mult, ALU.mult))
                v.tensor_scalar(r, r, ROOT_MIN, None, ALU.max).then_inc(rg_v, 1)
                n_root[0] += 1
                dve.wait_ge(rooted, n_root[0])
                chain(v.tensor_tensor(i_, i_, r, ALU.mult))
                for g in range(NRB):
                    last = v.tensor_tensor_scan(xc[:, g, :], a_[:, g, :], i_[:, g, :], 0.0, ALU.mult, ALU.add)
                chain(last)
                dve.wait_ge(rg_a, 4)
                v.tensor_tensor(mixed[0:RB, 0:NRB, 0:T], xc, proj[0:RB, 0:NRB, 0:T], ALU.mult)
                leave()

            def choose(l):
                enter(dve, f"choose{l}")
                tmp = part(8192, 2 * PH, KEYS)
                sv = part(10240, 2 * PH, TOPK)
                si = part(10496, 2 * PH, TOPK).bitcast(U32)
                sif = part(10752, 2 * PH, TOPK)
                cand = part(11008, PH, TOPK * TOPK)
                tmp2 = part(13056, PH, TOPK * TOPK)
                fv = part(15104, PH, TOPK)
                fi = part(15232, PH, TOPK).bitcast(U32)
                sel = [part(15360, PH, TOPK).bitcast(U32), part(15488, PH, TOPK).bitcast(U32)]
                self_ = [part(15616, PH, TOPK), part(15744, PH, TOPK)]
                eq = part(15872, P, TOPK)
                w = part(17920, PH, TOPK)
                wsum = part(18048, PH)
                picks = part(WORK, 3, P)

                def top16(values, indices, at, spare_, n):
                    for i in range(n):
                        last = v.max(values[:, i, 0:8], at(i))
                    chain(last)
                    for i in range(n):
                        v.max_index(indices[:, i, 0:8], values[:, i, 0:8], at(i))
                        last = v.match_replace(spare_[:, i, :], values[:, i, 0:8], at(i), NEG)
                    chain(last)
                    for i in range(n):
                        last = v.max(values[:, i, 8:16], spare_[:, i, :])
                    chain(last)
                    for i in range(n):
                        last = v.max_index(indices[:, i, 8:16], values[:, i, 8:16], spare_[:, i, :])
                    chain(last)

                for t in range(2):
                    dve.wait_ge(k_score, 2 * (l - 2) + t + 1)
                    top16(sv, si, lambda i: ps[:, 4 * t + i // 4, (i % 4) * P:(i % 4 + 1) * P], tmp, 2 * PH)
                    chain(v.tensor_copy(sif, si))
                    for h in range(PH):
                        last = v.tensor_tensor(
                            cand[:, h, :].rearrange("p (a b) -> p a b", a=TOPK),
                            sv[:, 2 * h, :].unsqueeze(2).to_broadcast([P, TOPK, TOPK]),
                            sv[:, 2 * h + 1, :].unsqueeze(1).to_broadcast([P, TOPK, TOPK]), ALU.add)
                    chain(last)
                    top16(fv, fi, lambda h: cand[:, h, :], tmp2, PH)
                    if t:
                        dve.wait_ge(k_turn, 2 * (l - 2) + 1)
                    v.tensor_tensor(w, fv, fv[:, :, 0:1].to_broadcast([P, PH, TOPK]), ALU.subtract)\
                        .then_inc(k_shift, 1)
                    v.tensor_scalar(sel[0], fi, 4, None, ALU.logical_shift_right)
                    chain(v.tensor_scalar(sel[1], fi, TOPK - 1, None, ALU.bitwise_and))
                    for i in range(2):
                        last = v.tensor_copy(self_[i], sel[i])
                    chain(last)
                    iota = const("iota")[:, 0:TOPK].unsqueeze(1).to_broadcast([P, P, TOPK])
                    for i in range(2):
                        place = self_[i].rearrange("p h k -> p (h k)").unsqueeze(2).to_broadcast([P, P, TOPK])
                        chain(v.tensor_tensor(eq, place, iota, ALU.is_equal))
                        for h in range(PH):
                            rows = eq[:, h * TOPK:(h + 1) * TOPK, :]
                            last = v.tensor_tensor(rows, rows, over(sif[:, 2 * h + i, :], TOPK), ALU.mult)
                        chain(last)
                        chain(v.tensor_reduce(picks[:, i, :], eq, AX_X, ALU.add))
                    dve.wait_ge(k_exp, 2 * (l - 2) + t + 1)
                    chain(v.tensor_reduce(wsum, w, AX_X, ALU.add))
                    chain(v.reciprocal(wsum, wsum))
                    v.tensor_tensor(picks[:, 2, :].rearrange("p (h k) -> p h k", h=PH), w,
                                    wsum.unsqueeze(2).to_broadcast([P, PH, TOPK]), ALU.mult).then_inc(k_pick, 1)
                    dve.wait_ge(k_pick, 2 * (l - 2) + t + 1)
                leave()

            def tables():
                w, left = chosen[:, 2, :], res[:, 3, :]
                v.tensor_copy(keys, chosen[:, 0:2, :])
                v.tensor_copy(places, const("iota").unsqueeze(2).to_broadcast([P, KEYS, GROUP]))
                for c in range(3):
                    chain(v.tensor_copy(weight3[:, c, :], w))
                    if c < 2:
                        chain(v.tensor_tensor(left, w, weight3[:, c, :], ALU.subtract))
                        w = left

            def spread(l, h):
                enter(dve, f"spread{l}{h}")
                base = (2 * (l - 2) + (h == "b")) * (T // (2 * GROUP))
                lo = HALF * (h == "b")

                def one(it):
                    for b in range(2):
                        at = bass.ds(it * (2 * GROUP) + b * GROUP, GROUP)
                        if not isinstance(it, int) or it + base:
                            dve.wait_ge(g_ready[b], it + base)
                        v.tensor_tensor(hot_j[:, b], places[:, lo:lo + HALF, :], over(keys[:, 1, at], HALF), ALU.is_equal)\
                            .then_inc(hot_j_made, 1)
                        v.tensor_tensor(hot_i[:, b], places, over(keys[:, 0, at], KEYS), ALU.is_equal)
                        dve.wait_ge(hot_j_made, it * 2 + (2 * base + b + 1))
                        v.tensor_tensor(hot_w[:, b], hot_j[:, b].unsqueeze(1).to_broadcast([P, 3, HALF, GROUP]),
                                        weight3[:, :, at].unsqueeze(2).to_broadcast([P, 3, HALF, GROUP]), ALU.mult)\
                            .then_inc(hot_ready[b], 1)
                one(0)
                with dve.Fori(1, T // (2 * GROUP)) as it:
                    one(it)
                leave()

            enter(dve, "lambda")
            v.memset(eps_col[:, 0:1], EPS1)
            v.memset(eps_col[:, 1:2], EPS2)
            dve.wait_ge(loaded, 16 * 6)
            for i in range(2):
                v.tensor_tensor(work[:, i * HD:(i + 1) * HD], param(f"lq{i + 1}", n=HD), param(f"lk{i + 1}", n=HD),
                                ALU.mult).then_inc(chain_v, 1)
            chain.n += 2
            dve.wait_ge(chain_v, chain.n)
            v.tensor_reduce(cols[:, 32:34], work[:, 0:2 * HD].rearrange("p (a b) -> p a b", a=2), AX_X, ALU.add)\
                .then_inc(lam_sum, 1)
            dve.wait_ge(lam_exp, 1)
            chain(v.tensor_tensor(neg_lam[:, :], cols[:, 35:36], cols[:, 34:35], ALU.subtract))
            v.tensor_scalar(neg_lam[:, :], neg_lam[:, :], -LAM_INIT, None, ALU.add)
            leave()

            for l in range(2):
                enter(dve, f"ada{l}")

                def rows(n):
                    dve.wait_ge(block_used, first_block(f"ada{l}") + (n + 1) * KD)
                    if n >= 2:
                        dve.wait_ge(ada_turned, 6 * l + n - 1)
                    v.tensor_copy(work[0:2, (n % 2) * D:(n % 2 + 1) * D].rearrange("p (c n) -> p c n", c=2),
                                  ps[0:2, 2 * (n % 2):2 * (n % 2) + 2, :]).then_inc(ada_rows, 1)

                def biased(n):
                    dve.wait_ge(ada_turned, 6 * l + n + 1)
                    v.tensor_tensor(mod[:, l, n * KD:(n + 1) * KD, :],
                                    pair[:, n % 2, 0:2 * KD].rearrange("p (m j) -> p m j", j=2),
                                    param(f"ada_b{l}", n * KD, n=KD).unsqueeze(2).to_broadcast([P, KD, 2]), ALU.add)\
                        .then_inc(ada_out, 1)

                for n in range(6):
                    rows(n)
                    if n:
                        biased(n - 1)
                biased(5)
                dve.wait_ge(ada_out, 6 * (l + 1))
                for q in (1, 4):
                    v.tensor_scalar(mod[:, l, q * KD:(q + 1) * KD, :], mod[:, l, q * KD:(q + 1) * KD, :], 1.0, None,
                                    ALU.add)
                leave()
                enter(dve, f"modulate{l}")
                for s in (CTX, LAT):
                    j = 1 if s == CTX else 0
                    for k in range(KD):
                        v.tensor_scalar(hT[:, k, s * T:(s + 1) * T], x[:, s, k, :], mod[:, l, KD + k, j:j + 1],
                                        mod[:, l, k, j:j + 1], ALU.mult, ALU.add)
                leave()
                project(f"project{l}", PROJECT[l])
                if l == 0:
                    heads_norm("heads_norm", [proj[:, j, :] for j in range(8)], param("q_gain"), 1.0)
                rope(l)
                attend(l)
                if l == 0:
                    pool_windows()
                else:
                    heads_norm("subln", [mixed[:, h, 0:T] for h in range(6)], param("subln"), 1.0 - LAM_INIT)
                    conformer()
                for s in ((CTX, LAT) if l == 0 else (LAT,)):
                    j = 1 if s == CTX else 0
                    enter(dve, f"out{l}{s}")
                    gated_sum(f"out{l}{s}", s, l, 2)
                    leave()
                    norm(f"norm1{l}{s}", s, l, 1, EPS1)
                    enter(dve, f"shift{l}{s}")
                    for k in range(KD):
                        v.tensor_scalar(h2[:, k, :], x[:, s, k, :], mod[:, l, 4 * KD + k, j:j + 1],
                                        mod[:, l, 3 * KD + k, j:j + 1], ALU.mult, ALU.add).then_inc(chain_v, 1)
                    chain.n += KD
                    dve.wait_ge(chain_v, chain.n)
                    split(x_split, h2)
                    leave()
                    enter(dve, f"hidden{l}{s}")
                    hidden(f"hidden{l}{s}", FH, 2, swiglu, hid)
                    gated_sum(f"hidden{l}{s}", s, l, 5)
                    leave()
                    norm(f"norm2{l}{s}", s, l, 2, EPS1)
            for l in (2, 3):
                project(f"project{l}", PROJECT[l])
                if l == 2:
                    gates()
                    mlstm()
                    mlstm_norm()
                else:
                    rglru()
                project(f"memory{l}", PROJECT_MEMORY)
                attend(l)
                enter(dve, f"out{l}{LAT}")
                plain_sum(f"out{l}{LAT}")
                leave()
                norm(f"norm1{l}{LAT}", LAT, l, 1, EPS2)
                project(f"query{l}", PROJECT_QUERY)
                choose(l)
                enter(dve, f"split{l}")
                split(x_split, x[:, LAT, :, :])
                tables()
                leave()
                for h in "ab":
                    spread(l, h)
                    enter(dve, f"hidden{l}{h}")
                    hidden(f"hidden{l}{h}", HALF, 1, weigh, coef)
                    if h == "b":
                        plain_sum(f"hidden{l}{h}")
                    leave()
                norm(f"norm2{l}{LAT}", LAT, l, 2, EPS2)


def constants():
    at, n = const_layout()
    c = np.zeros((P, n), np.float32)

    def put(name, value):
        lo, hi = at[name]
        c[:value.shape[0], lo:hi] = value.reshape(value.shape[0], -1)

    put("ident", np.eye(P))
    put("mean_d", np.full((P, P), 1.0 / D))
    put("mean_64", np.kron(np.eye(2), np.full((HD, HD), 1.0 / HD)))
    put("mean_128", np.full((P, P), 1.0 / P))
    put("mean_192", np.full((P, P), 1.0 / MDH))
    put("mean_192_half", np.kron(np.eye(2), np.ones((HD, 1)))[:, :, None] * np.full(P, 1.0 / MDH))
    put("mean_256", np.full((P, P), 1.0 / 256))
    put("ones", np.ones((P, P)))
    rot = np.zeros((P, P))
    angle_of = np.zeros(P, int)
    for f in range(P):
        axis, half, i = (f % HD) // 32, (f % 32) // 16, f % 16
        rot[f + 16 if half == 0 else f - 16, f] = -1.0 if half == 0 else 1.0
        angle_of[f] = axis * 16 + i
    put("rot", rot)
    pos = np.arange(T)
    freqs = np.float32(10000.0) ** (-np.arange(0, 32, 2, dtype=np.float32) / np.float32(32))
    ang = np.concatenate([(pos // 64).astype(np.float32)[:, None] * freqs,
                          (pos % 64).astype(np.float32)[:, None] * freqs], axis=1)
    put("cos", np.cos(ang)[:, angle_of].T)
    put("sin", np.sin(ang)[:, angle_of].T)
    inv = np.zeros((P, 2, T))
    for g, w in enumerate(WINDOWS):
        lo, hi = np.clip(pos - w // 2, 0, T), np.clip(pos + (w - 1 - w // 2) + 1, 0, T)
        inv[(g % 2) * 64:(g % 2 + 1) * 64, g // 2] = 1.0 / (hi - lo)
    put("inv_count", inv)
    put("iota", np.tile(np.arange(P), (P, 1)))
    rows = np.zeros((MH, MH, P))
    for h in range(MH):
        rows[h, h] = 1.0
    put("head_rows", rows)
    return c


def columns(v, width=P):
    v = v.reshape(-1, width).T
    return np.concatenate([v, np.zeros((P - width, v.shape[1]), v.dtype)]) if width < P else v


def by_column(w, width=P):
    k, f = w.shape
    return w.reshape(k // P, P, f // width, width).transpose(2, 1, 0, 3).reshape(f // width, P, -1)


def by_row(w, rows=P):
    return w.reshape(-1, rows, w.shape[1])


def turned(x):
    return x.T.reshape(-1, P, x.shape[0]).transpose(1, 0, 2)


def mlstm_order():
    a_ = [np.arange(h * MDH, h * MDH + P) for h in range(MH)]
    return np.concatenate(a_ + [np.arange(h * MDH + P, (h + 1) * MDH) for h in range(MH)])


def lay_out(i):
    a = {}
    a["consts"] = constants()
    at, n = param_layout()
    prm = np.zeros((P, n), np.float32)

    def put(name, value):
        lo, hi = at[name]
        prm[:value.shape[0], lo:hi] = value

    for l in range(2):
        put(f"ada_b{l}", columns(i["ada_b"][l]))
        for k in "12":
            put(f"ln{l}g{k}", columns(i[f"ln{k}_g"][l]))
            put(f"ln{l}b{k}", columns(i[f"ln{k}_b"][l]))
            put(f"ln{l + 2}g{k}", columns(i[f"ln{k}_g_2"][l]))
            put(f"ln{l + 2}b{k}", columns(i[f"ln{k}_b_2"][l]))
    put("q_gain", np.tile(i["ab_q_gain"][0], 2)[:, None])
    put("k_gain", np.tile(i["ab_k_gain"][0], 2)[:, None])
    put("pool_scale", columns(i["ab_pool_scale"][0]))
    pool_w = np.zeros((P, 2, P), np.float32)
    for g in range(4):
        lo = (g % 2) * 64
        pool_w[lo:lo + 64, g // 2, lo:lo + 64] = i["ab_w_pool"][0, g]
    put("pool_w", pool_w.reshape(P, -1))
    put("subln", columns(i["cd_subln_gain"][0]))
    put("conv_w", i["cd_conv_w"][0].reshape(CONV, 2, P).transpose(2, 1, 0).reshape(P, -1))
    put("conv_b", columns(i["cd_conv_b"][0]))
    put("conv_g", columns(i["cd_conv_ln_g"][0]))
    put("conv_bb", columns(i["cd_conv_ln_b"][0]))
    for name, src in (("lq1", "cd_lambda_q1"), ("lk1", "cd_lambda_k1"), ("lq2", "cd_lambda_q2"), ("lk2", "cd_lambda_k2")):
        put(name, np.broadcast_to(i[src][0], (P, HD)))
    order = mlstm_order()
    put("mnorm", columns(i["mlstm_norm_g_2"][0][order]))
    bg = i["mlstm_b_gates_2"][0]
    put("i_bias", bg[:MH, None])
    put("f_bias", bg[MH:, None])
    put("rconv_w", columns(i["rglru_conv_w_2"][0].reshape(-1), RB).reshape(P, RG_CONV, NRB).transpose(0, 2, 1).reshape(P, -1))
    for name, src in (("rconv_b", "rglru_conv_b_2"), ("r_ba", "rglru_b_a_2"), ("r_bx", "rglru_b_x_2"), ("r_lam", "rglru_lam_2")):
        put(name, columns(i[src][0], RB))
    a["params"] = prm
    a["x"] = turned(i["x"][0])
    a["ctx"] = turned(i["ctx"][0])
    a["mem"] = turned(i["mem_2"][0])
    a["cond"] = turned(np.stack([i["c"][0], i["c_ctx"]]))

    for l in range(2):
        a[f"ada{l}"] = i["ada_w"][l].reshape(KD, P, 6, D).transpose(2, 0, 1, 3).reshape(6 * KD, P, D)
        w = i["ffn_w_in"][l]
        a[f"ffn{l}_in"] = w.reshape(KD, P, 2, FH, P).transpose(3, 2, 1, 0, 4).reshape(2 * FH, P, D)
        a[f"ffn{l}_out"] = by_row(i["ffn_w_out"][l])
        a[f"kv{l}"] = by_column(i["xattn_w_kv_2"][l])
        a[f"pq{l}"] = by_column(i["peer_w_q_2"][l])
        a[f"subk{l}"] = i["peer_subkeys_2"][l].transpose(2, 0, 1)
        u = i["peer_u_2"][l].reshape(KEYS, KEYS, KD, P)
        a[f"peer{l}_u"] = u.transpose(1, 3, 2, 0).reshape(KEYS, P, D)
        a[f"peer{l}_v"] = i["peer_v_2"][l].reshape(KEYS, KEYS, D).transpose(1, 0, 2)
    heads = np.concatenate([np.arange(h * HD, (h + 1) * HD) for h in Q_ORDER])
    w = i["ab_w_in"][0]
    a["ab_in"] = by_column(np.concatenate([w[:, heads], w[:, 768:]], axis=1))
    w = i["ab_w_out"][0]
    a["ab_out"] = by_row(np.concatenate([w[heads], w[768:]]))
    a["cd_in"] = by_column(i["cd_w_in"][0])
    a["cd_out"] = by_row(i["cd_w_out"][0])
    w = i["mlstm_w_in_2"][0]
    W = MH * MDH
    a["ml_in"] = by_column(np.concatenate([w[:, s * W + order] for s in range(4)] + [w[:, 4 * W + 2 * MH:]], axis=1))
    a["gate_w"] = w[:, 4 * W:4 * W + 2 * MH].reshape(KD, P, 2 * MH).transpose(1, 0, 2)
    w = i["w_out_2"][0]
    a["ml_out"] = by_row(np.concatenate([w[order], w[W:]]))
    w = i["rglru_w_in_2"][0]
    a["rg_in_r"] = by_column(w[:, :2 * NRB * RB], RB)
    a["rg_in_q"] = by_column(w[:, 2 * NRB * RB:])
    a["rg_w"] = np.concatenate([i["rglru_w_a_2"][0], i["rglru_w_x_2"][0]]).transpose(1, 0, 2).reshape(RB, -1)
    w = i["w_out_2"][1]
    a["rg_out_q"] = by_row(w[NRB * RB:])
    a["rg_out_r"] = by_row(w[:NRB * RB], RB)
    return {k: np.ascontiguousarray(v) for k, v in a.items()}


def kernel(**inputs):
    import concourse.bacc as bacc
    from concourse.bass_utils import run_bass_kernel_spmd

    nc = bacc.Bacc("TRN2", target_bir_lowering=False, num_devices=1)
    arrays = {f"in_{k}": v for k, v in lay_out({k: np.asarray(v) for k, v in inputs.items()}).items()}
    aps = {k[3:]: nc.dram_tensor(k, v.shape, F32, kind="ExternalInput").ap() for k, v in arrays.items()}
    out = nc.dram_tensor("out", (P, KD, T), F32, kind="ExternalOutput").ap()
    program(nc, aps, out)
    got = run_bass_kernel_spmd(nc, [arrays], core_ids=[0]).results[0]["out"]
    return np.ascontiguousarray(got.transpose(1, 0, 2).reshape(D, T).T)[None]
```

```python
import math
from contextlib import ExitStack

import numpy as np

import concourse.bass as bass
from concourse import mybir

ALU = mybir.AluOpType
ACT = mybir.ActivationFunctionType
F32 = mybir.dt.float32
F32R = mybir.dt.float32r
BF16 = mybir.dt.bfloat16
U32 = mybir.dt.uint32
AX_X = mybir.AxisListType.X

P = 128
D = 1024
T = 256
KD = D // P
DEPTH = 2
HD = 64
FFN = 2816
FH = FFN // P
ALPHA = (2.0 * DEPTH) ** 0.25
LAM_INIT = 0.8 - 0.6 * math.exp(-0.3)
EPS1 = 1e-6
EPS2 = 1e-5
WINDOWS = (2, 4, 8, 16)
CONV = 31
CPAD = CONV // 2
RG_CONV = 4
RB = 96
NRB = 8
RG_C = 8.0
MH = 4
MDH = 192
PH = 8
KEYS = 128
TOPK = 16
NEG = -3.0e38
ROOT_MIN = 2.0 ** -115
R = 6
SPLIT = 3
PHASES = 3
CTX, LAT = 0, 1

Q_ORDER = [0, 3, 1, 4, 2, 5, 6, 9, 7, 10, 8, 11]


def const_layout():
    at, off = {}, 0
    for name, n in (("ident", P), ("mean_d", P), ("mean_64", P), ("mean_128", P), ("mean_192", P), ("mean_192_half", 2 * P), ("mean_256", P),
                    ("ones", P), ("rot", P), ("cos", T), ("sin", T), ("inv_count", 2 * T), ("iota", P),
                    ("head_rows", MH * P)):
        at[name] = (off, off + n)
        off += n
    return at, off


def param_layout():
    at, off = {}, 0
    names = [("ada_b0", 48), ("ada_b1", 48), ("q_gain", 1), ("k_gain", 1), ("pool_scale", 2), ("pool_w", 2 * P), ("subln", 1),
             ("conv_w", 2 * CONV), ("conv_b", 2), ("conv_g", 2), ("conv_bb", 2), ("lq1", HD), ("lk1", HD),
             ("lq2", HD), ("lk2", HD), ("mnorm", 6), ("i_bias", 1), ("f_bias", 1),
             ("rconv_w", NRB * RG_CONV), ("rconv_b", NRB), ("r_ba", NRB), ("r_bx", NRB), ("r_lam", NRB)]
    for n in range(4):
        names += [(f"ln{n}{k}", KD) for k in ("g1", "b1", "g2", "b2")]
    for name, n in names:
        at[name] = (off, off + n)
        off += n
    return at, off


def stage_list():
    s = [("lambda", "va")]
    for l in range(2):
        s += [(f"ada{l}", "pav" if l == 0 else "pv"), (f"modulate{l}", "av"), (f"project{l}", "pav")]
        s += [(f"attend{l}", "pavg" if l == 0 else "pav")]
        s += [("pool", "pv")] if l == 0 else [("subln", "pav")]
        for n in ((CTX, LAT) if l == 0 else (LAT,)):
            s += [(f"out{l}{n}", "pav"), (f"hidden{l}{n}", "pav")]
    for l in (2, 3):
        s += [(f"project{l}", "pav")]
        s += [("mlstm", "pavg"), ("mlstm_norm", "pav")] if l == 2 else [("rglru", "pav")]
        s += [(f"attend{l}", "pav"), (f"out{l}{LAT}", "pav"),
              (f"query{l}", "pavg"), (f"tables{l}", "v"), (f"spread{l}a", "pavg"),
              (f"hidden{l}a", "pav"), (f"spread{l}b", "pavg"), (f"hidden{l}b", "pav")]
    return s


STAGES = stage_list()


def stages_of(engine, before):
    n = 0
    for name, engines in STAGES:
        if name == before:
            return n
        n += engine in engines
    raise KeyError(before)


FEATURES, TOKENS = "features", "tokens"
PROJECT = {
    0: [(0, 8, 0, 2 * T, FEATURES, P), (8, 2, 0, 2 * T, TOKENS, P), (10, 2, 0, 2 * T, FEATURES, P)],
    1: [(18, 4, T, T, FEATURES, P), (0, 6, T, T, FEATURES, P), (6, 6, 0, 2 * T, FEATURES, P),
        (12, 6, 0, 2 * T, TOKENS, P)],
    2: [(0, 12, 0, T, FEATURES, P), (12, 6, 0, T, TOKENS, P), (18, 8, 0, T, FEATURES, P)],
    3: [(NRB, NRB, 0, T, FEATURES, RB), (0, NRB, 0, T, FEATURES, RB), (24, 2, 0, T, FEATURES, P)],
}
GLU = 4
PROJECT_MEMORY = [(0, 2, 0, T, FEATURES, P), (0, 2, 0, T, TOKENS, P)]
ROPE = {0: [(j, T) for j in range(8)], 1: [(j, 0) for j in range(6)] + [(j, T) for j in range(6, 12)]}



def project_tiles(l):
    return [(first + m, t0, nt, form) for first, n, t0, nt, form, _ in PROJECT[l] for m in range(n)]


HIDDEN = {"ffn": (FH, 2), "peer": (KEYS // 2, 1)}
WEIGHTS = [("ada0", "ada0", 48), ("project0", "ab_in", 12),
           ("out00", "ab_out", 8), ("hidden00", "ffn0", 0), ("out01", "ab_out", 8), ("hidden01", "ffn0", 0),
           ("ada1", "ada1", 48), ("project1", "cd_in", 22), ("out11", "cd_out", 8), ("hidden11", "ffn1", 0),
           ("project2", "ml_in", 26), ("project2", "kv0", 4), ("out21", "ml_out", 8), ("query2", "pq0", 16),
           ("hidden2a", "peer0a", 0), ("hidden2b", "peer0b", 0),
           ("project3", "rg_in_r", 16), ("project3", "rg_in_q", 2), ("project3", "kv1", 4),
           ("out31", "rg_out_q", 2), ("out31", "rg_out_r", NRB), ("query3", "pq1", 16),
           ("hidden3a", "peer1a", 0), ("hidden3b", "peer1b", 0)]


def blocks_of(tensor, n):
    if n:
        return n
    tiles, unit = HIDDEN[tensor.rstrip("01ab")]
    return tiles * (unit + 1)


def first_block(stage):
    total = 0
    for name, tensor, n in WEIGHTS:
        if name == stage:
            return total
        total += blocks_of(tensor, n)
    raise KeyError(stage)


def blocks_in(stage):
    return sum(blocks_of(tensor, n) for name, tensor, n in WEIGHTS if name == stage)


def after_input(stage, t, unit):
    if isinstance(t, int) and t < 2:
        return first_block(stage) + (t + 1) * unit
    return t * (unit + 1) + (first_block(stage) + unit - 2)


def after_output(stage, t, unit):
    return t * (unit + 1) + (first_block(stage) + 3 * unit + 1)


def split_before(stage):
    total = 0
    for name, tensor, n in WEIGHTS:
        if name == stage:
            return total
        total += 0 if n else blocks_of(tensor, n)
    raise KeyError(stage)


class Chain:

    def __init__(self, eng, sem):
        self.eng, self.sem, self.n = eng, sem, 0

    def __call__(self, ins):
        self.n += 1
        ins.then_inc(self.sem, 1)
        self.eng.wait_ge(self.sem, self.n)


class RingPlace:

    def __init__(self):
        self.at = 0

    def steps(self, eng, n, unit, step, phases=2):
        per = math.lcm(R // math.gcd(R, unit), phases)
        if self.at == 0 and n > per:
            self.steps(eng, per, unit, step, phases)
            self.steps(eng, n - per, unit, lambda i, par, b: step(i + per, par, b), phases)
            return
        turns = n // per
        if turns < 2:
            turns = 0
        base = self.at

        def blocks(k, it):
            out = []
            for b in range(unit):
                s = base + k * unit + b
                out.append((s % R, s // R + it * (per * unit // R), s + it * (per * unit), s % SPLIT))
            return out

        if turns:
            with eng.Fori(0, turns) as it:
                for k in range(per):
                    step(it * per + k, k % phases, blocks(k, it))
        for i in range(turns * per, n):
            step(i, i % phases, blocks(i, 0))
        self.at += n * unit


def program(nc, a, out):
    ctx = ExitStack()
    with ctx:
        def sb(name, shape, dt=F32):
            return ctx.enter_context(nc.sbuf_tensor(name, shape, dt))

        def sem(name):
            return ctx.enter_context(nc.semaphore(name))

        C_AT, C_N = const_layout()
        Q_AT, Q_N = param_layout()
        ring = sb("ring", [P, R, D])
        consts = sb("consts", [P, C_N])
        params = sb("params", [P, Q_N])
        x = sb("x", [P, 2, KD, T])
        res = sb("res", [P, KD, T])
        mod = sb("mod", [P, 2, 48, 2])
        cond = sb("cond", [P, 2, KD, 2])
        gate_w = sb("gate_w", [P, KD, 2 * MH])
        subk = sb("subk", [P, 2, KEYS])
        cols = sb("cols", [P, 128])
        neg_lam = sb("neg_lam", [P, 1])
        eps_col = sb("eps_col", [P, 2])
        arena = sb("arena", [P, 24064])
        w_split = sb("w_split", [P, SPLIT, 2, D], F32R)
        x_split = sb("x_split", [P, 2, KD, T], F32R)
        h_split = sb("h_split", [P, PHASES, 2, T], F32R)
        ps = ctx.enter_context(nc.psum_tensor("ps", [P, 8, 512], F32))
        wide = ps[:, 0:4, :].rearrange("p b (c n) -> p (b c) n", c=2)
        pair = ps[:, 4:6, :]
        single = ps[:, 6:8, :]

        def const(name, rows=P, lo_row=0):
            lo, hi = C_AT[name]
            return consts[lo_row:lo_row + rows, lo:hi]

        def param(name, i=0, rows=P, n=1):
            lo = Q_AT[name][0] + i
            return params[0:rows, lo:lo + n]

        def part(off, *dims):
            v = arena[:, off:off + int(np.prod(dims))]
            if len(dims) == 2:
                v = v.rearrange("p (a b) -> p a b", a=dims[0])
            elif len(dims) == 3:
                v = v.rearrange("p (a b c) -> p a b c", a=dims[0], b=dims[1])
            return v

        def over(v, n):
            return v.unsqueeze(1).to_broadcast([v.shape[0], n, v.shape[1]])

        PROJ, MIXED, WORK = 0, 13312, 18432
        proj = part(PROJ, 26, 512)
        mixed = part(MIXED, 10, 512)
        hT = part(MIXED, KD, 2 * T)
        work = part(WORK, 5632)
        MEM_K, MEM_V = PROJ + 24 * 512, MIXED + 8 * 512
        mem_k, mem_v = part(MEM_K, 2, 512), part(MEM_V, 2, 512)
        windows = part(6144, 10 * (T + 32) + 4 * T)
        glu_gate = part(11264, 2, T)
        conved = part(11776, 2, T)
        squares = glu_gate
        conv_in = part(12288, 2, T + 2 * CPAD)
        probs = part(WORK, 2, 2, 512)
        probsT = part(WORK + 2048, 2, 1024)
        diag = part(WORK + 4096, 4, P)
        h2 = part(0, KD, T)
        gate = part(2048, PHASES, T)
        hid = part(2048 + PHASES * T, PHASES, T)
        HALF = KEYS // 2
        G = part(0, T, HALF)
        chosen = res[:, 0:3, :]
        spare = x[:, CTX, :, :]
        small = part(WORK, 5632).bitcast(BF16)
        GROUP = 512 // HALF
        hot_i = small[:, 0:2 * GROUP * KEYS].rearrange("p (b n t) -> p b n t", b=2, t=GROUP)
        at = 2 * GROUP * KEYS
        hot_j = small[:, at:at + 2 * GROUP * HALF].rearrange("p (b n t) -> p b n t", b=2, t=GROUP)
        at += 2 * GROUP * HALF
        hot_w = small[:, at:at + 6 * GROUP * HALF].rearrange("p (b c n t) -> p b c n t", b=2, t=GROUP, c=3)
        at += 6 * GROUP * HALF
        keys = small[:, at:at + 2 * T].rearrange("p (i t) -> p i t", i=2)
        at += 2 * T
        weight3 = small[:, at:at + 3 * T].rearrange("p (c t) -> p c t", c=3)
        at += 3 * T
        places = small[:, at:at + GROUP * KEYS].rearrange("p (n t) -> p n t", t=GROUP)
        gelu = spare[:, 0:PHASES, :]
        coef = spare[:, PHASES:2 * PHASES, :]

        best = part(8192, 2 * PH, 2, TOPK)
        best_key = part(8704, 2 * PH, 2, TOPK).bitcast(U32)
        best_key_f = part(9216, 2 * PH, 2, TOPK)
        cand = part(9728, 2, 2, TOPK * TOPK)
        rest = part(10752, 2, TOPK * TOPK)
        top = part(11264, PH, 2, TOPK)
        top_at = part(11520, PH, 2, TOPK).bitcast(U32)
        half_at = [part(11776 + i * 256, PH, 2, TOPK).bitcast(U32) for i in range(2)]
        half_at_f = [part(12288 + i * 256, PH, 2, TOPK) for i in range(2)]
        picked = part(12800, PH * 4, TOPK, TOPK)
        picks = part(20992, 3, 2, P)
        top_w = part(21760, 2, P)
        top_sum = part(22016, 2, PH)
        rest_sums = part(22032, 2, TOPK * TOPK)

        stage = {e: sem(f"{n}_stages") for e, n in (("p", "tensor"), ("a", "scalar"), ("v", "vector"), ("g", "gpsimd"))}
        loaded = sem("loaded")
        filled = [sem(f"slot{i}_filled") for i in range(R)]
        block_used = sem("block_used")
        mem_loaded, subk_loaded, rg_loaded = sem("mem_loaded"), sem("subkeys_loaded"), sem("rg_loaded")
        tile_out = [sem("even_tile_out"), sem("odd_tile_out")]
        early_out = sem("early_tile_out")
        chain_a, chain_v = sem("scalar_chain"), sem("vector_chain")
        silu_done, ada_out = sem("silu_done"), sem("ada_out")
        squared, mean_ready, normed, turned_pos, roped = (sem(n) for n in (
            "squared", "mean_ready", "normed", "partner_ready", "roped"))
        s_ready, m_ready, e_ready, d_ready, t_ready, pt_ready, o_ready, o_out = (sem(n) for n in (
            "scores_ready", "max_ready", "exp_ready", "diag_ready", "turned", "turned_out", "heads_ready", "heads_out"))
        sum_ready = sem("sum_ready")
        res_ready, ln_mean, ln_centred, ln_squared, ln_var, ln_scaled, ln_x, x_high = (sem(n) for n in (
            "res_ready", "ln_mean", "ln_centred", "ln_squared", "ln_var", "ln_scaled", "ln_x", "x_high"))
        w_high, w_low = sem("weights_high"), sem("weights_low")
        gate_ready, hid_made, hid_high, hid_ready = (sem(n) for n in ("gate_ready", "hid_made", "hid_high", "hid_ready"))
        lam_sum, lam_exp = sem("lam_sum"), sem("lam_exp")
        pool_out = sem("pool_mixed")
        chain_g = sem("gpsimd_chain")
        conv_v, conv_a, conv_p = sem("conv_v"), sem("conv_a"), sem("conv_p")
        gates_p, gates_a, gates_v = sem("gates_p"), sem("gates_a"), sem("gates_v")
        m_cast, m_weight, m_mask, m_score, m_st, m_sum, m_head = (sem(n) for n in (
            "m_broadcast", "m_weights", "m_masked", "m_scores", "m_weighted", "m_summed", "m_divided"))
        mn_v, mn_p, mn_a = sem("mnorm_v"), sem("mnorm_p"), sem("mnorm_a")
        rg_v, rg_a, rg_p = sem("rglru_v"), sem("rglru_a"), sem("rglru_p")
        q_kept, k_score, k_best, k_cand, k_place, k_product, k_shift, k_exp, k_pick, k_turn, k_keep = (
            sem(n) for n in (
                "query_kept", "keys_scored", "best_of_half", "candidates_ready", "places_ready", "picked_products",
                "picks_shifted", "picks_exp", "picks_ready", "picks_turned", "picks_kept"))
        hot_ready = [sem("hot_ready0"), sem("hot_ready1")]
        hot_w_ready = [sem("hot_w_ready0"), sem("hot_w_ready1")]
        hot_j_made = sem("hot_j_made")
        ada_rows, ada_turned = sem("ada_rows"), sem("ada_turned")
        g_ready = [sem("g_ready0"), sem("g_ready1")]
        g_kept = [sem("g_kept0"), sem("g_kept1")]
        rooted = sem("rooted")
        stored = sem("stored")

        def enter(eng, name):
            for e in "pavg":
                n = stages_of(e, name)
                if n:
                    eng.wait_ge(stage[e], n)

        def units_of(l):
            units = []
            if l == 0:
                for s in (CTX, LAT):
                    for n, head in enumerate(Q_ORDER):
                        j, half, kv = n // 2, n % 2, head // 3
                        assert half == kv % 2
                        rows = slice(half * HD, (half + 1) * HD)
                        units.append(dict(
                            nk=T if s == CTX else 2 * T, diff=False, rows=(half * HD, HD),
                            q=[proj[rows, j, s * T + r * P:s * T + (r + 1) * P] for r in range(2)],
                            k=[proj[rows, 6 + kv // 2, 0:T if s == CTX else 2 * T]] * 2,
                            v=lambda c, kv=kv: proj[:, 8 + kv // 2, c * P + (kv % 2) * HD:c * P + (kv % 2 + 1) * HD],
                            out=mixed[rows, j, s * T:(s + 1) * T]))
            elif l == 1:
                for h in range(6):
                    for t in range(2):
                        units.append(dict(
                            nk=2 * T, diff=True, rows=(0, P),
                            q=[proj[r * HD:(r + 1) * HD, h, t * P:(t + 1) * P] for r in range(2)],
                            k=[proj[r * HD:(r + 1) * HD, 6 + h, :] for r in range(2)],
                            v=lambda c, h=h: proj[:, 12 + h, c * P:(c + 1) * P],
                            out=mixed[:, h, t * P:(t + 1) * P]))
            else:
                for h in range(4):
                    j, half = h // 2, h % 2
                    rows = slice(half * HD, (half + 1) * HD)
                    units.append(dict(
                        nk=T, diff=False, rows=(half * HD, HD),
                        q=[proj[rows, 24 + j, r * P:(r + 1) * P] for r in range(2)],
                        k=[mem_k[rows, j, T:2 * T]] * 2,
                        v=lambda c, j=j, half=half: mem_v[:, j, T + c * P + half * HD:T + c * P + (half + 1) * HD],
                        out=mixed[rows, (6 if l == 2 else 8) + j, 0:T]))
            return units

        def scores_at(i, nk):
            return ps[:, 2 * (i % 2):2 * (i % 2) + 2, 0:nk]

        def m_tiles(h, first):
            half = slice((h % 2) * HD, (h % 2 + 1) * HD)
            return [(slice(0, P), first + h), (half, first + 4 + h // 2)]

        def rg_tiles():
            return [proj[0:RB, 0:8, T:2 * T], proj[0:RB, 8:16, T:2 * T], proj[0:RB, 16:24, 0:T],
                    proj[0:RB, 16:24, T:2 * T], mixed[0:RB, 0:8, T:2 * T]]

        block = ctx.enter_context(nc.Block())

        @block.sync
        def _(sp):
            for dst, src in ((cond[:, 0, :, :], a["cond"]), (x[:, CTX, :, :], a["ctx"]), (x[:, LAT, :, :], a["x"]),
                             (params[:, :], a["params"]), (consts[:, :], a["consts"]), (gate_w[:, :, :], a["gate_w"])):
                sp.dma_start(dst, src).then_inc(loaded, 16)
            place = RingPlace()

            def fetch(t, i, blk):
                slot, _, seq, _ = blk
                src = t[i, :, :] if isinstance(i, int) else t[bass.ds(i, 1), :, :].rearrange("o p n -> (o p) n")
                if not isinstance(seq, int) or seq >= R:
                    sp.wait_ge(block_used, seq - (R - 1))
                sp.dma_start(ring[0:t.shape[1], slot, 0:t.shape[2]], src).then_inc(filled[slot], 16)

            def stream(t, n):
                place.steps(sp, n, 1, lambda i, par, b: fetch(t, i, b[0]))

            def stream_hidden(w_in, w_out, t0, n, unit):
                def one(i, par, b):
                    for j in range(unit):
                        fetch(w_in, (i + (2 + t0)) * unit + j, b[j])
                    fetch(w_out, i + t0, b[unit])
                place.steps(sp, 2 * unit, 1, lambda i, par, b: fetch(w_in, i + t0 * unit, b[0]))
                place.steps(sp, n - 2, unit + 1, one)
                place.steps(sp, 2, 1, lambda i, par, b: fetch(w_out, i + (t0 + n - 2), b[0]))

            for _, name, n in WEIGHTS:
                if n:
                    stream(a[name], n)
                elif name.startswith("ffn"):
                    stream_hidden(a[name + "_in"], a[name + "_out"], 0, FH, 2)
                else:
                    stream_hidden(a[name[:-1] + "_u"], a[name[:-1] + "_v"], HALF * (name[-1] == "b"), HALF, 1)

        @block.gpsimd
        def _(pool):
            chain = Chain(pool, chain_g)
            g_ = nc.gpsimd

            def pool_windows():
                enter(pool, "attend0")
                W = T + 32
                U, S2, S4, S8, S16 = (windows[:, i * 2 * W:(i + 1) * 2 * W].rearrange("p (n t) -> p n t", n=2)
                                      for i in range(5))
                chain(g_.memset(windows[:, 0:10 * W], 0.0))
                for s in range(2):
                    chain(g_.tensor_copy(U[:, :, 16:16 + T], proj[:, 10:12, s * T:(s + 1) * T]))
                    chain(g_.tensor_tensor(S2[:, :, 1:W], U[:, :, 0:W - 1], U[:, :, 1:W], ALU.add))
                    chain(g_.tensor_tensor(S4[:, :, 2:W - 1], S2[:, :, 1:W - 2], S2[:, :, 3:W], ALU.add))
                    chain(g_.tensor_tensor(S8[:, :, 4:W - 3], S4[:, :, 2:W - 5], S4[:, :, 6:W - 1], ALU.add))
                    chain(g_.tensor_tensor(S16[:, :, 8:W - 7], S8[:, :, 4:W - 11], S8[:, :, 12:W - 3], ALU.add))
                    pooled = windows[:, 10 * W + 2 * s * T:10 * W + 2 * (s + 1) * T].rearrange("p (n t) -> p n t", n=2)
                    inv = const("inv_count").rearrange("p (n t) -> p n t", n=2)
                    for g, S in enumerate((S2, S4, S8, S16)):
                        rows, n = slice((g % 2) * 64, (g % 2 + 1) * 64), g // 2
                        last = g_.tensor_tensor(pooled[rows, n, :], S[rows, n, 16:16 + T], inv[rows, n, :], ALU.mult)
                    chain(last)
                    chain(g_.tensor_tensor(pooled, pooled, U[:, :, 16:16 + T], ALU.subtract))
                pool.drain().then_inc(stage["g"], 1)

            pool_windows()
            def causal():
                enter(pool, "mlstm")
                for h in range(MH):
                    for c in range(2):
                        pool.wait_ge(m_weight, 3 * h + c + 1)
                        w = work[:, (2 * (h % 2) + c) * T:(2 * (h % 2) + c + 1) * T]
                        nc.gpsimd.affine_select(out=w, in_=w, compare_op=ALU.is_ge, fill=0.0, base=-P * c,
                                                pattern=[[1, T]], channel_multiplier=-1).then_inc(m_mask, 1)
                pool.drain().then_inc(stage["g"], 1)

            def rows_of_j(l, h):
                enter(pool, f"spread{l}{h}")
                base = (2 * (l - 2) + (h == "b")) * (T // (2 * GROUP))

                def one(it):
                    for b in range(2):
                        at = bass.ds(it * (2 * GROUP) + b * GROUP, GROUP)
                        pool.wait_ge(hot_j_made, it * 2 + (2 * base + b + 1))
                        if not isinstance(it, int) or it + base:
                            pool.wait_ge(g_ready[b], it + base)
                        nc.gpsimd.tensor_tensor(hot_w[:, b, 2], hot_j[:, b],
                                                over(weight3[:, 2, at], HALF),
                                                ALU.mult).then_inc(hot_w_ready[b], 1)
                one(0)
                with pool.Fori(1, T // (2 * GROUP)) as it:
                    one(it)
                pool.drain().then_inc(stage["g"], 1)

            def choose(l):
                enter(pool, f"query{l}")
                base = PH * (l - 2)
                t_ = nc.gpsimd.tensor_tensor
                grid = [P, TOPK, TOPK]

                def sums(h):
                    pool.wait_ge(k_best, base + h + 1)
                    if h >= 2:
                        pool.wait_ge(k_place, base + h - 1)
                    for t in range(2):
                        last = t_(cand[:, h % 2, t, :].rearrange("p (a b) -> p a b", a=TOPK),
                                  best[:, 2 * h, t, :].unsqueeze(2).to_broadcast(grid),
                                  best[:, 2 * h + 1, t, :].unsqueeze(1).to_broadcast(grid), ALU.add)
                    last.then_inc(k_cand, 1)

                def products(h):
                    pool.wait_ge(k_place, base + h + 1)
                    for t in range(2):
                        for i in range(2):
                            rows = picked[:, 4 * h + 2 * i + t]
                            last = t_(rows, rows, over(best_key_f[:, 2 * h + i, t, :], TOPK), ALU.mult)
                    last.then_inc(k_product, 1)

                for h in range(PH):
                    sums(h)
                    if h:
                        products(h - 1)
                products(PH - 1)
                pool.drain().then_inc(stage["g"], 1)

            for l in (2, 3):
                if l == 3:
                    enter(pool, "project3")
                    pool.dma_start(work[0:RB, 2560:2560 + 2 * NRB * RB], a["rg_w"]).then_inc(rg_loaded, 16)
                enter(pool, f"project{l}")
                pool.dma_start(res[:, :, :], a["mem"]).then_inc(mem_loaded, 16)
                pool.dma_start(subk[:, :, :], a[f"subk{l - 2}"]).then_inc(subk_loaded, 16)
                if l == 2:
                    causal()
                choose(l)
                for h in "ab":
                    rows_of_j(l, h)
            for e in "pav":
                pool.wait_ge(stage[e], stages_of(e, "hidden3b") + 1)
            pool.dma_start(out, x[:, LAT, :, :]).then_inc(stored, 16)
            pool.wait_ge(stored, 16)

        @block.tensor
        def _(pe):
            place = RingPlace()
            n_out = [0, 0]
            n_unit, n_ln, n_hid, n_mean = [0], [0], [0], [0]
            mm = nc.tensor.matmul

            def leave():
                pe.drain().then_inc(stage["p"], 1)

            def wait_filled(blk):
                slot, turn, _, _ = blk
                pe.wait_ge(filled[slot], (turn + 1) * 16)

            def ada(l):
                enter(pe, f"ada{l}")
                pe.wait_ge(loaded, 16 * 6)
                pe.wait_ge(silu_done, 1)

                def turn(n):
                    pe.wait_ge(ada_rows, 6 * l + n + 1)
                    if n >= 2:
                        pe.wait_ge(ada_out, 6 * l + n - 1)
                    for m in range(KD):
                        last = mm(pair[:, n % 2, 2 * m:2 * m + 2],
                                  work[0:2, (n % 2) * D + m * P:(n % 2) * D + (m + 1) * P], const("ident", 2)[:, 0:2],
                                  start=True, stop=True)
                    last.then_inc(ada_turned, 1)

                def one(n, par, b):
                    for k in range(KD):
                        wait_filled(b[k])
                        for c in range(2):
                            last = mm(ps[0:2, 2 * par + c, :], cond[:, 1, k, :],
                                      ring[:, b[k][0], c * 512:(c + 1) * 512], start=(k == 0), stop=(k == KD - 1))
                        last.then_inc(block_used, 1)
                    if n:
                        turn(n - 1)
                place.steps(pe, 6, KD, one)
                turn(5)
                leave()

            def project(src, runs):
                for _, n, t0, nt, form, width in runs:
                    def one(m, par, b):
                        wait_filled(b[0])
                        if isinstance(m, int):
                            if n_out[par] + m // 2:
                                pe.wait_ge(tile_out[par], n_out[par] + m // 2)
                        else:
                            pe.wait_ge(tile_out[par], m // 2 + n_out[par])
                        w = ring[:, b[0][0], 0:KD * width].rearrange("p (k c) -> p k c", k=KD)
                        if form == FEATURES:
                            for k in range(KD):
                                last = mm(pair[0:width, par, 0:nt], w[:, k, :], src[:, k, t0:t0 + nt],
                                          start=(k == 0), stop=(k == KD - 1))
                        else:
                            for t in range(nt // P):
                                for k in range(KD):
                                    last = mm(pair[:, par, t * P:(t + 1) * P],
                                              src[:, k, t0 + t * P:t0 + (t + 1) * P], w[:, k, :],
                                              start=(k == 0), stop=(k == KD - 1))
                        last.then_inc(block_used, 1)

                    place.steps(pe, n, 1, one)
                    n_out[0] += (n + 1) // 2
                    n_out[1] += n // 2

            def means(name, ones, n, tiles):
                enter(pe, name)
                for i in range(tiles):
                    pe.wait_ge(squared, n_mean[0] + i + 1)
                    if n_mean[0] + i >= 2:
                        pe.wait_ge(normed, n_mean[0] + i - 1)
                    mm(pair[:, i % 2, 0:n], const(ones), work[:, (i % 2) * 512:(i % 2) * 512 + n],
                       start=True, stop=True).then_inc(mean_ready, 1)
                n_mean[0] += tiles
                leave()

            def project_early(l):
                enter(pe, f"project{l}")
                tiles = project_tiles(l)
                out0, rope0 = len(project_tiles(0)) * l, len(ROPE[0]) * l

                def product(n, b):
                    _, t0, nt, form = tiles[n]
                    wait_filled(b)
                    if n >= 2:
                        pe.wait_ge(early_out, out0 + n - 1)
                    w = ring[:, b[0], :].rearrange("p (k c) -> p k c", k=KD)
                    for t in range(1 if form == FEATURES else nt // P):
                        for k in range(KD):
                            if form == FEATURES:
                                last = mm(pair[:, n % 2, 0:nt], w[:, k, :], hT[:, k, t0:t0 + nt],
                                          start=(k == 0), stop=(k == KD - 1))
                            else:
                                last = mm(pair[:, n % 2, t * P:(t + 1) * P],
                                          hT[:, k, t0 + t * P:t0 + (t + 1) * P], w[:, k, :],
                                          start=(k == 0), stop=(k == KD - 1))
                    last.then_inc(block_used, 1)

                def mean(i):
                    pe.wait_ge(squared, i + 1)
                    if i >= 2:
                        pe.wait_ge(normed, i - 1)
                    mm(single[:, i % 2, :], const("mean_64"), work[:, (i % 2) * 512:(i % 2 + 1) * 512],
                       start=True, stop=True).then_inc(mean_ready, 1)

                def partner(i):
                    j, lat = ROPE[l][i]
                    if l == 0:
                        pe.wait_ge(normed, i + 1)
                    else:
                        pe.wait_ge(early_out, out0 + GLU + i + 1)
                    if rope0 + i >= 2:
                        pe.wait_ge(roped, rope0 + i - 1)
                    mm(ps[:, i % 2, 0:T], const("rot"), proj[:, j, lat:lat + T],
                       start=True, stop=True).then_inc(turned_pos, 1)

                def conv_mean(i):
                    pe.wait_ge(conv_v if i == 0 else conv_a, 1 if i == 0 else 2)
                    for k in range(2):
                        last = mm(ps[:, 2 + i, 0:T], const("mean_256"), (squares if i else conved)[:, k, :],
                                  start=(k == 0), stop=(k == 1))
                    last.then_inc(conv_p, 1)

                for n in range(len(tiles)):
                    place.steps(pe, 1, 1, lambda _, par, b: product(n, b[0]))
                    if l == 1 and n >= len(tiles) - 4 and n < len(tiles) - 2:
                        conv_mean(n - (len(tiles) - 4))
                    if l == 0 and 0 <= n - 1 < len(ROPE[0]):
                        mean(n - 1)
                    i = n - 2 if l == 0 else n - 1 - GLU
                    if 0 <= i < len(ROPE[l]):
                        partner(i)
                if l == 0:
                    n_mean[0] += len(ROPE[0])
                leave()

            def attend(l):
                units = units_of(l)
                enter(pe, f"attend{l}")
                base = n_unit[0]

                def scores(i):
                    u = units[i]
                    if base + i >= 2:
                        pe.wait_ge(e_ready, base + i - 1)
                    for r in range(2):
                        last = mm(scores_at(i, u["nk"])[:, r, :], u["q"][r], u["k"][r], start=True, stop=True)
                    last.then_inc(s_ready, 1)

                def turn(i):
                    u = units[i]
                    pe.wait_ge(d_ready, base + i + 1)
                    if base + i:
                        pe.wait_ge(pt_ready, base + i)
                    for c in range(u["nk"] // P):
                        for r in range(2):
                            e = probs[:, i % 2, r, c * P:(c + 1) * P]
                            dg = diag[:, 2 * (i % 2) + r, :]
                            if u["diff"]:
                                last = mm(pair[:, 0, c * P:(c + 1) * P], e, dg, start=(r == 0), stop=(r == 1))
                            else:
                                at = (c % 2) * T + r * P
                                last = mm(pair[:, c // 2, at:at + P], e, dg, start=True, stop=True)
                    last.then_inc(t_ready, 1)

                def heads(i):
                    u = units[i]
                    pe.wait_ge(pt_ready, base + i + 1)
                    if base + i >= 2:
                        pe.wait_ge(o_out, base + i - 1)
                    nq = P if u["diff"] else 2 * P
                    lo, m = u["rows"]
                    chunks = u["nk"] // P
                    for c in range(chunks):
                        last = mm(single[lo:lo + m, i % 2, 0:nq], u["v"](c), probsT[:, i % 2, c * nq:(c + 1) * nq],
                                  start=(c == 0), stop=(c == chunks - 1))
                    last.then_inc(o_ready, 1)

                n = len(units)
                scores(0)
                for i in range(n):
                    if i + 1 < n:
                        scores(i + 1)
                    if i:
                        heads(i - 1)
                    turn(i)
                heads(n - 1)
                n_unit[0] += n
                leave()

            def accumulate(rhs, blk, rows, first, final):
                for m in range(KD):
                    last = mm(wide[:, m, :], ring[0:rows, blk[0], m * P:(m + 1) * P], rhs,
                              start=(first and m % 2 == 0), stop=final, skip_group_check=True)
                    if final and m % 2 and m < KD - 1:
                        last.then_inc(sum_ready, 1)
                return last

            def passes(dst, w, at, rhs, first, final, shared=False):
                for i, (wp, rp) in enumerate(((0, 0), (0, 1), (1, 0))):
                    last = mm(dst, w_split[:, w, wp, at:at + P], rhs[rp], start=(first and i == 0),
                              stop=(final and i == 2), skip_group_check=shared)
                return last

            def out_project(name, tiles):
                enter(pe, name)

                def one(i, par, b):
                    rhs, rows = tiles[i]
                    wait_filled(b[0])
                    last = accumulate(rhs, b[0], rows, i == 0, i == len(tiles) - 1)
                    last.then_inc(block_used, 1)
                for i in range(len(tiles)):
                    place.steps(pe, 1, 1, lambda _, par, b: one(i, par, b))
                norm()
                leave()

            def norm():
                for k in range(KD):
                    pe.wait_ge(res_ready, KD * n_ln[0] + k + 1)
                    last = mm(pair[:, 0, 0:T], const("mean_d"), res[:, k, :], start=(k == 0), stop=(k == KD - 1))
                last.then_inc(ln_mean, 1)
                for k in range(KD):
                    pe.wait_ge(ln_squared, 4 * n_ln[0] + k // 2 + 1)
                    last = mm(pair[:, 1, 0:T], const("mean_d"), work[:, k * T:(k + 1) * T],
                              start=(k == 0), stop=(k == KD - 1))
                last.then_inc(ln_var, 1)
                n_ln[0] += 1

            def hidden(name, n, unit, opens=True, ends=True):
                enter(pe, name)
                base, w_base = n_hid[0], split_before(name) - first_block(name)

                def go_in(t, ph, blks):
                    if not isinstance(t, int) or t >= PHASES:
                        pe.wait_ge(hid_ready, t + (base - 2))
                    for j, b in enumerate(blks):
                        pe.wait_ge(w_low, b[2] + (w_base + 1))
                        for k in range(KD):
                            last = passes(ps[:, 4 + ph, j * T:(j + 1) * T], b[3], k * P,
                                          [x_split[:, i, k, :] for i in range(2)], k == 0, k == KD - 1)
                        last.then_inc(block_used, 1)

                def go_out(t, ph, b, first=False, final=False):
                    pe.wait_ge(hid_ready, t + (base + 1))
                    pe.wait_ge(w_low, b[2] + (w_base + 1))
                    for m in range(KD):
                        last = passes(wide[:, m, :], b[3], m * P, [h_split[:, ph, i, :] for i in range(2)],
                                      first and m % 2 == 0, final, shared=True)
                        if final and ends and m % 2 and m < KD - 1:
                            last.then_inc(sum_ready, 1)
                    last.then_inc(block_used, 1)

                def both(i, ph, b, first=False):
                    go_in(i + 2, (ph + 2) % PHASES, b[0:unit])
                    go_out(i, ph, b[unit], first)

                for t in range(2):
                    place.steps(pe, 1, unit, lambda _, ph, b, t=t: go_in(t, t, b))
                place.steps(pe, 1, unit + 1, lambda i, ph, b: both(0, 0, b, first=opens))
                place.steps(pe, n - 3, unit + 1, lambda i, ph, b: both(i + 1, (ph + 1) % PHASES, b), PHASES)
                for t in (n - 2, n - 1):
                    place.steps(pe, 1, 1, lambda _, ph, b, t=t: go_out(t, t % PHASES, b[0], final=(t == n - 1)))
                n_hid[0] += n
                if ends:
                    norm()
                leave()

            def pool_mix():
                enter(pe, "pool")
                for s in range(2):
                    for n in range(2):
                        at = 10 * (T + 32) + (2 * s + n) * T
                        last = mm(ps[:, 4 + 2 * s + n, 0:T], param("pool_w", n * P, n=P), windows[:, at:at + T],
                                  start=True, stop=True)
                    last.then_inc(pool_out, 1)
                leave()

            def gates():
                for g in range(2):
                    for k in range(KD):
                        last = mm(ps[0:MH, g, 0:T], gate_w[:, k, g * MH:(g + 1) * MH], x[:, LAT, k, :],
                                  start=(k == 0), stop=(k == KD - 1))
                last.then_inc(gates_p, 1)

            def gate_columns():
                pe.wait_ge(gates_v, 2)
                for c in range(2):
                    last = mm(single[:, 0, c * MH:(c + 1) * MH], work[0:MH, 2048 + c * P:2048 + (c + 1) * P],
                              const("ident", MH)[:, 0:MH], start=True, stop=True)
                last.then_inc(gates_p, 1)

            def mlstm():
                enter(pe, "mlstm")

                def spread_rows(h):
                    if h >= 2:
                        pe.wait_ge(m_weight, 3 * (h - 1))
                    for i, at in enumerate((2304, 2560)):
                        last = mm(pair[:, h % 2, i * T:(i + 1) * T], const("head_rows", MH)[:, h * P:(h + 1) * P],
                                  work[0:MH, at:at + T], start=True, stop=True)
                    last.then_inc(m_cast, 1)

                def score(h):
                    if h >= 2:
                        pe.wait_ge(m_st, h - 1)
                    for c in range(2):
                        for i, ((rows, kt), (_, qt)) in enumerate(zip(m_tiles(h, 6), m_tiles(h, 0))):
                            last = mm(wide[:, 4 * (h % 2) + c, :], proj[rows, kt, c * P:(c + 1) * P],
                                      proj[rows, qt, 0:T], start=(i == 0), stop=(i == 1))
                    last.then_inc(m_score, 1)

                def sums(h):
                    pe.wait_ge(m_st, h + 1)
                    if h >= 2:
                        pe.wait_ge(m_head, h - 1)
                    (_, ta), (half, tb) = m_tiles(h, 12)
                    w = [work[:, (2 * (h % 2) + c) * T:(2 * (h % 2) + c + 1) * T] for c in range(2)]
                    for c in range(2):
                        mm(wide[:, 4 * (h % 2) + 2, :], proj[:, ta, c * P:(c + 1) * P], w[c],
                           start=(c == 0), stop=(c == 1))
                    for c in range(2):
                        mm(single[half, h % 2, 0:T], proj[:, tb, c * P + half.start:c * P + half.stop], w[c],
                           start=(c == 0), stop=(c == 1))
                    for c in range(2):
                        last = mm(wide[:, 4 * (h % 2) + 3, :], const("ones"), w[c], start=(c == 0), stop=(c == 1))
                    last.then_inc(m_sum, 1)

                for h in range(MH):
                    spread_rows(h)
                    score(h)
                    if h:
                        sums(h - 1)
                sums(MH - 1)
                leave()

            def mlstm_norm():
                enter(pe, "mlstm_norm")
                for v in range(2):
                    if v:
                        pe.wait_ge(mn_a, 1)
                    for h in range(MH):
                        for i, (_, t) in enumerate(m_tiles(h, 0)):
                            src = work[:, t * T:(t + 1) * T] if v else mixed[:, t, 0:T]
                            ones = const("mean_192_half")[:, (h % 2) * P:(h % 2 + 1) * P] if i else const("mean_192")
                            last = mm(wide[:, 4 * v + h, :], ones, src, start=(i == 0), stop=(i == 1))
                    last.then_inc(mn_p, 1)
                leave()

            def rglru():
                enter(pe, "rglru")
                pe.wait_ge(rg_loaded, 16)
                w = work[0:RB, 2560:2560 + 2 * NRB * RB].rearrange("p (g c) -> p g c", c=RB)
                pe.wait_ge(rg_v, 1)
                for g in range(2 * NRB):
                    dst = ps[0:RB, g // 2, (g % 2) * T:(g % 2 + 1) * T]
                    last = mm(dst, w[:, g, :], proj[0:RB, g % NRB, T:2 * T], start=True, stop=True)
                last.then_inc(rg_p, 1)
                leave()

            def choose(l):
                enter(pe, f"query{l}")
                pe.wait_ge(subk_loaded, 16 * (l - 1))
                base = 2 * PH * (l - 2)

                def query(m, b):
                    wait_filled(b)
                    if m >= 2:
                        pe.wait_ge(q_kept, base + m - 1)
                    for k in range(KD):
                        last = mm(pair[:, m % 2, 0:T], ring[:, b[0], k * P:(k + 1) * P], x[:, LAT, k, :],
                                  start=(k == 0), stop=(k == KD - 1))
                    last.then_inc(block_used, 1)

                def score(m):
                    pe.wait_ge(q_kept, base + m + 1)
                    if m >= 4:
                        pe.wait_ge(k_best, PH * (l - 2) + m // 2 - 1)
                    for t in range(2):
                        last = mm(ps[:, m % 4, t * P:(t + 1) * P], proj[:, m, t * P:(t + 1) * P], subk[:, m % 2, :],
                                  start=True, stop=True)
                    last.then_inc(k_score, 1)

                for m in range(2 * PH):
                    place.steps(pe, 1, 1, lambda _, par, b, m=m: query(m, b[0]))
                    if m:
                        score(m - 1)
                score(2 * PH - 1)
                pe.wait_ge(k_pick, l - 1)
                for t in range(2):
                    for i in range(3):
                        last = mm(ps[:, 4 + t, i * P:(i + 1) * P], picks[:, i, t, :], const("ident"),
                                  start=True, stop=True)
                    last.then_inc(k_turn, 1)
                leave()

            def spread(l, h):
                enter(pe, f"spread{l}{h}")
                base = (2 * (l - 2) + (h == "b")) * (T // (2 * GROUP))

                def one(it):
                    for b in range(2):
                        pe.wait_ge(hot_ready[b], it + (base + 1))
                        pe.wait_ge(hot_w_ready[b], it + (base + 1))
                        if not isinstance(it, int) or it + base:
                            pe.wait_ge(g_kept[b], it + base)
                        for u in range(GROUP):
                            for c in range(3):
                                last = mm(single[:, b, u * HALF:(u + 1) * HALF], hot_i[:, b, :, u],
                                          hot_w[:, b, c, :, u], start=(c == 0), stop=(c == 2))
                        last.then_inc(g_ready[b], 1)
                one(0)
                with pe.Fori(1, T // (2 * GROUP)) as it:
                    one(it)
                leave()

            for l in range(2):
                ada(l)
                project_early(l)
                attend(l)
                if l == 0:
                    pool_mix()
                else:
                    means("subln", "mean_128", T, 6)
                for n in ((CTX, LAT) if l == 0 else (LAT,)):
                    lo = n * T if l == 0 else 0
                    out_project(f"out{l}{n}", [(mixed[:, k, lo:lo + T], P) for k in range(KD)])
                    hidden(f"hidden{l}{n}", FH, 2)
            for l in (2, 3):
                enter(pe, f"project{l}")
                if l == 2:
                    gates()
                project(x[:, LAT, :, :], PROJECT[l])
                pe.wait_ge(mem_loaded, 16 * (l - 1))
                project(res, PROJECT_MEMORY)
                if l == 2:
                    gate_columns()
                leave()
                if l == 2:
                    mlstm()
                    mlstm_norm()
                    tiles = [(mixed[:, k, 0:T], P) for k in range(KD)]
                else:
                    rglru()
                    tiles = [(mixed[:, k, 0:T], P) for k in (8, 9)] + [(mixed[0:RB, k, 0:T], RB) for k in range(NRB)]
                attend(l)
                out_project(f"out{l}{LAT}", tiles)
                choose(l)
                for h in "ab":
                    spread(l, h)
                    hidden(f"hidden{l}{h}", HALF, 1, opens=(h == "a"), ends=(h == "b"))

        def hidden_steps(eng, place, name, n, unit, part_of, make):
            place.at = first_block(name)

            def parts(b):
                for blk in b:
                    part_of(blk)
            place.steps(eng, 2, unit, lambda i, ph, b: parts(b))
            make(0, 0)
            place.steps(eng, 1, unit + 1, lambda i, ph, b: (parts(b), make(1, 1)))
            place.steps(eng, 1, unit + 1, lambda i, ph, b: (parts(b), make(2, 2)))

            def one(i, ph, b):
                parts(b)
                make(i + 3, ph)
            place.steps(eng, n - 4, unit + 1, one, PHASES)
            place.steps(eng, 2, 1, lambda i, ph, b: parts(b))
            make(n - 1, (n - 1) % PHASES)

        @block.scalar
        def _(act):
            place = RingPlace()
            n_unit, n_ln, n_hid, n_sq = [0], [0], [0], [0]
            f = nc.scalar.activation

            def leave():
                act.drain().then_inc(stage["a"], 1)

            def project(name, runs, at, done):
                done += first_block(name)
                for first, n, _, nt, _, width in runs:
                    def one(i):
                        for par in range(2):
                            act.wait_ge(block_used, 2 * i + (done + par + 1))
                            lo = at + (first + par) * 512
                            dst = arena[0:width, lo + i * 1024:lo + i * 1024 + nt] if isinstance(i, int) else \
                                arena[0:width, bass.ds(i * 1024 + lo, nt)]
                            f(dst, pair[0:width, par, 0:nt], ACT.Copy).then_inc(tile_out[par], 1)
                    if n > 2:
                        with act.Fori(0, n // 2) as it:
                            one(it)
                    else:
                        one(0)
                    done += n

            def memory(l):
                n = sum(run[1] for run in PROJECT[l])
                project(f"project{l}", PROJECT_MEMORY[0:1], MEM_K + T, n)
                project(f"project{l}", PROJECT_MEMORY[1:2], MEM_V + T, n + 2)

            def project_early(l):
                enter(act, f"project{l}")

                for n, (j, _, nt, _) in enumerate(project_tiles(l)):
                    act.wait_ge(block_used, first_block(f"project{l}") + n + 1)
                    f(proj[:, j, 0:nt], pair[:, n % 2, 0:nt], ACT.Copy).then_inc(early_out, 1)
                    if l == 0 and n < len(ROPE[0]):
                        act.wait_ge(early_out, n + 1)
                        if n >= 2:
                            act.wait_ge(mean_ready, n - 1)
                        f(work[:, (n % 2) * 512:(n % 2 + 1) * 512], proj[:, j, :], ACT.Square).then_inc(squared, 1)
                    if l == 0 and 0 <= n - 1 < len(ROPE[0]):
                        b = (n - 1) % 2
                        act.wait_ge(mean_ready, n)
                        if n >= 3:
                            act.wait_ge(normed, n - 2)
                        root(work[:, 1024 + b * 512:1024 + (b + 1) * 512], single[:, b, :], 0)
                    if l == 1 and n == GLU - 1:
                        act.wait_ge(early_out, len(project_tiles(0)) + GLU)
                        f(glu_gate, proj[:, 20:22, 0:T], ACT.Sigmoid).then_inc(conv_a, 1)
                    if l == 1 and n == len(project_tiles(1)) - 4:
                        act.wait_ge(conv_v, 2)
                        f(squares, conved, ACT.Square).then_inc(conv_a, 1)
                    if l == 1 and n == len(project_tiles(1)) - 3:
                        act.wait_ge(conv_p, 2)
                        root(work[:, 1024:1024 + T], ps[:, 3, 0:T], 0)
                if l == 0:
                    n_sq[0] += len(ROPE[0])
                leave()

            def modulate(l):
                for k in range(KD):
                    f(hT[:, k, 0:T], x[:, CTX, k, :], ACT.Identity, scale=mod[:, l, KD + k, 1:2], bias=mod[:, l, k, 1:2])

            def root(dst, src, eps):
                f(dst, src, ACT.Sqrt, bias=eps_col[0:dst.shape[0], eps:eps + 1]).then_inc(rooted, 1)

            def heads_squares(name, tiles):
                enter(act, name)
                for i in range(len(tiles) + 1):
                    if i < len(tiles):
                        n = tiles[i].shape[1]
                        if i >= 2:
                            act.wait_ge(mean_ready, n_sq[0] + i - 1)
                        f(work[:, (i % 2) * 512:(i % 2) * 512 + n], tiles[i], ACT.Square).then_inc(squared, 1)
                    if i:
                        b = (i - 1) % 2
                        act.wait_ge(mean_ready, n_sq[0] + i)
                        if i >= 3:
                            act.wait_ge(normed, n_sq[0] + i - 2)
                        root(work[:, 1024 + b * 512:1024 + b * 512 + n], pair[:, b, 0:n], 0)
                n_sq[0] += len(tiles)
                leave()

            def attend(l):
                units = units_of(l)
                enter(act, f"attend{l}")
                base = n_unit[0]
                if l == 1:
                    for k in range(2):
                        f(mixed[:, 6 + k, 0:T], conved[:, k, :], ACT.Silu,
                          bias=param("conv_bb", k), scale=param("conv_g", k))

                def exps(i):
                    act.wait_ge(m_ready, base + i + 1)
                    if base + i >= 2:
                        act.wait_ge(t_ready, base + i - 1)
                    b = 4 * (i % 2)
                    for r in range(2):
                        last = f(probs[:, i % 2, r, 0:units[i]["nk"]], scores_at(i, units[i]["nk"])[:, r, :], ACT.Exp,
                                 bias=cols[:, 8 + b + r:9 + b + r], scale=HD ** -0.5,
                                 accum_out=cols[:, 16 + b + r:17 + b + r])
                    last.then_inc(e_ready, 1)

                def heads(i):
                    u = units[i]
                    act.wait_ge(o_ready, base + i + 1)
                    lo, m = u["rows"]
                    f(u["out"], single[lo:lo + m, i % 2, 0:P if u["diff"] else 2 * P], ACT.Copy).then_inc(o_out, 1)

                n = len(units)
                exps(0)
                for i in range(n):
                    if i + 1 < n:
                        exps(i + 1)
                    if i:
                        heads(i - 1)
                heads(n - 1)
                n_unit[0] += n
                leave()

            def norm(s, ln, k12, follow=None):
                for q in range(4):
                    act.wait_ge(ln_centred, 4 * n_ln[0] + q + 1)
                    f(work[:, q * 2 * T:(q + 1) * 2 * T].rearrange("p (k t) -> p k t", k=2), res[:, 2 * q:2 * q + 2, :],
                      ACT.Square).then_inc(ln_squared, 1)
                act.wait_ge(ln_var, n_ln[0] + 1)
                root(work[:, 4096:4096 + T], pair[:, 1, 0:T], 0 if ln < 2 else 1)

                def high(k):
                    act.wait_ge(ln_x, KD * n_ln[0] + k + 1)
                    if follow == "split":
                        f(x_split[:, 0, k, :], x[:, s, k, :], ACT.Copy).then_inc(x_high, 1)
                    else:
                        j = 1 if s == CTX else 0
                        f(x_split[:, 0, k, :], x[:, s, k, :], ACT.Identity, scale=mod[:, ln, 4 * KD + k, j:j + 1],
                          bias=mod[:, ln, 3 * KD + k, j:j + 1]).then_inc(x_high, 1)
                for k in range(KD):
                    act.wait_ge(ln_scaled, KD * n_ln[0] + k + 1)
                    f(x[:, s, k, :], res[:, k, :], ACT.Identity, bias=param(f"ln{ln}b{k12}", k)).then_inc(ln_x, 1)
                    if follow and k:
                        high(k - 1)
                if follow:
                    high(KD - 1)
                n_ln[0] += 1

            def hidden(name, n, unit, func, at, dst, after=None):
                enter(act, name)
                base = n_hid[0]

                def high(b):
                    slot, turn, seq, w = b
                    act.wait_ge(filled[slot], (turn + 1) * 16)
                    act.wait_ge(block_used, seq - (SPLIT - 1))
                    f(w_split[:, w, 0, :], ring[:, slot, :], ACT.Copy).then_inc(w_high, 1)

                def one(t, ph):
                    act.wait_ge(block_used, after_input(name, t, unit))
                    if not isinstance(t, int) or t >= PHASES:
                        act.wait_ge(hid_ready, t + (base - 2))
                    f(dst[:, ph, :], ps[:, 4 + ph, at:at + T], func).then_inc(gate_ready, 1)
                hidden_steps(act, place, name, n, unit, high, one)
                n_hid[0] += n
                if after:
                    norm(*after)
                leave()

            def spread(l, h):
                enter(act, f"spread{l}{h}")
                base = (2 * (l - 2) + (h == "b")) * (T // (2 * GROUP))
                with act.Fori(0, T // (2 * GROUP)) as it:
                    for b in range(2):
                        act.wait_ge(g_ready[b], it + (base + 1))
                        f(arena[:, bass.ds(it * 1024 + b * 512, 512)], single[:, b, :], ACT.Copy).then_inc(g_kept[b], 1)
                leave()

            enter(act, "lambda")
            act.wait_ge(lam_sum, 1)
            f(cols[:, 34:36], cols[:, 32:34], ACT.Exp).then_inc(lam_exp, 1)
            leave()
            for l in range(2):
                if l == 0:
                    enter(act, "ada0")
                    act.wait_ge(loaded, 16 * 6)
                    f(cond[:, 1, :, :], cond[:, 0, :, :], ACT.Silu).then_inc(silu_done, 1)
                    leave()
                enter(act, f"modulate{l}")
                modulate(l)
                leave()
                project_early(l)
                attend(l)
                if l == 1:
                    heads_squares("subln", [mixed[:, h, 0:T] for h in range(6)])
                for n in ((CTX, LAT) if l == 0 else (LAT,)):
                    enter(act, f"out{l}{n}")
                    norm(n, l, 1, "shift")
                    leave()
                    hidden(f"hidden{l}{n}", FH, 2, ACT.Silu, T, gate, (n, l, 2))
            for l in (2, 3):
                enter(act, f"project{l}")
                if l == 2:
                    act.wait_ge(gates_v, 1)
                    f(work[0:MH, 768:1024], work[0:MH, 512:768], ACT.Exp, scale=-1.0).then_inc(gates_a, 1)
                project(f"project{l}", PROJECT[l], PROJ, 0)
                memory(l)
                leave()
                if l == 2:
                    enter(act, "mlstm")
                    for h in range(MH):
                        act.wait_ge(m_cast, h + 1)
                        if h >= 2:
                            act.wait_ge(m_sum, h - 1)
                            act.wait_ge(m_head, h - 1)
                        for c in range(2):
                            at = (2 * (h % 2) + c) * T
                            f(work[:, at:at + T], pair[:, h % 2, 0:T], ACT.Exp, scale=-1.0,
                              bias=cols[:, c * MH + h:c * MH + h + 1]).then_inc(m_weight, 1)
                        f(work[:, 1024 + (h % 2) * T:1024 + (h % 2 + 1) * T], pair[:, h % 2, T:2 * T],
                          ACT.Exp).then_inc(m_weight, 1)
                    leave()
                    enter(act, "mlstm_norm")
                    act.wait_ge(mn_v, 1)
                    f(work[:, 0:6 * T].rearrange("p (k t) -> p k t", k=6), mixed[:, 0:6, 0:T],
                      ACT.Square).then_inc(mn_a, 1)
                    act.wait_ge(mn_p, 2)
                    root(work[:, 2048:2048 + MH * T].rearrange("p (h t) -> p h t", h=MH), wide[:, 4:8, :], 1)
                    f(proj[:, 18:24, 0:T], proj[:, 18:24, 0:T], ACT.Sigmoid).then_inc(mn_a, 1)
                    leave()
                else:
                    enter(act, "rglru")
                    r, i_, a_, th = rg_tiles()[1:5]
                    act.wait_ge(rg_v, 1)
                    f(cols[0:RB, 16:24], cols[0:RB, 8:16], ACT.Exp, scale=-1.0).then_inc(rg_a, 1)
                    act.wait_ge(rg_p, 1)
                    for g in range(NRB):
                        f(r[:, g, :], ps[0:RB, g // 2, (g % 2) * T:(g % 2 + 1) * T],
                          ACT.Sigmoid, bias=param("r_ba", g, RB))
                        last = f(i_[:, g, :],
                                 ps[0:RB, 4 + g // 2, (g % 2) * T:(g % 2 + 1) * T],
                                 ACT.Sigmoid, bias=param("r_bx", g, RB))
                    last.then_inc(rg_a, 1)
                    act.wait_ge(rg_a, 2)
                    act.wait_ge(rg_v, 2)
                    for g in range(NRB):
                        f(a_[:, g, :], r[:, g, :], ACT.Exp,
                          scale=cols[0:RB, 24 + g:25 + g])
                        last = f(th[:, g, :], r[:, g, :], ACT.Tanh,
                                 scale=cols[0:RB, 32 + g:33 + g])
                    last.then_inc(rg_a, 1)
                    act.wait_ge(rg_v, 3)
                    f(r, r, ACT.Sqrt).then_inc(rooted, 1)
                    f(proj[0:RB, 0:NRB, 0:T], proj[0:RB, 0:NRB, 0:T], ACT.Gelu).then_inc(rg_a, 1)
                    leave()
                attend(l)
                enter(act, f"out{l}{LAT}")
                norm(LAT, l, 1, "split")
                leave()
                enter(act, f"query{l}")
                for m in range(2 * PH):
                    act.wait_ge(block_used, first_block(f"query{l}") + m + 1)
                    f(proj[:, m, 0:T], pair[:, m % 2, 0:T], ACT.Copy).then_inc(q_kept, 1)
                act.wait_ge(k_shift, l - 1)
                f(top_w, top_w, ACT.Exp).then_inc(k_exp, 1)
                for t in range(2):
                    act.wait_ge(k_turn, 2 * (l - 2) + t + 1)
                    f(chosen[:, :, t * P:(t + 1) * P], ps[:, 4 + t, 0:3 * P].rearrange("p (a b) -> p a b", a=3),
                      ACT.Copy).then_inc(k_keep, 1)
                leave()
                for h in "ab":
                    spread(l, h)
                    hidden(f"hidden{l}{h}", HALF, 1, ACT.Gelu, 0, gelu, (LAT, l, 2) if h == "b" else None)

        @block.vector
        def _(dve):
            chain = Chain(dve, chain_v)
            place = RingPlace()
            n_unit, n_ln, n_follow, n_hid, n_sq, n_root = [0], [0], [0], [0], [0], [0]
            v = nc.vector

            def leave():
                dve.drain().then_inc(stage["v"], 1)

            def inverse_root(t):
                n_root[0] += 1
                dve.wait_ge(rooted, n_root[0])
                chain(v.reciprocal(t, t))

            def heads_norm(name, tiles, gain, factor):
                enter(dve, name)
                chain(v.tensor_scalar(cols[:, 40:41], gain, factor, None, ALU.mult))
                for i, t in enumerate(tiles):
                    n = t.shape[1]
                    r = work[:, 1024 + (i % 2) * 512:1024 + (i % 2) * 512 + n]
                    inverse_root(r)
                    v.scalar_tensor_tensor(t, t, cols[:, 40:41], r, ALU.mult, ALU.mult).then_inc(normed, 1)
                n_sq[0] += len(tiles)
                leave()

            def rotate(l, i):
                base = len(ROPE[0]) if l else 0
                j, lat = ROPE[l][i]
                t = proj[:, j, lat:lat + T]
                s = work[:, 2048 + (i % 2) * T:2048 + (i % 2 + 1) * T]
                dve.wait_ge(turned_pos, base + i + 1)
                v.tensor_tensor(s, ps[:, i % 2, 0:T], const("sin"), ALU.mult)
                chain(v.tensor_tensor(t, t, const("cos"), ALU.mult))
                v.tensor_tensor(t, t, s, ALU.add).then_inc(roped, 1)

            def project_early(l):
                enter(dve, f"project{l}")
                for i in range(len(ROPE[l])):
                    if l == 0:
                        t = proj[:, i, :]
                        r = work[:, 1024 + (i % 2) * 512:1024 + (i % 2 + 1) * 512]
                        inverse_root(r)
                        v.scalar_tensor_tensor(t, t, param("q_gain") if i < 6 else param("k_gain"), r,
                                               ALU.mult, ALU.mult).then_inc(normed, 1)
                        if i:
                            rotate(l, i - 1)
                    else:
                        conv_taps(2 * i, 2 * i + 2)
                        rotate(l, i)
                if l == 0:
                    n_sq[0] += len(ROPE[0])
                    rotate(l, len(ROPE[0]) - 1)
                else:
                    conv_taps(2 * len(ROPE[1]), CONV)
                    dve.wait_ge(conv_p, 1)
                    v.tensor_tensor(conved, conved, over(ps[:, 2, 0:T], 2), ALU.subtract).then_inc(conv_v, 1)
                    inverse_root(work[:, 1024:1024 + T])
                    v.tensor_tensor(conved, conved, over(work[:, 1024:1024 + T], 2), ALU.mult)
                leave()

            def conv_taps(lo, hi):
                if lo == 0:
                    chain(v.memset(conv_in, 0.0))
                    dve.wait_ge(conv_a, 1)
                    chain(v.tensor_tensor(conv_in[:, :, CPAD:CPAD + T], proj[:, 18:20, 0:T], glu_gate, ALU.mult))
                for i in range(lo, hi):
                    for k in range(2):
                        w = param("conv_w", k * CONV + i)
                        if i == 0:
                            last = v.tensor_scalar(conved[:, k, :], conv_in[:, k, 0:T], w, param("conv_b", k),
                                                   ALU.mult, ALU.add)
                        else:
                            last = v.scalar_tensor_tensor(conved[:, k, :], conv_in[:, k, i:i + T], w, conved[:, k, :],
                                                          ALU.mult, ALU.add)
                    if i < CONV - 1:
                        chain(last)
                    else:
                        last.then_inc(conv_v, 1)

            def attend(l):
                units = units_of(l)
                enter(dve, f"attend{l}")
                base = n_unit[0]

                def maxima(i):
                    b = 4 * (i % 2)
                    dve.wait_ge(s_ready, base + i + 1)
                    chain(v.tensor_reduce(cols[:, b:b + 2], scores_at(i, units[i]["nk"]), AX_X, ALU.max))
                    v.tensor_scalar(cols[:, 8 + b:10 + b], cols[:, b:b + 2], -HD ** -0.5, None,
                                    ALU.mult).then_inc(m_ready, 1)

                def diagonals(i):
                    b = 4 * (i % 2)
                    dve.wait_ge(e_ready, base + i + 1)
                    chain(v.reciprocal(cols[:, 24 + b:26 + b], cols[:, 16 + b:18 + b]))
                    for r in range(2):
                        second = neg_lam[:, 0:1] if units[i]["diff"] and r else None
                        op = (ALU.mult, ALU.mult) if second is not None else (ALU.mult,)
                        last = v.tensor_scalar(diag[:, 2 * (i % 2) + r, :], const("ident"),
                                               cols[:, 24 + b + r:25 + b + r], second, *op)
                    last.then_inc(d_ready, 1)

                def turned(i):
                    u = units[i]
                    dve.wait_ge(t_ready, base + i + 1)
                    if base + i >= 2:
                        dve.wait_ge(o_ready, base + i - 1)
                    n = u["nk"] * (1 if u["diff"] else 2)
                    v.tensor_copy(probsT[:, i % 2, 0:n], ps[:, 4:6, :].rearrange("p b n -> p (b n)")[:, 0:n])\
                        .then_inc(pt_ready, 1)

                n = len(units)
                maxima(0)
                for i in range(n):
                    diagonals(i)
                    if i + 1 < n:
                        maxima(i + 1)
                    turned(i)
                n_unit[0] += n
                leave()

            def gated_sum(name, s, l, part_):
                j = 1 if s == CTX else 0
                chain(v.tensor_scalar(res[:, :, :], x[:, s, :, :], ALPHA, None, ALU.mult))
                for k in range(KD):
                    complete(name, k)
                    v.scalar_tensor_tensor(res[:, k, :], wide[:, k, :], mod[:, l, part_ * KD + k, j:j + 1],
                                           res[:, k, :], ALU.mult, ALU.add).then_inc(res_ready, 1)

            def complete(name, k):
                if k < KD - 2:
                    dve.wait_ge(sum_ready, 3 * n_ln[0] + k // 2 + 1)
                else:
                    dve.wait_ge(block_used, first_block(name) + blocks_in(name))

            def plain_sum(name):
                for k in range(KD):
                    complete(name, k)
                    v.scalar_tensor_tensor(res[:, k, :], x[:, LAT, k, :], ALPHA, wide[:, k, :], ALU.mult, ALU.add)\
                        .then_inc(res_ready, 1)

            def norm(s, ln, k12, follow=None):
                dve.wait_ge(ln_mean, n_ln[0] + 1)
                for q in range(4):
                    two = res[:, 2 * q:2 * q + 2, :]
                    v.tensor_tensor(two, two, over(pair[:, 0, 0:T], 2), ALU.subtract).then_inc(ln_centred, 1)
                inverse_root(work[:, 4096:4096 + T])
                dve.wait_ge(ln_centred, 4 * (n_ln[0] + 1))
                for k in range(KD):
                    v.scalar_tensor_tensor(res[:, k, :], res[:, k, :], param(f"ln{ln}g{k12}", k),
                                           work[:, 4096:4096 + T], ALU.mult, ALU.mult).then_inc(ln_scaled, 1)
                if follow:
                    j = 1 if s == CTX else 0
                    src = x[:, s, :, :]
                    if follow == "shift":
                        src = h2
                        for k in range(KD):
                            dve.wait_ge(ln_x, KD * n_ln[0] + k + 1)
                            last = v.tensor_scalar(h2[:, k, :], x[:, s, k, :], mod[:, ln, 4 * KD + k, j:j + 1],
                                                   mod[:, ln, 3 * KD + k, j:j + 1], ALU.mult, ALU.add)
                        chain(last)
                    for k in range(KD):
                        dve.wait_ge(x_high, KD * n_follow[0] + k + 1)
                        v.tensor_tensor(x_split[:, 1, k, :], src[:, k, :], x_split[:, 0, k, :].bitcast(F32),
                                        ALU.subtract)
                    n_follow[0] += 1
                n_ln[0] += 1

            def hidden(name, n, unit, make, raw):
                base, w_base = n_hid[0], split_before(name) - first_block(name)

                def low(b):
                    slot, _, seq, w = b
                    dve.wait_ge(w_high, seq + (w_base + 1))
                    v.tensor_tensor(w_split[:, w, 1, :], ring[:, slot, :], w_split[:, w, 0, :].bitcast(F32),
                                    ALU.subtract).then_inc(w_low, 1)

                def one(t, ph):
                    dve.wait_ge(gate_ready, t + (base + 1))
                    make(t, ph).then_inc(hid_made, 1)
                    dve.wait_ge(hid_made, t + (base + 1))
                    if not isinstance(t, int) or t >= PHASES:
                        dve.wait_ge(block_used, after_output(name, t - PHASES, unit))
                    v.tensor_copy(h_split[:, ph, 0, :], raw[:, ph, :]).then_inc(hid_high, 1)
                    dve.wait_ge(hid_high, t + (base + 1))
                    v.tensor_tensor(h_split[:, ph, 1, :], raw[:, ph, :], h_split[:, ph, 0, :].bitcast(F32),
                                    ALU.subtract).then_inc(hid_ready, 1)
                hidden_steps(dve, place, name, n, unit, low, one)
                n_hid[0] += n

            def swiglu(t, ph):
                return v.tensor_tensor(hid[:, ph, :], ps[:, 4 + ph, 0:T], gate[:, ph, :], ALU.mult)

            def weigh(t, ph):
                g = G[:, :, t] if isinstance(t, int) else G[:, :, bass.ds(t, 1)].rearrange("p n o -> p (n o)")
                return v.tensor_tensor(coef[:, ph, :], gelu[:, ph, :], g, ALU.mult)

            def pool_scaled():
                enter(dve, "pool")
                for s in range(2):
                    dve.wait_ge(pool_out, s + 1)
                    for n in range(2):
                        v.tensor_scalar(mixed[:, 6 + n, s * T:(s + 1) * T], ps[:, 4 + 2 * s + n, 0:T],
                                        param("pool_scale", n), None, ALU.mult)
                leave()

            def log1p(dst, e, s, s2):
                chain(v.tensor_scalar(s, e, 2.0, None, ALU.add))
                chain(v.reciprocal(s, s))
                chain(v.tensor_tensor(s, s, e, ALU.mult))
                chain(v.tensor_tensor(s2, s, s, ALU.mult))
                chain(v.tensor_scalar(dst, s2, 1.0 / 17, None, ALU.mult))
                for n in range(15, 2, -2):
                    chain(v.scalar_tensor_tensor(dst, dst, 1.0 / n, s2, ALU.add, ALU.mult))
                chain(v.scalar_tensor_tensor(dst, dst, 1.0, s, ALU.add, ALU.mult))
                chain(v.tensor_scalar(dst, dst, 2.0, None, ALU.mult))

            def gates():
                enter(dve, "project2")

                def row(i):
                    return work[0:MH, i * T:(i + 1) * T]
                ig, fg, nf, e, F, t1, t2, lf, g, mx, fl, one = (row(i) for i in range(12))
                dve.wait_ge(gates_p, 1)
                v.tensor_scalar(ig, ps[0:MH, 0, 0:T], param("i_bias", 0, MH), None, ALU.add)
                v.memset(one, 1.0)
                chain(v.tensor_scalar(fg, ps[0:MH, 1, 0:T], param("f_bias", 0, MH), None, ALU.add))
                chain(v.tensor_scalar(nf, fg, -1.0, None, ALU.mult))
                v.tensor_tensor(nf, nf, fg, ALU.max).then_inc(gates_v, 1)
                dve.wait_ge(gates_a, 1)
                log1p(lf, e, t1, t2)
                chain(v.tensor_scalar(fg, fg, 0.0, None, ALU.min))
                chain(v.tensor_tensor(lf, fg, lf, ALU.subtract))
                chain(v.tensor_tensor_scan(F, one, lf, 0.0, ALU.mult, ALU.add))
                v.tensor_tensor(g, ig, F, ALU.subtract).then_inc(gates_v, 1)
                dve.wait_ge(gates_v, 2)
                chain(v.tensor_tensor_scan(mx, one, g, 0.0, ALU.mult, ALU.max))
                chain(v.tensor_tensor(fl, F, mx, ALU.add))
                chain(v.tensor_scalar(fl, fl, -1.0, None, ALU.mult))
                dve.wait_ge(gates_p, 2)
                v.tensor_copy(cols[:, 0:2 * MH], single[:, 0, 0:2 * MH])
                leave()

            def mlstm():
                enter(dve, "mlstm")

                def weighted(h):
                    dve.wait_ge(m_score, h + 1)
                    dve.wait_ge(m_mask, 2 * h + 2)
                    for c in range(2):
                        w = work[:, (2 * (h % 2) + c) * T:(2 * (h % 2) + c + 1) * T]
                        last = v.scalar_tensor_tensor(w, wide[:, 4 * (h % 2) + c, :], MDH ** -0.5, w,
                                                      ALU.mult, ALU.mult)
                    last.then_inc(m_st, 1)

                def divided(h):
                    dve.wait_ge(m_sum, h + 1)
                    dve.wait_ge(m_weight, 3 * h + 3)
                    floor = work[:, 1024 + (h % 2) * T:1024 + (h % 2 + 1) * T]
                    den = wide[:, 4 * (h % 2) + 3, :]
                    chain(v.tensor_tensor(floor, den, floor, ALU.max))
                    chain(v.scalar_tensor_tensor(floor, den, -1.0, floor, ALU.mult, ALU.max))
                    chain(v.reciprocal(floor, floor))
                    (_, ta), (half, tb) = m_tiles(h, 0)
                    v.tensor_tensor(mixed[:, ta, 0:T], wide[:, 4 * (h % 2) + 2, :], floor, ALU.mult)
                    v.tensor_tensor(mixed[half, tb, 0:T], single[half, h % 2, 0:T], floor[half, :], ALU.mult)\
                        .then_inc(m_head, 1)

                for h in range(MH):
                    weighted(h)
                    if h:
                        divided(h - 1)
                divided(MH - 1)
                leave()

            def mlstm_norm():
                enter(dve, "mlstm_norm")
                for i in range(2):
                    dve.wait_ge(mn_p, i + 1)
                    if i:
                        rstd = work[:, 2048:2048 + MH * T].rearrange("p (h t) -> p h t", h=MH)
                        inverse_root(work[:, 2048:2048 + MH * T])
                    for h in range(MH):
                        for rows, t in m_tiles(h, 0):
                            src = rstd[rows, h, :] if i else wide[rows, h, :]
                            last = v.tensor_tensor(mixed[rows, t, 0:T], mixed[rows, t, 0:T], src,
                                                   ALU.mult if i else ALU.subtract)
                    last.then_inc(mn_v, 1)
                    dve.wait_ge(mn_v, i + 1)
                dve.wait_ge(mn_a, 2)
                for t in range(6):
                    v.scalar_tensor_tensor(mixed[:, t, 0:T], mixed[:, t, 0:T], param("mnorm", t),
                                           proj[:, 18 + t, 0:T], ALU.mult, ALU.mult)
                leave()

            def rglru():
                enter(dve, "project3")
                W = T + RG_CONV - 1
                xp = work[0:RB, 0:NRB * W].rearrange("p (g t) -> p g t", g=NRB)
                xc, r, i_, a_, th = rg_tiles()
                chain(v.tensor_scalar(cols[0:RB, 8:16], param("r_lam", 0, RB, NRB), -1.0, None, ALU.mult))
                chain(v.tensor_tensor(cols[0:RB, 8:16], cols[0:RB, 8:16], param("r_lam", 0, RB, NRB), ALU.max))
                v.memset(xp[:, :, 0:RG_CONV - 1], 0.0)
                n = (sum(run[1] for run in PROJECT[2] + PROJECT_MEMORY) + NRB) // 2
                for par in range(2):
                    dve.wait_ge(tile_out[par], n)
                chain(v.tensor_copy(xp[:, :, RG_CONV - 1:W], proj[0:RB, 8:16, 0:T]))
                for j in range(RG_CONV):
                    for g in range(NRB):
                        w = param("rconv_w", g * RG_CONV + j, RB)
                        if j == 0:
                            last = v.tensor_scalar(xc[:, g, :], xp[:, g, 0:T], w, param("rconv_b", g, RB),
                                                   ALU.mult, ALU.add)
                        else:
                            last = v.scalar_tensor_tensor(xc[:, g, :], xp[:, g, j:j + T], w, xc[:, g, :],
                                                          ALU.mult, ALU.add)
                    if j < RG_CONV - 1:
                        chain(last)
                last.then_inc(rg_v, 1)
                dve.wait_ge(rg_v, 1)
                leave()
                enter(dve, "rglru")
                dve.wait_ge(rg_a, 1)
                log1p(cols[0:RB, 48:56], cols[0:RB, 16:24], cols[0:RB, 56:64], cols[0:RB, 64:72])
                chain(v.tensor_scalar(cols[0:RB, 72:80], param("r_lam", 0, RB, NRB), -1.0, 0.0, ALU.mult, ALU.max))
                chain(v.tensor_tensor(cols[0:RB, 48:56], cols[0:RB, 48:56], cols[0:RB, 72:80], ALU.add))
                v.tensor_scalar(cols[0:RB, 24:32], cols[0:RB, 48:56], -RG_C, None, ALU.mult)
                v.tensor_scalar(cols[0:RB, 32:40], cols[0:RB, 48:56], RG_C, None, ALU.mult).then_inc(rg_v, 1)
                dve.wait_ge(rg_a, 2)
                chain(v.tensor_tensor(i_, i_, xc, ALU.mult))
                dve.wait_ge(rg_a, 3)
                chain(v.tensor_scalar(r, th, 1.0, None, ALU.add))
                chain(v.reciprocal(r, r))
                chain(v.scalar_tensor_tensor(r, th, 2.0, r, ALU.mult, ALU.mult))
                v.tensor_scalar(r, r, ROOT_MIN, None, ALU.max).then_inc(rg_v, 1)
                n_root[0] += 1
                dve.wait_ge(rooted, n_root[0])
                chain(v.tensor_tensor(i_, i_, r, ALU.mult))
                for g in range(NRB):
                    last = v.tensor_tensor_scan(xc[:, g, :], a_[:, g, :], i_[:, g, :], 0.0, ALU.mult, ALU.add)
                chain(last)
                dve.wait_ge(rg_a, 4)
                v.tensor_tensor(mixed[0:RB, 0:NRB, 0:T], xc, proj[0:RB, 0:NRB, 0:T], ALU.mult)
                leave()

            def choose(l):
                enter(dve, f"query{l}")
                base = PH * (l - 2)

                def top16(batch):
                    for wait, values, _, scores, _ in batch:
                        wait()
                        last = v.max(values[:, 0:8], scores)
                    chain(last)
                    for _, values, _, scores, left in batch:
                        v.match_replace(left, values[:, 0:8], scores, NEG)
                    for _, values, indices, scores, _ in batch:
                        last = v.max_index(indices[:, 0:8], values[:, 0:8], scores)
                    chain(last)
                    for _, values, _, _, left in batch:
                        last = v.max(values[:, 8:16], left)
                    chain(last)
                    for _, values, indices, _, left in batch:
                        last = v.max_index(indices[:, 8:16], values[:, 8:16], left)
                    chain(last)

                def scored(m):
                    return lambda: dve.wait_ge(k_score, 2 * base + m + 1)

                def summed(h):
                    return lambda: dve.wait_ge(k_cand, base + h + 1)

                def best_of(h):
                    batch = []
                    if h < PH:
                        batch += [(scored(m), best[:, m, t], best_key[:, m, t], ps[:, m % 4, t * P:(t + 1) * P],
                                   rest[:, m % 2, t * P:(t + 1) * P]) for m in (2 * h, 2 * h + 1) for t in range(2)]
                    if h:
                        batch += [(summed(h - 1), top[:, h - 1, t], top_at[:, h - 1, t], cand[:, (h - 1) % 2, t, :],
                                   rest_sums[:, t, :]) for t in range(2)]
                    top16(batch)
                    if h < PH:
                        v.tensor_copy(best_key_f[:, 2 * h:2 * h + 2], best_key[:, 2 * h:2 * h + 2]).then_inc(k_best, 1)

                def finals(h):
                    v.tensor_scalar(half_at[0][:, h], top_at[:, h], 4, None, ALU.logical_shift_right)
                    chain(v.tensor_scalar(half_at[1][:, h], top_at[:, h], TOPK - 1, None, ALU.bitwise_and))
                    for i in range(2):
                        last = v.tensor_copy(half_at_f[i][:, h], half_at[i][:, h])
                    chain(last)
                    for i in range(2):
                        at = half_at_f[i][:, h].rearrange("p t k -> p (t k)")
                        last = v.tensor_tensor(picked[:, 4 * h + 2 * i:4 * h + 2 * i + 2].rearrange("p t k n -> p (t k) n"),
                                               at.unsqueeze(2).to_broadcast([P, 2 * TOPK, TOPK]),
                                               over(const("iota")[:, 0:TOPK], 2 * TOPK), ALU.is_equal)
                    last.then_inc(k_place, 1)

                def key_of(h):
                    dve.wait_ge(k_product, base + h + 1)
                    for i in range(2):
                        last = v.tensor_reduce(picks[:, i, :, h * TOPK:(h + 1) * TOPK],
                                               picked[:, 4 * h + 2 * i:4 * h + 2 * i + 2], AX_X, ALU.add)
                    return last

                for h in range(PH + 1):
                    best_of(h)
                    if h:
                        finals(h - 1)
                    if 2 <= h < PH:
                        key_of(h - 2)
                by_head = top_w.rearrange("p t (h k) -> p h t k", h=PH)
                dve.wait_ge(k_place, base + PH)
                v.tensor_tensor(by_head, top, top[:, :, :, 0:1].to_broadcast([P, PH, 2, TOPK]), ALU.subtract)\
                    .then_inc(k_shift, 1)
                key_of(PH - 2)
                dve.wait_ge(k_exp, l - 1)
                w = top_w.rearrange("p t (h k) -> p t h k", h=PH)
                chain(v.tensor_reduce(top_sum, w, AX_X, ALU.add))
                chain(v.reciprocal(top_sum, top_sum))
                v.tensor_tensor(picks[:, 2].rearrange("p t (h k) -> p t h k", h=PH), w,
                                top_sum.unsqueeze(3).to_broadcast([P, 2, PH, TOPK]), ALU.mult)
                key_of(PH - 1).then_inc(k_pick, 1)
                leave()

            def tables():
                w, left = chosen[:, 2, :], res[:, 3, :]
                v.tensor_copy(keys, chosen[:, 0:2, :])
                v.tensor_copy(places, const("iota").unsqueeze(2).to_broadcast([P, KEYS, GROUP]))
                for c in range(3):
                    chain(v.tensor_copy(weight3[:, c, :], w))
                    if c < 2:
                        chain(v.tensor_tensor(left, w, weight3[:, c, :], ALU.subtract))
                        w = left

            def spread(l, h):
                enter(dve, f"spread{l}{h}")
                base = (2 * (l - 2) + (h == "b")) * (T // (2 * GROUP))
                lo = HALF * (h == "b")

                def one(it):
                    for b in range(2):
                        at = bass.ds(it * (2 * GROUP) + b * GROUP, GROUP)
                        if not isinstance(it, int) or it + base:
                            dve.wait_ge(g_ready[b], it + base)
                        v.tensor_tensor(hot_j[:, b], places[:, lo:lo + HALF, :], over(keys[:, 1, at], HALF), ALU.is_equal)\
                            .then_inc(hot_j_made, 1)
                        v.tensor_tensor(hot_i[:, b], places, over(keys[:, 0, at], KEYS), ALU.is_equal)
                        dve.wait_ge(hot_j_made, it * 2 + (2 * base + b + 1))
                        v.tensor_tensor(hot_w[:, b, 0:2], hot_j[:, b].unsqueeze(1).to_broadcast([P, 2, HALF, GROUP]),
                                        weight3[:, 0:2, at].unsqueeze(2).to_broadcast([P, 2, HALF, GROUP]), ALU.mult)\
                            .then_inc(hot_ready[b], 1)
                one(0)
                with dve.Fori(1, T // (2 * GROUP)) as it:
                    one(it)
                leave()

            enter(dve, "lambda")
            v.memset(eps_col[:, 0:1], EPS1)
            v.memset(eps_col[:, 1:2], EPS2)
            dve.wait_ge(loaded, 16 * 6)
            for i in range(2):
                v.tensor_tensor(work[:, i * HD:(i + 1) * HD], param(f"lq{i + 1}", n=HD), param(f"lk{i + 1}", n=HD),
                                ALU.mult).then_inc(chain_v, 1)
            chain.n += 2
            dve.wait_ge(chain_v, chain.n)
            v.tensor_reduce(cols[:, 32:34], work[:, 0:2 * HD].rearrange("p (a b) -> p a b", a=2), AX_X, ALU.add)\
                .then_inc(lam_sum, 1)
            dve.wait_ge(lam_exp, 1)
            chain(v.tensor_tensor(neg_lam[:, :], cols[:, 35:36], cols[:, 34:35], ALU.subtract))
            v.tensor_scalar(neg_lam[:, :], neg_lam[:, :], -LAM_INIT, None, ALU.add)
            leave()

            for l in range(2):
                enter(dve, f"ada{l}")

                def rows(n):
                    dve.wait_ge(block_used, first_block(f"ada{l}") + (n + 1) * KD)
                    if n >= 2:
                        dve.wait_ge(ada_turned, 6 * l + n - 1)
                    v.tensor_copy(work[0:2, (n % 2) * D:(n % 2 + 1) * D].rearrange("p (c n) -> p c n", c=2),
                                  ps[0:2, 2 * (n % 2):2 * (n % 2) + 2, :]).then_inc(ada_rows, 1)

                def biased(n):
                    dve.wait_ge(ada_turned, 6 * l + n + 1)
                    v.tensor_tensor(mod[:, l, n * KD:(n + 1) * KD, :],
                                    pair[:, n % 2, 0:2 * KD].rearrange("p (m j) -> p m j", j=2),
                                    param(f"ada_b{l}", n * KD, n=KD).unsqueeze(2).to_broadcast([P, KD, 2]), ALU.add)\
                        .then_inc(ada_out, 1)

                for n in range(6):
                    rows(n)
                    if n:
                        biased(n - 1)
                biased(5)
                dve.wait_ge(ada_out, 6 * (l + 1))
                for q in (1, 4):
                    v.tensor_scalar(mod[:, l, q * KD:(q + 1) * KD, :], mod[:, l, q * KD:(q + 1) * KD, :], 1.0, None,
                                    ALU.add)
                leave()
                enter(dve, f"modulate{l}")
                for k in range(KD):
                    v.tensor_scalar(hT[:, k, T:2 * T], x[:, LAT, k, :], mod[:, l, KD + k, 0:1], mod[:, l, k, 0:1],
                                    ALU.mult, ALU.add)
                leave()
                project_early(l)
                attend(l)
                if l == 0:
                    pool_scaled()
                else:
                    heads_norm("subln", [mixed[:, h, 0:T] for h in range(6)], param("subln"), 1.0 - LAM_INIT)
                for s in ((CTX, LAT) if l == 0 else (LAT,)):
                    j = 1 if s == CTX else 0
                    enter(dve, f"out{l}{s}")
                    gated_sum(f"out{l}{s}", s, l, 2)
                    norm(s, l, 1, "shift")
                    leave()
                    enter(dve, f"hidden{l}{s}")
                    hidden(f"hidden{l}{s}", FH, 2, swiglu, hid)
                    gated_sum(f"hidden{l}{s}", s, l, 5)
                    norm(s, l, 2)
                    leave()
            for l in (2, 3):
                if l == 2:
                    gates()
                    mlstm()
                    mlstm_norm()
                else:
                    rglru()
                attend(l)
                enter(dve, f"out{l}{LAT}")
                plain_sum(f"out{l}{LAT}")
                norm(LAT, l, 1, "split")
                leave()
                choose(l)
                enter(dve, f"tables{l}")
                tables()
                leave()
                for h in "ab":
                    spread(l, h)
                    enter(dve, f"hidden{l}{h}")
                    hidden(f"hidden{l}{h}", HALF, 1, weigh, coef)
                    if h == "b":
                        plain_sum(f"hidden{l}{h}")
                        norm(LAT, l, 2)
                    leave()


def constants():
    at, n = const_layout()
    c = np.zeros((P, n), np.float32)

    def put(name, value):
        lo, hi = at[name]
        c[:value.shape[0], lo:hi] = value.reshape(value.shape[0], -1)

    put("ident", np.eye(P))
    put("mean_d", np.full((P, P), 1.0 / D))
    put("mean_64", np.kron(np.eye(2), np.full((HD, HD), 1.0 / HD)))
    put("mean_128", np.full((P, P), 1.0 / P))
    put("mean_192", np.full((P, P), 1.0 / MDH))
    put("mean_192_half", np.kron(np.eye(2), np.ones((HD, 1)))[:, :, None] * np.full(P, 1.0 / MDH))
    put("mean_256", np.full((P, P), 1.0 / 256))
    put("ones", np.ones((P, P)))
    rot = np.zeros((P, P))
    angle_of = np.zeros(P, int)
    for f in range(P):
        axis, half, i = (f % HD) // 32, (f % 32) // 16, f % 16
        rot[f + 16 if half == 0 else f - 16, f] = -1.0 if half == 0 else 1.0
        angle_of[f] = axis * 16 + i
    put("rot", rot)
    pos = np.arange(T)
    freqs = np.float32(10000.0) ** (-np.arange(0, 32, 2, dtype=np.float32) / np.float32(32))
    ang = np.concatenate([(pos // 64).astype(np.float32)[:, None] * freqs,
                          (pos % 64).astype(np.float32)[:, None] * freqs], axis=1)
    put("cos", np.cos(ang)[:, angle_of].T)
    put("sin", np.sin(ang)[:, angle_of].T)
    inv = np.zeros((P, 2, T))
    for g, w in enumerate(WINDOWS):
        lo, hi = np.clip(pos - w // 2, 0, T), np.clip(pos + (w - 1 - w // 2) + 1, 0, T)
        inv[(g % 2) * 64:(g % 2 + 1) * 64, g // 2] = 1.0 / (hi - lo)
    put("inv_count", inv)
    put("iota", np.tile(np.arange(P), (P, 1)))
    rows = np.zeros((MH, MH, P))
    for h in range(MH):
        rows[h, h] = 1.0
    put("head_rows", rows)
    return c


def columns(v, width=P):
    v = v.reshape(-1, width).T
    return np.concatenate([v, np.zeros((P - width, v.shape[1]), v.dtype)]) if width < P else v


def by_column(w, width=P):
    k, f = w.shape
    return w.reshape(k // P, P, f // width, width).transpose(2, 1, 0, 3).reshape(f // width, P, -1)


def by_row(w, rows=P):
    return w.reshape(-1, rows, w.shape[1])


def turned(x):
    return x.T.reshape(-1, P, x.shape[0]).transpose(1, 0, 2)


def mlstm_order():
    a_ = [np.arange(h * MDH, h * MDH + P) for h in range(MH)]
    return np.concatenate(a_ + [np.arange(h * MDH + P, (h + 1) * MDH) for h in range(MH)])


def lay_out(i):
    a = {}
    a["consts"] = constants()
    at, n = param_layout()
    prm = np.zeros((P, n), np.float32)

    def put(name, value):
        lo, hi = at[name]
        prm[:value.shape[0], lo:hi] = value

    for l in range(2):
        put(f"ada_b{l}", columns(i["ada_b"][l]))
        for k in "12":
            put(f"ln{l}g{k}", columns(i[f"ln{k}_g"][l]))
            put(f"ln{l}b{k}", columns(i[f"ln{k}_b"][l]))
            put(f"ln{l + 2}g{k}", columns(i[f"ln{k}_g_2"][l]))
            put(f"ln{l + 2}b{k}", columns(i[f"ln{k}_b_2"][l]))
    put("q_gain", np.tile(i["ab_q_gain"][0], 2)[:, None])
    put("k_gain", np.tile(i["ab_k_gain"][0], 2)[:, None])
    put("pool_scale", columns(i["ab_pool_scale"][0]))
    pool_w = np.zeros((P, 2, P), np.float32)
    for g in range(4):
        lo = (g % 2) * 64
        pool_w[lo:lo + 64, g // 2, lo:lo + 64] = i["ab_w_pool"][0, g]
    put("pool_w", pool_w.reshape(P, -1))
    put("subln", columns(i["cd_subln_gain"][0]))
    put("conv_w", i["cd_conv_w"][0].reshape(CONV, 2, P).transpose(2, 1, 0).reshape(P, -1))
    put("conv_b", columns(i["cd_conv_b"][0]))
    put("conv_g", columns(i["cd_conv_ln_g"][0]))
    put("conv_bb", columns(i["cd_conv_ln_b"][0]))
    for name, src in (("lq1", "cd_lambda_q1"), ("lk1", "cd_lambda_k1"), ("lq2", "cd_lambda_q2"), ("lk2", "cd_lambda_k2")):
        put(name, np.broadcast_to(i[src][0], (P, HD)))
    order = mlstm_order()
    put("mnorm", columns(i["mlstm_norm_g_2"][0][order]))
    bg = i["mlstm_b_gates_2"][0]
    put("i_bias", bg[:MH, None])
    put("f_bias", bg[MH:, None])
    put("rconv_w", columns(i["rglru_conv_w_2"][0].reshape(-1), RB).reshape(P, RG_CONV, NRB).transpose(0, 2, 1).reshape(P, -1))
    for name, src in (("rconv_b", "rglru_conv_b_2"), ("r_ba", "rglru_b_a_2"), ("r_bx", "rglru_b_x_2"), ("r_lam", "rglru_lam_2")):
        put(name, columns(i[src][0], RB))
    a["params"] = prm
    a["x"] = turned(i["x"][0])
    a["ctx"] = turned(i["ctx"][0])
    a["mem"] = turned(i["mem_2"][0])
    a["cond"] = turned(np.stack([i["c"][0], i["c_ctx"]]))

    for l in range(2):
        a[f"ada{l}"] = i["ada_w"][l].reshape(KD, P, 6, D).transpose(2, 0, 1, 3).reshape(6 * KD, P, D)
        w = i["ffn_w_in"][l]
        a[f"ffn{l}_in"] = w.reshape(KD, P, 2, FH, P).transpose(3, 2, 1, 0, 4).reshape(2 * FH, P, D)
        a[f"ffn{l}_out"] = by_row(i["ffn_w_out"][l])
        a[f"kv{l}"] = by_column(i["xattn_w_kv_2"][l])
        a[f"pq{l}"] = by_column(i["peer_w_q_2"][l])
        a[f"subk{l}"] = i["peer_subkeys_2"][l].transpose(2, 0, 1)
        u = i["peer_u_2"][l].reshape(KEYS, KEYS, KD, P)
        a[f"peer{l}_u"] = u.transpose(1, 3, 2, 0).reshape(KEYS, P, D)
        a[f"peer{l}_v"] = i["peer_v_2"][l].reshape(KEYS, KEYS, D).transpose(1, 0, 2)
    heads = np.concatenate([np.arange(h * HD, (h + 1) * HD) for h in Q_ORDER])
    w = i["ab_w_in"][0]
    a["ab_in"] = by_column(np.concatenate([w[:, heads], w[:, 768:]], axis=1))
    w = i["ab_w_out"][0]
    a["ab_out"] = by_row(np.concatenate([w[heads], w[768:]]))
    w = by_column(i["cd_w_in"][0])
    a["cd_in"] = np.concatenate([w[-GLU:], w[:-GLU]])
    a["cd_out"] = by_row(i["cd_w_out"][0])
    w = i["mlstm_w_in_2"][0]
    W = MH * MDH
    a["ml_in"] = by_column(np.concatenate([w[:, s * W + order] for s in range(4)] + [w[:, 4 * W + 2 * MH:]], axis=1))
    a["gate_w"] = w[:, 4 * W:4 * W + 2 * MH].reshape(KD, P, 2 * MH).transpose(1, 0, 2)
    w = i["w_out_2"][0]
    a["ml_out"] = by_row(np.concatenate([w[order], w[W:]]))
    w = i["rglru_w_in_2"][0]
    r = by_column(w[:, :2 * NRB * RB], RB)
    a["rg_in_r"] = np.concatenate([r[NRB:], r[:NRB]])
    a["rg_in_q"] = by_column(w[:, 2 * NRB * RB:])
    a["rg_w"] = np.concatenate([i["rglru_w_a_2"][0], i["rglru_w_x_2"][0]]).transpose(1, 0, 2).reshape(RB, -1)
    w = i["w_out_2"][1]
    a["rg_out_q"] = by_row(w[NRB * RB:])
    a["rg_out_r"] = by_row(w[:NRB * RB], RB)
    return {k: np.ascontiguousarray(v) for k, v in a.items()}


def kernel(**inputs):
    import concourse.bacc as bacc
    from concourse.bass_utils import run_bass_kernel_spmd

    nc = bacc.Bacc("TRN2", target_bir_lowering=False, num_devices=1)
    arrays = {f"in_{k}": v for k, v in lay_out({k: np.asarray(v) for k, v in inputs.items()}).items()}
    aps = {k[3:]: nc.dram_tensor(k, v.shape, F32, kind="ExternalInput").ap() for k, v in arrays.items()}
    out = nc.dram_tensor("out", (P, KD, T), F32, kind="ExternalOutput").ap()
    program(nc, aps, out)
    got = run_bass_kernel_spmd(nc, [arrays], core_ids=[0]).results[0]["out"]
    return np.ascontiguousarray(got.transpose(1, 0, 2).reshape(D, T).T)[None]
```
